# Optimizing a Trainium2 kernel written in Bass

```python
import math
import jax, jax.numpy as jnp
from jax import lax
import numpy as np

D_MODEL = 2048
BATCH = 1
SEQ = 256
DEPTH = 1

D_MIX = D_MODEL
D_SSM = D_MIX // 2
D_ATTN = D_MIX - D_SSM
HEAD_DIM = 64
N_HEADS = D_ATTN // HEAD_DIM
SSM_GROUP = 16
N_SSM_GROUPS = D_SSM // SSM_GROUP
SSM_STATE = 64
DILATIONS = ((128, 1), (512, 4), (2048, 16))
D_FF = ((8 * D_MODEL // 3 + 127) // 128) * 128
DT_MIN = 0.001
DT_MAX = 0.1
EPS = 1e-6
NEG_INF = -1e30


def rmsnorm(x, g):
    x32 = x.astype(jnp.float32)
    y = x32 * lax.rsqrt(jnp.mean(x32 * x32, axis=-1, keepdims=True) + EPS) * g.astype(jnp.float32)
    return y.astype(x.dtype)

def swiglu(x, w_gate, w_up, w_down):
    return (jax.nn.silu(x @ w_gate) * (x @ w_up)) @ w_down

def _ssm_combine(left, right):
    ar_i, ai_i, br_i, bi_i = left
    ar_j, ai_j, br_j, bi_j = right
    ar = ar_j * ar_i - ai_j * ai_i
    ai = ar_j * ai_i + ai_j * ar_i
    br = ar_j * br_i - ai_j * bi_i + br_j
    bi = ar_j * bi_i + ai_j * br_i + bi_j
    return (ar, ai, br, bi)

def s5_mixer(u, log_dt, a_re, a_im, b_re, b_im, c_re, c_im, d, w_glu, b_glu):
    Bsz, S, _ = u.shape
    f32 = jnp.float32
    u32 = u.astype(f32).reshape(Bsz, S, N_SSM_GROUPS, SSM_GROUP)
    lr = a_re.astype(f32)
    li = a_im.astype(f32)
    dt = jnp.exp(log_dt.astype(f32))[:, None]
    mag = jnp.exp(lr * dt)
    lb_re = mag * jnp.cos(li * dt)
    lb_im = mag * jnp.sin(li * dt)
    den = lr * lr + li * li
    nr = lb_re - 1.0
    ni = lb_im
    f_re = (nr * lr + ni * li) / den
    f_im = (ni * lr - nr * li) / den
    br = b_re.astype(f32)
    bi = b_im.astype(f32)
    bb_re = f_re[..., None] * br - f_im[..., None] * bi
    bb_im = f_re[..., None] * bi + f_im[..., None] * br
    bu_re = jnp.einsum('bsgh,gph->sbgp', u32, bb_re)
    bu_im = jnp.einsum('bsgh,gph->sbgp', u32, bb_im)
    a_re_t = jnp.broadcast_to(lb_re[None, None], (S, 1, N_SSM_GROUPS, SSM_STATE))
    a_im_t = jnp.broadcast_to(lb_im[None, None], (S, 1, N_SSM_GROUPS, SSM_STATE))
    _, _, s_re, s_im = lax.associative_scan(_ssm_combine, (a_re_t, a_im_t, bu_re, bu_im), axis=0)
    y = (jnp.einsum('sbgp,ghp->bsgh', s_re, c_re.astype(f32))
         - jnp.einsum('sbgp,ghp->bsgh', s_im, c_im.astype(f32))
         + d.astype(f32) * u32)
    y = jax.nn.gelu(y).reshape(Bsz, S, D_SSM)
    return y * jax.nn.sigmoid(y @ w_glu.astype(f32) + b_glu.astype(f32))

def dilated_branch(q, k, v, window, dilation):
    Bsz, S, H, E = q.shape
    nk = window // dilation
    blk = nk
    L = S // dilation
    nb = -(-L // blk)
    Lp = nb * blk

    def gather(t):
        t = t.reshape(Bsz, L, dilation, H, E).transpose(0, 2, 1, 3, 4)
        t = jnp.pad(t, ((0, 0), (0, 0), (0, Lp - L), (0, 0), (0, 0)))
        return t.reshape(Bsz, dilation, nb, blk, H, E)

    qb, kb, vb = gather(q), gather(k), gather(v)

    def with_prev(t):
        prev = jnp.pad(t, ((0, 0), (0, 0), (1, 0), (0, 0), (0, 0), (0, 0)))[:, :, :-1]
        return jnp.concatenate([prev, t], axis=3)

    kk, vv = with_prev(kb), with_prev(vb)
    s = jnp.einsum('bgnqhe,bgnkhe->bgnhqk', qb, kk) * (1.0 / math.sqrt(E))
    qi = jnp.arange(blk)[:, None]
    kj = jnp.arange(2 * blk)[None, :]
    dist = blk + qi - kj
    kpos = (jnp.arange(nb)[:, None, None] - 1) * blk + kj[None]
    valid = (dist >= 0)[None] & (dist <= nk)[None] & (kpos >= 0)
    s = jnp.where(valid[None, None, :, None], s, NEG_INF)
    m = jnp.max(s, axis=-1, keepdims=True)
    p = jnp.exp(s - m)
    den = jnp.sum(p, axis=-1, keepdims=True)
    o = jnp.einsum('bgnhqk,bgnkhe->bgnqhe', p / den, vv)
    lse = (m + jnp.log(den))[..., 0].transpose(0, 1, 2, 4, 3)
    o = o.reshape(Bsz, dilation, Lp, H, E)[:, :, :L].transpose(0, 2, 1, 3, 4).reshape(Bsz, S, H, E)
    lse = lse.reshape(Bsz, dilation, Lp, H)[:, :, :L].transpose(0, 2, 1, 3).reshape(Bsz, S, H)
    return o, lse

def dilated_attention(q, k, v):
    Bsz, S, _ = q.shape
    f32 = jnp.float32
    q = q.astype(f32).reshape(Bsz, S, N_HEADS, HEAD_DIM)
    k = k.astype(f32).reshape(Bsz, S, N_HEADS, HEAD_DIM)
    v = v.astype(f32).reshape(Bsz, S, N_HEADS, HEAD_DIM)
    outs, lses = [], []
    for window, dilation in DILATIONS:
        o, lse = dilated_branch(q, k, v, window, dilation)
        outs.append(o)
        lses.append(lse)
    w = jax.nn.softmax(jnp.stack(lses, axis=0), axis=0)
    o = jnp.sum(w[..., None] * jnp.stack(outs, axis=0), axis=0)
    return o.reshape(Bsz, S, D_ATTN)

def first_inputs(seed: int = 0) -> dict:
    key = jax.random.key(seed)
    ks = jax.random.split(key, 32)
    f32 = jnp.float32
    G, P, Hg = N_SSM_GROUPS, SSM_STATE, SSM_GROUP

    def nrm(k, shape, scale):
        return jax.random.normal(k, shape, f32) * scale

    def gain(k, shape):
        return 1.0 + 0.01 * jax.random.normal(k, shape, f32)

    a_im = jnp.broadcast_to(math.pi * jnp.arange(P, dtype=f32), (DEPTH, G, P))
    a_im = a_im + 0.01 * jax.random.normal(ks[9], (DEPTH, G, P), f32)
    return {
        "x": jax.random.normal(ks[0], (BATCH, SEQ, D_MODEL), f32),
        "ffn1_norm": gain(ks[1], (DEPTH, D_MODEL)),
        "ffn1_w_gate": nrm(ks[2], (DEPTH, D_MODEL, D_FF), D_MODEL ** -0.5),
        "ffn1_w_up": nrm(ks[3], (DEPTH, D_MODEL, D_FF), D_MODEL ** -0.5),
        "ffn1_w_down": nrm(ks[4], (DEPTH, D_FF, D_MODEL), D_FF ** -0.5),
        "mix_norm": gain(ks[5], (DEPTH, D_MODEL)),
        "w_in": nrm(ks[6], (DEPTH, D_MODEL, 3 * D_ATTN + D_SSM), D_MODEL ** -0.5),
        "ssm_log_dt": jax.random.uniform(ks[7], (DEPTH, G), f32, math.log(DT_MIN), math.log(DT_MAX)),
        "ssm_a_re": -0.5 + 0.01 * jax.random.normal(ks[8], (DEPTH, G, P), f32),
        "ssm_a_im": a_im,
        "ssm_b_re": nrm(ks[10], (DEPTH, G, P, Hg), (2 * Hg) ** -0.5),
        "ssm_b_im": nrm(ks[11], (DEPTH, G, P, Hg), (2 * Hg) ** -0.5),
        "ssm_c_re": nrm(ks[12], (DEPTH, G, Hg, P), (2 * P) ** -0.5),
        "ssm_c_im": nrm(ks[13], (DEPTH, G, Hg, P), (2 * P) ** -0.5),
        "ssm_d": nrm(ks[14], (DEPTH, G, Hg), 1.0),
        "ssm_w_glu": nrm(ks[15], (DEPTH, D_SSM, D_SSM), D_SSM ** -0.5),
        "ssm_b_glu": nrm(ks[16], (DEPTH, D_SSM), 0.01),
        "ssm_out_norm": gain(ks[17], (DEPTH, D_SSM)),
        "attn_out_norm": gain(ks[18], (DEPTH, D_ATTN)),
        "w_out": nrm(ks[19], (DEPTH, D_MIX, D_MODEL), D_MIX ** -0.5),
        "ffn2_norm": gain(ks[20], (DEPTH, D_MODEL)),
        "ffn2_w_gate": nrm(ks[21], (DEPTH, D_MODEL, D_FF), D_MODEL ** -0.5),
        "ffn2_w_up": nrm(ks[22], (DEPTH, D_MODEL, D_FF), D_MODEL ** -0.5),
        "ffn2_w_down": nrm(ks[23], (DEPTH, D_FF, D_MODEL), D_FF ** -0.5),
        "final_norm": gain(ks[24], (D_MODEL,)),
    }

def first_block(x, ffn1_norm, ffn1_w_gate, ffn1_w_up, ffn1_w_down, mix_norm, w_in,
              ssm_log_dt, ssm_a_re, ssm_a_im, ssm_b_re, ssm_b_im, ssm_c_re, ssm_c_im, ssm_d,
              ssm_w_glu, ssm_b_glu, ssm_out_norm, attn_out_norm, w_out,
              ffn2_norm, ffn2_w_gate, ffn2_w_up, ffn2_w_down, final_norm):
    h = x
    for l in range(DEPTH):
        h = h + 0.5 * swiglu(rmsnorm(h, ffn1_norm[l]), ffn1_w_gate[l], ffn1_w_up[l], ffn1_w_down[l])
        hn = rmsnorm(h, mix_norm[l])
        proj = hn @ w_in[l]
        q, k, v, u = jnp.split(proj, [D_ATTN, 2 * D_ATTN, 3 * D_ATTN], axis=-1)
        y_ssm = s5_mixer(u, ssm_log_dt[l], ssm_a_re[l], ssm_a_im[l], ssm_b_re[l], ssm_b_im[l],
                         ssm_c_re[l], ssm_c_im[l], ssm_d[l], ssm_w_glu[l], ssm_b_glu[l])
        y_att = dilated_attention(q, k, v)
        mixed = jnp.concatenate([rmsnorm(y_ssm, ssm_out_norm[l]).astype(h.dtype),
                                 rmsnorm(y_att, attn_out_norm[l]).astype(h.dtype)], axis=-1)
        h = h + mixed @ w_out[l]
        h = h + 0.5 * swiglu(rmsnorm(h, ffn2_norm[l]), ffn2_w_gate[l], ffn2_w_up[l], ffn2_w_down[l])
    return rmsnorm(h, final_norm)


_first_inputs = first_inputs


def first_inputs(seed=0):
    import zlib

    import numpy as np

    out = dict(_first_inputs(seed))
    spreads = {}
    factors = {'ffn1_norm': 8.0,
     'mix_norm': 14.974,
     'ssm_a_re': 64.0,
     'ssm_b_re': 2.809,
     'ssm_b_im': 2.83,
     'ssm_c_re': 2.829,
     'ssm_c_im': 2.795,
     'ssm_b_glu': 64.0,
     'ssm_out_norm': 64.0,
     'attn_out_norm': 64.0,
     'ffn2_norm': 46.967,
     'final_norm': 32.276}
    for name, (base, spread) in spreads.items():
        noise = np.random.default_rng([zlib.crc32(name.encode()), seed]).standard_normal(out[name].shape)
        drawn = base * np.exp(spread * noise) if base else spread * noise
        out[name] = __import__('jax').numpy.asarray(drawn.astype(out[name].dtype))
    for name, factor in factors.items():
        out[name] = (out[name] * factor).astype(out[name].dtype)
    return out


_narrow_inputs = first_inputs


def first_inputs(seed=0):
    out = dict(_narrow_inputs(seed))
    wider = {'ssm_a_re': 12.0,
     'ssm_out_norm': 6.98,
     'attn_out_norm': 6.89,
     'ffn2_norm': 4.59,
     'final_norm': 6.39}
    for name, times in wider.items():
        mean = out[name].mean()
        out[name] = (mean + times * (out[name] - mean)).astype(out[name].dtype)
    return out


GRID_W = 64
CTX_LEN = 256
NH_A = 8
DK_A = 128
DV_A = 256
QK_A = NH_A * DK_A
V_A = NH_A * DV_A
CONV_W = 3
CHUNK = 64
M_INIT = -1e30
NH_B = 16
NKV_B = 4
HD_B = 128
Q_B = NH_B * HD_B
KV_B = NKV_B * HD_B
ROT_HALF = HD_B // 2
ROPE_THETA = 10000.0
Q_BLOCK = 128
ALPHA = (2 * DEPTH) ** 0.25
BETA = (8 * DEPTH) ** -0.25
KV_WIDTHS = (2 * QK_A, V_A, 4 * NH_A, KV_B, KV_B)
N_KV = 2 * QK_A + V_A + 4 * NH_A + 2 * KV_B
OUT_WIDTHS = (V_A, V_A, Q_B, Q_B, 2 * D_MODEL)
N_IN = N_KV + 2 * V_A + 2 * Q_B + 2 * D_MODEL


def _split(p, widths, start=0):
    outs = []
    off = start
    for w in widths:
        outs.append(p[..., off:off + w])
        off += w
    return outs

def layer_norm(x, w=None, b=None):
    xf = x.astype(jnp.float32)
    mu = xf.mean(-1, keepdims=True)
    var = jnp.mean(jnp.square(xf - mu), -1, keepdims=True)
    y = (xf - mu) * lax.rsqrt(var + EPS)
    if w is not None:
        y = y * w.astype(jnp.float32) + b.astype(jnp.float32)
    return y.astype(x.dtype)

def rms_norm(x, w):
    xf = x.astype(jnp.float32)
    y = xf * lax.rsqrt(jnp.mean(jnp.square(xf), -1, keepdims=True) + EPS)
    return (y * w.astype(jnp.float32)).astype(x.dtype)

def dwconv_centred(x, w, b):
    T = x.shape[1]
    pad = CONV_W // 2
    xp = jnp.pad(x, ((0, 0), (pad, CONV_W - 1 - pad), (0, 0)))
    y = b
    for j in range(CONV_W):
        y = y + xp[:, j:j + T] * w[j]
    return y

def rope_tables(n):
    rows_n = n // GRID_W
    row = jnp.repeat(jnp.arange(rows_n), GRID_W).astype(jnp.float32)
    col = jnp.tile(jnp.arange(GRID_W), rows_n).astype(jnp.float32)
    inv = ROPE_THETA ** (-jnp.arange(0, ROT_HALF, 2, dtype=jnp.float32) / ROT_HALF)
    ang_r = row[:, None] * inv[None]
    ang_c = col[:, None] * inv[None]
    return (jnp.cos(ang_r), jnp.sin(ang_r), jnp.cos(ang_c), jnp.sin(ang_c))

def _rot(xh, cos, sin):
    h = xh.shape[-1] // 2
    x1, x2 = xh[..., :h], xh[..., h:]
    cos = cos[None, :, None, :]
    sin = sin[None, :, None, :]
    return jnp.concatenate([x1 * cos - x2 * sin, x1 * sin + x2 * cos], axis=-1)

def apply_rope_2d(x, rope):
    cr, sr, cc, sc = rope
    xf = x.astype(jnp.float32)
    y = jnp.concatenate([_rot(xf[..., :ROT_HALF], cr, sr),
                         _rot(xf[..., ROT_HALF:], cc, sc)], axis=-1)
    return y.astype(x.dtype)

def zero_state(b):
    return (jnp.zeros((b, NH_A, DV_A, DK_A), jnp.float32),
            jnp.zeros((b, NH_A, DK_A), jnp.float32),
            jnp.full((b, NH_A), M_INIT, jnp.float32))

def mlstm_chunked(q, k, v, log_i, log_f, state):
    B, T, H, _ = q.shape
    nc = T // CHUNK

    def to_chunks(a):
        a = a.reshape((B, nc, CHUNK, H) + a.shape[3:])
        return jnp.moveaxis(a, (1, 3), (0, 2))

    tril = jnp.tril(jnp.ones((CHUNK, CHUNK), bool))

    def step(carry, xs):
        C0, n0, m0 = carry
        qc, kc, vc, ic, fc = xs
        b = jnp.cumsum(fc, axis=-1)
        d = jnp.where(tril, b[..., :, None] - b[..., None, :] + ic[..., None, :], -jnp.inf)
        m_inter = b + m0[..., None]
        m = jnp.maximum(m_inter, d.max(-1))
        w = jnp.exp(d - m[..., None])
        a = jnp.exp(m_inter - m)
        s = jnp.einsum('bhjd,bhsd->bhjs', qc, kc) * w
        num = (a[..., None] * jnp.einsum('bhvd,bhjd->bhjv', C0, qc)
               + jnp.einsum('bhjs,bhsv->bhjv', s, vc))
        den = a * jnp.einsum('bhd,bhjd->bhj', n0, qc) + s.sum(-1)
        h = num / jnp.maximum(jnp.abs(den), jnp.exp(-m))[..., None]
        m_end = m[..., -1]
        w_end = jnp.exp(b[..., -1:] - b + ic - m_end[..., None])
        a_end = a[..., -1]
        C = a_end[..., None, None] * C0 + jnp.einsum('bhs,bhsv,bhsd->bhvd', w_end, vc, kc)
        n = a_end[..., None] * n0 + jnp.einsum('bhs,bhsd->bhd', w_end, kc)
        return (C, n, m_end), h

    xs = tuple(to_chunks(a) for a in (q, k, v, log_i, log_f))
    state, h = lax.scan(step, state, xs)
    h = jnp.moveaxis(h, (0, 2), (1, 3)).reshape(B, T, H, v.shape[-1])
    return h, state

def mlstm_final_state(k, v, log_i, log_f):
    b = jnp.cumsum(log_f, axis=1)
    g = b[:, -1:] - b + log_i
    m = g.max(axis=1)
    w = jnp.exp(g - m[:, None])
    C = jnp.einsum('bth,bthv,bthd->bhvd', w, v, k)
    n = jnp.einsum('bth,bthd->bhd', w, k)
    return (C, n, m)

def _flip(*arrs):
    return [jnp.flip(a, axis=1) for a in arrs]

def mlstm_inputs(qk_pre, v_a, if_a, conv_w, conv_b, b_if):
    B, T = v_a.shape[:2]
    qk = jax.nn.silu(dwconv_centred(qk_pre, conv_w, conv_b)).astype(jnp.float32)
    q = qk[..., :QK_A].reshape(B, T, NH_A, DK_A)
    k = qk[..., QK_A:].reshape(B, T, NH_A, DK_A) * (DK_A ** -0.5)
    v = v_a.astype(jnp.float32).reshape(B, T, NH_A, DV_A)
    gt = (if_a + b_if).astype(jnp.float32).reshape(B, T, 4, NH_A)
    fwd = (gt[:, :, 0], jax.nn.log_sigmoid(gt[:, :, 1]))
    bwd = (gt[:, :, 2], jax.nn.log_sigmoid(gt[:, :, 3]))
    return q, k, v, fwd, bwd

def attn_kv(k_b, v_b, k_norm_w, rope):
    B, T = k_b.shape[:2]
    k = rms_norm(k_b.reshape(B, T, NKV_B, HD_B), k_norm_w)
    if rope is not None:
        k = apply_rope_2d(k, rope)
    return k, v_b.reshape(B, T, NKV_B, HD_B)

def attend_blocks(q, k_all, v_all):
    B, S = q.shape[:2]
    G = NH_B // NKV_B
    nb = S // Q_BLOCK
    qb = q.reshape(B, nb, Q_BLOCK, NKV_B, G, HD_B).transpose(1, 0, 2, 3, 4, 5)
    scale = HD_B ** -0.5

    def one(qblk):
        s = jnp.einsum('bqkgd,btkd->bkgqt', qblk, k_all).astype(jnp.float32) * scale
        p = jax.nn.softmax(s, axis=-1).astype(v_all.dtype)
        return jnp.einsum('bkgqt,btkd->bqkgd', p, v_all)

    o = lax.map(one, qb)
    return o.transpose(1, 0, 2, 3, 4, 5).reshape(B, S, Q_B)

def branch_merge(h_a, o_attn, o_a, z_a, z_b, g_logits, mh_norm_w, w_ba, w_bb, w_out):
    B, T = h_a.shape[:2]
    h = rms_norm(h_a, mh_norm_w.reshape(NH_A, DV_A)).reshape(B, T, V_A)
    y_a = (jax.nn.sigmoid(o_a) * h * jax.nn.silu(z_a)) @ w_ba
    y_b = (o_attn * jax.nn.silu(z_b)) @ w_bb
    g_a, g_b = jnp.split(g_logits, 2, axis=-1)
    return (jax.nn.sigmoid(g_a) * y_a + jax.nn.sigmoid(g_b) * y_b) @ w_out

def trunk_layer(x, ctx, c, c_ctx, rope, w_mod, b_mod, w_in, b_if, conv_w, conv_b,
                mh_norm_w, q_norm_w, k_norm_w, w_ba, w_bb, w_out, ln_w, ln_b, update_ctx):
    B, S = x.shape[:2]
    T_c = ctx.shape[1]
    shift, scale, gate = [m[:, None, :] for m in jnp.split(jax.nn.silu(c) @ w_mod + b_mod, 3, axis=-1)]
    shift_c, scale_c, gate_c = jnp.split(jax.nn.silu(c_ctx) @ w_mod + b_mod, 3, axis=-1)
    u = layer_norm(x) * (1 + scale) + shift
    u_c = layer_norm(ctx) * (1 + scale_c) + shift_c
    p = u @ w_in
    p_c = u_c @ (w_in if update_ctx else w_in[:, :N_KV])

    qk_c, va_c, if_c, kb_c, vb_c = _split(p_c, KV_WIDTHS)
    qc, kc, vc, gf_c, gb_c = mlstm_inputs(qk_c, va_c, if_c, conv_w, conv_b, b_if)
    k_bc, v_bc = attn_kv(kb_c, vb_c, k_norm_w, None)
    if update_ctx:
        h_cf, st_f = mlstm_chunked(qc, kc, vc, *gf_c, zero_state(B))
        h_cb, st_b = mlstm_chunked(*_flip(qc, kc, vc, *gb_c), zero_state(B))
        h_c = (h_cf + jnp.flip(h_cb, axis=1)).astype(ctx.dtype)
        o_ac, z_ac, q_bc, z_bc, g_c = _split(p_c, OUT_WIDTHS, N_KV)
        q_bc = rms_norm(q_bc.reshape(B, T_c, NH_B, HD_B), q_norm_w)
        o_attn_c = attend_blocks(q_bc, k_bc, v_bc)
        out_c = branch_merge(h_c, o_attn_c, o_ac, z_ac, z_bc, g_c, mh_norm_w, w_ba, w_bb, w_out)
        ctx_new = layer_norm(ALPHA * ctx + gate_c * out_c, ln_w, ln_b)
    else:
        st_f = mlstm_final_state(kc, vc, *gf_c)
        st_b = mlstm_final_state(*_flip(kc, vc, *gb_c))
        ctx_new = ctx

    qk_l, va_l, if_l, kb_l, vb_l = _split(p, KV_WIDTHS)
    o_a, z_a, q_b, z_b, g_l = _split(p, OUT_WIDTHS, N_KV)
    ql, kl, vl, gf_l, gb_l = mlstm_inputs(qk_l, va_l, if_l, conv_w, conv_b, b_if)
    h_f, _ = mlstm_chunked(ql, kl, vl, *gf_l, st_f)
    h_b, _ = mlstm_chunked(*_flip(ql, kl, vl, *gb_l), st_b)
    h_l = (h_f + jnp.flip(h_b, axis=1)).astype(x.dtype)

    q_l = apply_rope_2d(rms_norm(q_b.reshape(B, S, NH_B, HD_B), q_norm_w), rope)
    k_bl, v_bl = attn_kv(kb_l, vb_l, k_norm_w, rope)
    k_all = jnp.concatenate([k_bc, k_bl], axis=1)
    v_all = jnp.concatenate([v_bc, v_bl], axis=1)
    o_attn = attend_blocks(q_l, k_all, v_all)

    out = branch_merge(h_l, o_attn, o_a, z_a, z_b, g_l, mh_norm_w, w_ba, w_bb, w_out)
    x_new = layer_norm(ALPHA * x + gate * out, ln_w, ln_b)
    return x_new, ctx_new

def second_inputs(seed: int = 0) -> dict:
    key = jax.random.key(seed)
    ks = jax.random.split(key, 20)
    D = D_MODEL
    nrm = jax.random.normal
    b_if_i = 0.1 * nrm(ks[8], (DEPTH, 2, 1, NH_A))
    b_if_f = 3.0 + 0.5 * nrm(ks[9], (DEPTH, 2, 1, NH_A))
    b_if = jnp.concatenate([b_if_i, b_if_f], axis=2).reshape(DEPTH, 4 * NH_A)
    return {
        "x": nrm(ks[0], (BATCH, SEQ, D), jnp.float32),
        "c": nrm(ks[1], (BATCH, D), jnp.float32),
        "ctx": nrm(ks[2], (BATCH, CTX_LEN, D), jnp.float32),
        "c_ctx": nrm(ks[3], (D,), jnp.float32),
        "w_mod": 0.5 * D ** -0.5 * nrm(ks[4], (DEPTH, D, 3 * D), jnp.float32),
        "b_mod": 0.01 * nrm(ks[5], (DEPTH, 3 * D), jnp.float32),
        "w_in": D ** -0.5 * nrm(ks[6], (DEPTH, D, N_IN), jnp.float32),
        "b_if": b_if.astype(jnp.float32),
        "conv_w": CONV_W ** -0.5 * nrm(ks[7], (DEPTH, CONV_W, 2 * QK_A), jnp.float32),
        "conv_b": 0.01 * nrm(ks[10], (DEPTH, 2 * QK_A), jnp.float32),
        "mh_norm_w": 1.0 + 0.02 * nrm(ks[11], (DEPTH, V_A), jnp.float32),
        "q_norm_w": 1.0 + 0.02 * nrm(ks[12], (DEPTH, HD_B), jnp.float32),
        "k_norm_w": 1.0 + 0.02 * nrm(ks[13], (DEPTH, HD_B), jnp.float32),
        "w_branch_a": BETA * V_A ** -0.5 * nrm(ks[14], (DEPTH, V_A, D), jnp.float32),
        "w_branch_b": BETA * Q_B ** -0.5 * nrm(ks[15], (DEPTH, Q_B, D), jnp.float32),
        "w_out": BETA * D ** -0.5 * nrm(ks[16], (DEPTH, D, D), jnp.float32),
        "ln_w": 1.0 + 0.02 * nrm(ks[17], (DEPTH, D), jnp.float32),
        "ln_b": 0.01 * nrm(ks[18], (DEPTH, D), jnp.float32),
    }

def second_block(x, c, ctx, c_ctx, w_mod, b_mod, w_in, b_if, conv_w, conv_b, mh_norm_w,
              q_norm_w, k_norm_w, w_branch_a, w_branch_b, w_out, ln_w, ln_b):
    rope = rope_tables(x.shape[1])
    for layer in range(DEPTH):
        x, ctx = trunk_layer(x, ctx, c, c_ctx, rope, w_mod[layer], b_mod[layer], w_in[layer],
                             b_if[layer], conv_w[layer], conv_b[layer], mh_norm_w[layer],
                             q_norm_w[layer], k_norm_w[layer], w_branch_a[layer],
                             w_branch_b[layer], w_out[layer], ln_w[layer], ln_b[layer],
                             layer < DEPTH - 1)
    return x


_first_inputs_2 = second_inputs


def second_inputs(seed=0):
    import zlib

    import numpy as np

    out = dict(_first_inputs_2(seed))
    spreads = {}
    factors = {'c': 2.965,
     'ctx': 8.0,
     'c_ctx': 8.0,
     'w_mod': 2.834,
     'b_mod': 8.0,
     'w_in': 2.858,
     'b_if': 6.435,
     'conv_w': 195.265,
     'conv_b': 200.0,
     'mh_norm_w': 200.0,
     'q_norm_w': 8.0,
     'k_norm_w': 8.0,
     'w_branch_a': 3.116,
     'w_branch_b': 7.319,
     'w_out': 2.855,
     'ln_w': 24.008,
     'ln_b': 46.902}
    for name, (base, spread) in spreads.items():
        noise = np.random.default_rng([zlib.crc32(name.encode()), seed]).standard_normal(out[name].shape)
        drawn = base * np.exp(spread * noise) if base else spread * noise
        out[name] = __import__('jax').numpy.asarray(drawn.astype(out[name].dtype))
    for name, factor in factors.items():
        out[name] = (out[name] * factor).astype(out[name].dtype)
    return out


_narrow_inputs_2 = second_inputs


def second_inputs(seed=0):

    out = dict(_narrow_inputs_2(seed))
    wider = {'conv_b': 12.0, 'mh_norm_w': 3.49, 'ln_w': 3.26, 'ln_b': 3.28}
    for name, times in wider.items():
        mean = out[name].mean()
        out[name] = (mean + times * (out[name] - mean)).astype(out[name].dtype)
    return out


def setup_inputs(seed=0):
    out = dict(first_inputs(seed))
    for name, value in second_inputs(seed + 1).items():
        if name != "x":
            out[name + "_2"] = value
    return out


def reference(
    x, ffn1_norm, ffn1_w_gate, ffn1_w_up, ffn1_w_down, mix_norm, w_in, ssm_log_dt, ssm_a_re,
    ssm_a_im, ssm_b_re, ssm_b_im, ssm_c_re, ssm_c_im, ssm_d, ssm_w_glu, ssm_b_glu, ssm_out_norm,
    attn_out_norm, w_out, ffn2_norm, ffn2_w_gate, ffn2_w_up, ffn2_w_down, final_norm, c_2,
    ctx_2, c_ctx_2, w_mod_2, b_mod_2, w_in_2, b_if_2, conv_w_2, conv_b_2, mh_norm_w_2,
    q_norm_w_2, k_norm_w_2, w_branch_a_2, w_branch_b_2, w_out_2, ln_w_2, ln_b_2,
):
    x = first_block(
        x, ffn1_norm, ffn1_w_gate, ffn1_w_up, ffn1_w_down, mix_norm, w_in, ssm_log_dt, ssm_a_re,
        ssm_a_im, ssm_b_re, ssm_b_im, ssm_c_re, ssm_c_im, ssm_d, ssm_w_glu, ssm_b_glu,
        ssm_out_norm, attn_out_norm, w_out, ffn2_norm, ffn2_w_gate, ffn2_w_up, ffn2_w_down,
        final_norm,
    )
    return second_block(
        x, c_2, ctx_2, c_ctx_2, w_mod_2, b_mod_2, w_in_2, b_if_2, conv_w_2, conv_b_2,
        mh_norm_w_2, q_norm_w_2, k_norm_w_2, w_branch_a_2, w_branch_b_2, w_out_2, ln_w_2,
        ln_b_2,
    )


_drawn_inputs = setup_inputs


def setup_inputs(seed=0):
    import zlib

    import numpy as np

    out = dict(_drawn_inputs(seed))
    spreads = {}
    factors = {}
    for name, (base, spread) in spreads.items():
        noise = np.random.default_rng([zlib.crc32(name.encode()), seed]).standard_normal(out[name].shape)
        drawn = base * np.exp(spread * noise) if base else spread * noise
        out[name] = __import__('jax').numpy.asarray(drawn.astype(out[name].dtype))
    for name, factor in factors.items():
        out[name] = (out[name] * factor).astype(out[name].dtype)
    return out
```

```python
from contextlib import ExitStack

import numpy as np

import concourse.bass as bass
from concourse import mybir

F32 = mybir.dt.float32
F32R = mybir.dt.float32r
I32 = mybir.dt.int32
ALU = mybir.AluOpType
ACT = mybir.ActivationFunctionType
X_AXIS = mybir.AxisListType.X

P = 128
SEQ = 256
D = 2048
KT = D // P
D_FF = 5504
FT = D_FF // P
BLK = 512
HALF = D // 2
N_HEADS1, HD1 = 16, 64
GROUP, STATE = 16, 64
ST = 32
FRAME = 128
EPS = 1e-6
SLOTS = 4
LEAD = 4
BIG_NEG = -1e30
TWO_PI = 6.283185307179586
NH_A, DK_A, DV_A = 8, 128, 256
VA = DV_A + 1
NH_B, NKV_B, HD_B = 16, 4, 128
GRID_W = 64
ALPHA = 2.0 ** 0.25
N_IN = 17440
GATE0 = 2 * NH_A * DK_A + NH_A * DV_A
KB0 = GATE0 + 4 * NH_A

JOBS = [("ffn1", None, None), ("w_in", 8, 8), ("glu", 4, 2), ("w_out", 8, 4), ("ffn2", None, None),
        ("mod", 8, 12), ("ctx_k", 8, 2), ("ctx_v", 8, 4), ("ctx_kv", 8, 2),
        ("x_qk", 8, 4), ("x_v", 8, 4), ("x_kv", 8, 2), ("x_o", 8, 4), ("x_z", 8, 4), ("x_q", 8, 4), ("x_zb", 8, 4),
        ("x_g", 8, 8), ("ba", 8, 4), ("bb", 8, 4), ("wo", 8, 4)]
DOWN_CHUNKS = 44
FFN_CHUNKS = 11 * 16 + 2 * DOWN_CHUNKS


def plan():
    chunk, pair, where = 0, 0, {}
    for name, nch, nb in JOBS:
        where[name] = (chunk, pair)
        chunk += FFN_CHUNKS if nch is None else nch * nb
        pair += 13 if nch is None else nb // 2
    where["end"] = (chunk, pair)
    return where


AT = plan()
TOTAL_CHUNKS = AT["end"][0]


class Steps:

    def __init__(self, eng, sem):
        self.eng, self.sem, self.n = eng, sem, 0

    def did(self, ins):
        self.n += 1
        ins.then_inc(self.sem, 1)
        return self.n

    def settle(self):
        self.eng.wait_ge(self.sem, self.n)


def build(nc, A, out):
    ctx = ExitStack()
    with ctx:
        def sem(name):
            return ctx.enter_context(nc.semaphore(name))

        top = [16512]

        def at(name, shape, dt=F32, offset=None):
            size = 4 * int(np.prod(shape[1:]))
            if offset is None:
                offset = top[0]
                top[0] += -(-size // 32) * 32
            assert offset + size <= 229344, (name, offset, size)
            return nc.alloc_sbuf_tensor_at(name, shape, dt, offset=offset)

        class Region:
            def __init__(self, offset):
                self.o = offset

            def __call__(self, name, shape, dt=F32):
                t = at(name, shape, dt, offset=self.o)
                self.o += -(-4 * int(np.prod(shape[1:])) // 32) * 32
                return t

        resid = at("resid", [P, 2, D])
        act_hi = at("act_hi", [P, KT, SEQ], F32R)
        act_lo = at("act_lo", [P, KT, SEQ], F32R)
        junk_full = at("junk_full", [P, 2, D], offset=16512 + 4 * 2 * D)
        junk_low = at("junk_low", [P, 2, HALF], offset=16512 + 4 * 2 * D)
        junk_high = at("junk_high", [P, 2, HALF], offset=16512 + 4 * 2 * D + 4 * 2 * HALF)
        w_raw = at("w_raw", [P, SLOTS, 2 * BLK])
        w_hi = at("w_hi", [P, SLOTS, 2 * BLK], F32R)
        w_lo = at("w_lo", [P, SLOTS, 2 * BLK], F32R)
        ident = at("ident_sb", [P, P])
        gains = at("gains_sb", [P, 4, KT])
        stat = at("stat", [P, 64])
        dscale = at("dscale", [P, 2, P])
        stage0 = top[0]

        r = Region(stage0)
        g_hi = r("g_hi", [P, FT, SEQ], F32R)
        g_lo = r("g_lo", [P, FT, SEQ], F32R)
        silu_gate = r("silu_gate", [P, 2, BLK])
        gated = r("gated", [P, 2, BLK])

        acc = ctx.enter_context(nc.psum_tensor("acc", [P, 2, 2, BLK], F32))
        pst = ctx.enter_context(nc.psum_tensor("pst", [P, 4, BLK], F32))

        w_raw_ready = [sem(f"w_raw_ready{s}") for s in range(SLOTS)]
        w_hi_done, w_lo_done, w_used = sem("w_hi_done"), sem("w_lo_done"), sem("w_used")
        fetched = [sem("fetched_a"), sem("fetched_b")]
        consts_ready, x_ready = sem("consts_ready"), sem("x_ready")
        act_steps, dve_steps = sem("act_steps"), sem("dve_steps")
        nt_square, nt_mean, nt_root, nt_diag = sem("nt_square"), sem("nt_mean"), sem("nt_root"), sem("nt_diag")
        nt_turned, nt_hi, nt_lo = sem("nt_turned"), sem("nt_hi"), sem("nt_lo")
        g_turned, g_hi_done, g_lo_done = sem("g_turned"), sem("g_hi_done"), sem("g_lo_done")
        steps = None
        out_done = sem("out_done")

        def cols(w, k0, col, n=BLK):
            return w.rearrange("(k p) n -> p k n", p=P)[:, k0:k0 + 2, bass.ds(col, n)]

        def load_chunk(sp, s, src, c=None):
            c = s if c is None else c
            if not isinstance(c, int) or c >= SLOTS:
                sp.wait_ge(w_lo_done, c - SLOTS + 1)
            view = w_raw[:, s % SLOTS, :]
            if len(src.shape) == 3:
                view = view.rearrange("p (k n) -> p k n", k=src.shape[1])
            sp.dma_start(view, src).then_inc(w_raw_ready[s % SLOTS], 16)

        def round_chunk(act, s, c=None, q=None):
            if s >= TOTAL_CHUNKS:
                return
            act.wait_ge(w_raw_ready[s % SLOTS], 16 * ((s // SLOTS if q is None else q) + 1))
            c = s if c is None else c
            if not isinstance(c, int) or c >= SLOTS:
                act.wait_ge(w_used, c - SLOTS + 1)
            act.activation(w_hi[:, s % SLOTS, :], w_raw[:, s % SLOTS, :], ACT.Copy).then_inc(w_hi_done, 1)

        def rest_chunk(dve, s, c=None):
            if s >= TOTAL_CHUNKS:
                return
            dve.wait_ge(w_hi_done, (s if c is None else c) + 1)
            dve.tensor_tensor(w_lo[:, s % SLOTS, :], w_raw[:, s % SLOTS, :],
                              w_hi[:, s % SLOTS, :].bitcast(F32), ALU.subtract).then_inc(w_lo_done, 1)

        def split_ahead(eng, s0, k, i, nch, first=LEAD, last=None):
            for j in range(first, nch + LEAD if last is None else last):
                s = s0 + j
                c = None if i is None else i * k + s
                if eng is nc_act:
                    round_chunk(eng, s, c, None if i is None else i * (k // SLOTS) + s // SLOTS)
                else:
                    rest_chunk(eng, s, c)

        nc_act, nc_dve = nc.scalar, nc.vector

        def block_product(pe, s0, c0, hi, lo, par, nch, pair, halves=(0, 1)):
            pe.wait_ge(fetched[par], pair + 1)
            for j in range(nch):
                pe.wait_ge(w_lo_done, c0 + j + 1)
                slot = (s0 + j) % SLOTS
                for kk in range(2):
                    k = 2 * j + kk
                    wh = w_hi[:, slot, kk * BLK:(kk + 1) * BLK]
                    wl = w_lo[:, slot, kk * BLK:(kk + 1) * BLK]
                    for h in halves:
                        xh, xl = hi[:, k, h * P:(h + 1) * P], lo[:, k, h * P:(h + 1) * P]
                        o = acc[:, par, h, :]
                        pe.matmul(o, xh, wh, start=k == 0, stop=False)
                        pe.matmul(o, xh, wl, start=False, stop=False)
                        mm = pe.matmul(o, xl, wh, start=False, stop=k == 2 * nch - 1)
                mm.then_inc(w_used, 1)

        turns = {}
        turn_count = [0, 0, 0]

        def plan_turn(name, n, normed):
            turns[name] = (turn_count[0], turn_count[1], n, normed)
            turn_count[0] += n
            turn_count[1] += int(normed)

        for name, n, normed in (("ffn1", 16, True), ("mix", 16, True), ("y", 8, False), ("ssm", 8, True),
                                ("att", 8, True), ("ffn2", 16, True), ("u_ctx", 16, True), ("u_x", 16, True),
                                ("ha", 16, False), ("ob", 16, False), ("merge", 16, False)):
            plan_turn(name, n, normed)

        def turn_act(act, name, src, gain=None, junk=None, width=D, dst=0, bias=None):
            t0, c0, n, normed = turns[name]
            if normed:
                for h in range(2):
                    act.activation(junk[:, h, :], src[:, h, :], ACT.Square,
                                   accum_out=stat[:, h:h + 1]).then_inc(nt_square, 1)
                act.wait_ge(nt_mean, c0 + 1)
                act.activation(stat[:, 4:6], stat[:, 2:4], ACT.Sqrt).then_inc(nt_root, 1)
            for k in range(n):
                act.wait_ge(nt_turned, t0 + k + 1)
                o, i = act_hi[:, dst + k, :], pst[:, (t0 + k) % 4, 0:SEQ]
                if bias is not None:
                    ins = act.activation(o, i, ACT.Identity, scale=gain[:, k:k + 1], bias=bias[:, k:k + 1])
                elif gain is not None:
                    ins = act.activation(o, i, ACT.Copy, scale=gain[:, k:k + 1])
                else:
                    ins = act.activation(o, i, ACT.Copy)
                ins.then_inc(nt_hi, 1)

        def turn_dve(dve, name, gain=None, width=D, dst=0, bias=None, tmp=None):
            t0, c0, n, normed = turns[name]
            if normed:
                dve.wait_ge(nt_square, 2 * (c0 + 1))
                dve.tensor_scalar(stat[:, 2:4], stat[:, 0:2], 1.0 / width, EPS, ALU.mult, ALU.add).then_inc(nt_mean, 1)
                dve.wait_ge(nt_root, c0 + 1)
                steps.did(dve.reciprocal(stat[:, 6:8], stat[:, 4:6]))
                steps.settle()
                for h in range(2):
                    dve.tensor_scalar(dscale[:, h, :], ident[:], stat[:, 6 + h:7 + h], None,
                                      ALU.mult).then_inc(nt_diag, 1)
            for k in range(n):
                dve.wait_ge(nt_hi, t0 + k + 1)
                o, i = act_lo[:, dst + k, :], pst[:, (t0 + k) % 4, 0:SEQ]
                hi = act_hi[:, dst + k, :].bitcast(F32)
                if bias is not None:
                    steps.did(dve.tensor_scalar(tmp[:, k % 2, :], i, gain[:, k:k + 1], bias[:, k:k + 1],
                                                ALU.mult, ALU.add))
                    steps.settle()
                    ins = dve.tensor_tensor(o, tmp[:, k % 2, :], hi, ALU.subtract)
                elif gain is not None:
                    ins = dve.scalar_tensor_tensor(out=o, in0=i, scalar=gain[:, k:k + 1], in1=hi,
                                                   op0=ALU.mult, op1=ALU.subtract)
                else:
                    ins = dve.tensor_tensor(o, i, hi, ALU.subtract)
                ins.then_inc(nt_lo, 1)

        def turn_pe(pe, name, src):
            t0, c0, n, normed = turns[name]
            if normed:
                pe.wait_ge(nt_diag, 2 * (c0 + 1))
            for k in range(n):
                if t0 + k >= 4:
                    pe.wait_ge(nt_lo, t0 + k - 3)
                for h in range(2):
                    o = pst[:, (t0 + k) % 4, h * P:(h + 1) * P]
                    lhs = src[:, h, k * P:(k + 1) * P]
                    if normed:
                        mm = pe.matmul(o, lhs, dscale[:, h, :], start=True, stop=True)
                    else:
                        mm = pe.transpose(o, lhs, ident[:])
                mm.then_inc(nt_turned, 1)

        def turned(eng, name):
            t0, _, n, _ = turns[name]
            eng.wait_ge(nt_lo, t0 + n)

        NB = 11

        def ffn_iterations(eng, name, it):
            s0, p0 = AT[name]
            it(0, s0, s0, p0, None)
            with eng.Fori(1, NB - 1) as i:
                it(i, s0, i * 16 + s0, i + p0, i)
            it(NB - 1, s0 + 16 * (NB - 1), s0 + 16 * (NB - 1), p0 + NB - 1, None)

        def first(b):
            return isinstance(b, int) and b == 0

        def ffn_sp(sp, name, w_gate, w_up, w_down):
            def it(b, s, c, p, i):
                col = D_FF - BLK if isinstance(b, int) and b == NB - 1 else b * BLK
                for m, w in enumerate((w_gate, w_up)):
                    for j in range(8):
                        load_chunk(sp, s + 8 * m + j, cols(w, 2 * j, col), c + 8 * m + j)
            ffn_iterations(sp, name, it)
            s1 = AT[name][0] + 16 * NB
            wd = w_down.rearrange("(k p) n -> p k n", p=P)
            with sp.Fori(0, 2) as i:
                for j in range(DOWN_CHUNKS):
                    load_chunk(sp, s1 + j, wd[:, min(j, FT - 1), bass.ds(i * 1024, 1024)],
                               i * DOWN_CHUNKS + s1 + j)

        def tiles_of(b):
            return slice(FT - 4, FT) if isinstance(b, int) and b == NB - 1 else (
                slice(4 * b, 4 * b + 4) if isinstance(b, int) else bass.ds(b * 4, 4))

        turned_tiles = pst[:, 0:2, :].rearrange("p a (b t) -> p (a b) t", b=2)

        def ffn_act(act, name, n_use):
            b0 = NB * n_use

            def hi_tiles(b):
                act.wait_ge(g_turned, b + (b0 + 1))
                act.activation(g_hi[:, tiles_of(b), :], turned_tiles, ACT.Copy).then_inc(g_hi_done, 1)

            def it(b, s, c, p, i):
                split_ahead(act, s, 16, i, 16, LEAD, 8 + LEAD)
                act.wait_ge(w_used, c + 8)
                act.wait_ge(fetched[1], p + 1)
                act.activation(silu_gate[:], acc[:, 0, :, :], ACT.Silu).then_inc(fetched[0], 1)
                if not first(b):
                    hi_tiles(b - 1)
                split_ahead(act, s, 16, i, 16, 8 + LEAD, 16 + LEAD)
            ffn_iterations(act, name, it)
            hi_tiles(NB - 1)
            s1 = AT[name][0] + 16 * NB
            with act.Fori(0, 2) as i:
                split_ahead(act, s1, DOWN_CHUNKS, i, DOWN_CHUNKS)

        def ffn_dve(dve, name, n_use):
            b0 = NB * n_use

            def lo_tiles(b):
                dve.wait_ge(g_hi_done, b + (b0 + 1))
                dve.tensor_tensor(g_lo[:, tiles_of(b), :], turned_tiles,
                                  g_hi[:, tiles_of(b), :].bitcast(F32), ALU.subtract).then_inc(g_lo_done, 1)

            def it(b, s, c, p, i):
                split_ahead(dve, s, 16, i, 16, LEAD, 8 + LEAD)
                if not first(b):
                    lo_tiles(b - 1)
                split_ahead(dve, s, 16, i, 16, 8 + LEAD, 16 + LEAD)
                dve.wait_ge(w_used, c + 16)
                dve.wait_ge(fetched[0], p + 2)
                if not first(b):
                    dve.wait_ge(g_turned, b + b0)
                dve.tensor_tensor(gated[:], silu_gate[:], acc[:, 1, :, :], ALU.mult).then_inc(fetched[1], 1)
            ffn_iterations(dve, name, it)
            lo_tiles(NB - 1)
            s1 = AT[name][0] + 16 * NB
            with dve.Fori(0, 2) as i:
                split_ahead(dve, s1, DOWN_CHUNKS, i, DOWN_CHUNKS)
                dve.wait_ge(w_used, i * DOWN_CHUNKS + (s1 + DOWN_CHUNKS))
                for par in range(2):
                    o = resid[:, :, bass.ds(i * 1024 + par * BLK, BLK)]
                    dve.scalar_tensor_tensor(out=o, in0=acc[:, par, :, :], scalar=0.5, in1=o,
                                             op0=ALU.mult, op1=ALU.add).then_inc(fetched[par], 1)

        def ffn_pe(pe, name, n_use):
            b0 = NB * n_use

            def turn_gated(b, p):
                pe.wait_ge(fetched[1], p + 2)
                pe.wait_ge(g_lo_done, b + (b0 + 1))
                for t in range(4):
                    for h in range(2):
                        mm = pe.transpose(turned_tiles[:, t, h * P:(h + 1) * P],
                                          gated[:, h, t * P:(t + 1) * P], ident[:])
                mm.then_inc(g_turned, 1)

            def it(b, s, c, p, i):
                block_product(pe, s, c, act_hi, act_lo, 0, 8, p)
                if not first(b):
                    turn_gated(b - 1, p - 1)
                block_product(pe, s + 8, c + 8, act_hi, act_lo, 1, 8, p)
            ffn_iterations(pe, name, it)
            s0, p0 = AT[name]
            turn_gated(NB - 1, p0 + NB - 1)
            s1 = s0 + 16 * NB
            pe.wait_ge(g_lo_done, NB + b0 + 1)
            with pe.Fori(0, 2) as i:
                for par in range(2):
                    pe.wait_ge(fetched[par], i + (p0 + NB + 1))
                for j in range(FT):
                    pe.wait_ge(w_lo_done, i * DOWN_CHUNKS + (s1 + j + (1 if j < FT - 1 else 2)))
                    slot = (s1 + j) % SLOTS
                    for par in range(2):
                        wh = w_hi[:, slot, par * BLK:(par + 1) * BLK]
                        wl = w_lo[:, slot, par * BLK:(par + 1) * BLK]
                        for h in range(2):
                            gh, gl = g_hi[:, j, h * P:(h + 1) * P], g_lo[:, j, h * P:(h + 1) * P]
                            o = acc[:, par, h, :]
                            pe.matmul(o, gh, wh, start=j == 0, stop=False)
                            pe.matmul(o, gh, wl, start=False, stop=False)
                            mm = pe.matmul(o, gl, wh, start=False, stop=j == FT - 1)
                    mm.then_inc(w_used, 1 if j < FT - 1 else 2)

        def job(name):
            nch, nb = next((n, b) for j, n, b in JOBS if j == name)
            return AT[name] + (nch, nb)

        def pairs(eng, name, body):
            s0, p0, nch, nb = job(name)
            if nb == 2 or name == JOBS[-1][0]:
                for i in range(nb // 2):
                    s = s0 + 2 * nch * i
                    body(i, s, s, p0 + i)
            else:
                with eng.Fori(0, nb // 2) as i:
                    body(i, s0, i * (2 * nch) + s0, i + p0)

        def stream_sp(sp, name, w, col0):
            nch = job(name)[2]

            def body(i, s, c, p):
                for m in range(2):
                    for j in range(nch):
                        load_chunk(sp, s + nch * m + j, cols(w, 2 * j, (i * 2 + m) * BLK + col0), c + nch * m + j)
            pairs(sp, name, body)

        def stream_pe(pe, name, halves=(0, 1)):
            nch = job(name)[2]

            def body(i, s, c, p):
                for m in range(2):
                    block_product(pe, s + nch * m, c + nch * m, act_hi, act_lo, m, nch, p, halves)
            pairs(pe, name, body)

        def stream_split(eng, name, fetch=None):
            nch = job(name)[2]

            def body(i, s, c, p):
                for m in range(2):
                    split_ahead(eng, s + nch * m, 2 * nch, None if isinstance(i, int) else i, nch)
                    if fetch is not None:
                        eng.wait_ge(w_used, c + nch * (m + 1))
                        fetch(m, i * 2 + m, p)
            pairs(eng, name, body)

        r = Region(stage0)
        prj = r("prj", [P, 2, 4 * HALF])
        q_nat, k_nat, v_nat, u_nat = (prj[:, :, n * HALF:(n + 1) * HALF] for n in range(4))
        att, ssm_y, spare = q_nat, k_nat, v_nat
        u_t = r("u_t", [P, 8, SEQ])
        mix_x = r.o
        r = Region(mix_x)
        q_t, k_t = r("q_t", [P, 8, SEQ]), r("k_t", [P, 8, SEQ])
        log_mask = r("log_mask", [P, 3 * P])
        scores, probs, probs_t = (r(n, [P, 2, 3 * P]) for n in ("scores", "probs", "probs_t"))
        row_max, row_sum, row_inv = (r(n, [P, 2 * N_HEADS1]) for n in ("row_max", "row_sum", "row_inv"))
        r = Region(mix_x)
        rot_cos, rot_sin = r("rot_cos", [P, ST, FRAME]), r("rot_sin", [P, ST, FRAME])
        c_re, c_im, cf_re, cf_im = (r(n, [P, ST, 2 * GROUP]) for n in ("c_re", "c_im", "cf_re", "cf_im"))
        b_re, b_im = (r(n, [P, 8, P]) for n in ("b_re", "b_im"))
        par_ = r("ssm_par", [P, 24, ST])
        r2 = Region(r.o)
        turn_tmp = r2("turn_tmp", [P, ST, FRAME // 2])
        prod = r("prod", [P, 4, SEQ])
        st_z = r("st_z", [P, 2, SEQ])
        st_s = r("st_s", [P, 2, 2, SEQ])
        row_d = at("row_d", [P, HALF], offset=stage0 + 4 * 4 * D + 4 * 8 * SEQ + 4 * 2 * ST * FRAME)
        row_bglu = at("row_bglu", [P, HALF], offset=stage0 + 4 * 4 * D + 4 * 8 * SEQ + 4 * 2 * ST * FRAME + 4 * HALF)

        att_consts, ssm_consts, row_ready = sem("att_consts"), sem("ssm_consts"), sem("row_ready")
        tq_turned, tq_fetched = sem("tq_turned"), [sem("tq_fetched_act"), sem("tq_fetched_dve")]
        at_scores, at_max, at_probs, at_turned, at_copied, at_out, at_fetched = (
            sem("at_" + n) for n in ("scores", "max", "probs", "turned", "copied", "out", "fetched"))
        sp_step = sem("ssm_par_act")
        sp_dve = sem("ssm_par_dve")
        ssm_b, ssm_b_read, ssm_s, ssm_y_done, ssm_y_read, ssm_gelu = (
            sem(n) for n in ("ssm_b", "ssm_b_read", "ssm_s", "ssm_y_done", "ssm_y_read", "ssm_gelu"))
        glu_pre, glu_sig, glu_out = sem("glu_pre"), sem("glu_sig"), sem("glu_out")

        def fetch_prj(act):
            def fetch(m, blk, p, off):
                act.activation(prj[:, :, bass.ds(blk * BLK + off, BLK)], acc[:, m, :, :],
                               ACT.Copy).then_inc(fetched[m], 1)
            return fetch

        TQ = [(q_t, 0, n) for n in range(4)] + [(k_t, HALF, n) for n in range(4)] + [(u_t, 3 * HALF, n) for n in range(4)]

        def turn_qku_pe(pe):
            s0, p0, nch, nb = job("w_in")
            for m in range(2):
                pe.wait_ge(fetched[m], p0 + nb // 2 + 1)
            for n, (dst, col, t) in enumerate(TQ):
                if n >= 4:
                    pe.wait_ge(tq_fetched[n % 2], (n - 4) // 2 + 1)
                for tt in range(2):
                    for h in range(2):
                        c = col + (2 * t + tt) * P
                        mm = pe.transpose(pst[:, n % 4, tt * SEQ + h * P:tt * SEQ + (h + 1) * P],
                                          prj[:, h, c:c + P], ident[:])
                mm.then_inc(tq_turned, 1)

        def turn_qku_fetch(eng, par, copy):
            for n, (dst, col, t) in enumerate(TQ):
                if n % 2 == par:
                    eng.wait_ge(tq_turned, n + 1)
                    copy(dst[:, 2 * t:2 * t + 2, :], pst[:, n % 4, :].rearrange("p (a t) -> p a t", a=2)).then_inc(
                        tq_fetched[par], 1)

        def head_rows(n):
            return slice(64 * (n % 2), 64 * (n % 2) + 64), n // 2

        def attention1_pe(pe):
            for par in range(2):
                pe.wait_ge(tq_fetched[par], 6)
            for s in range(N_HEADS1 + 2):
                if s < N_HEADS1:
                    if s >= 2:
                        pe.wait_ge(at_max, s - 1)
                    rows, t = head_rows(s)
                    pe.matmul(pst[:, s % 2, 0:P], q_t[rows, t, 0:P], k_t[rows, t, 0:P], start=True, stop=True)
                    pe.matmul(pst[:, s % 2, P:3 * P], q_t[rows, t, P:SEQ], k_t[rows, t, :],
                              start=True, stop=True).then_inc(at_scores, 1)
                if 1 <= s <= N_HEADS1:
                    n = s - 1
                    pe.wait_ge(at_probs, n + 1)
                    if n >= 2:
                        pe.wait_ge(at_copied, n - 1)
                    for b in range(3):
                        mm = pe.transpose(pst[:, 2 + n % 2, b * P:(b + 1) * P],
                                          probs[:, n % 2, b * P:(b + 1) * P], ident[:])
                    mm.then_inc(at_turned, 1)
                if s >= 2:
                    n = s - 2
                    pe.wait_ge(at_copied, n + 1)
                    if n >= 2:
                        pe.wait_ge(at_fetched, n - 1)
                    o = acc[:, 0, n % 2, :]
                    v = v_nat[:, :, n * HD1:(n + 1) * HD1]
                    pe.matmul(o[:, 0:HD1], probs_t[:, n % 2, 0:P], v[:, 0, :], start=True, stop=True)
                    pe.matmul(o[:, HD1:2 * HD1], probs_t[:, n % 2, P:2 * P], v[:, 0, :], start=True, stop=False)
                    pe.matmul(o[:, HD1:2 * HD1], probs_t[:, n % 2, 2 * P:3 * P], v[:, 1, :],
                              start=False, stop=True).then_inc(at_out, 1)

        def attention1_act(act):
            for s in range(N_HEADS1 + 1):
                if s < N_HEADS1:
                    act.wait_ge(at_max, s + 1)
                    if s >= 2:
                        act.wait_ge(at_turned, s - 1)
                    for h, (a, b) in enumerate(((0, P), (P, 3 * P))):
                        ins = act.activation(probs[:, s % 2, a:b], scores[:, s % 2, a:b], ACT.Exp,
                                             bias=row_max[:, 2 * s + h:2 * s + h + 1],
                                             accum_out=row_sum[:, 2 * s + h:2 * s + h + 1])
                    ins.then_inc(at_probs, 1)
                if s >= 1:
                    n = s - 1
                    act.wait_ge(at_turned, n + 1)
                    if n >= 2:
                        act.wait_ge(at_out, n - 1)
                    act.activation(probs_t[:, n % 2, :], pst[:, 2 + n % 2, 0:3 * P], ACT.Copy).then_inc(at_copied, 1)

        def attention1_dve(dve):
            dve.wait_ge(att_consts, 16)
            for s in range(N_HEADS1 + 2):
                if s < N_HEADS1:
                    dve.wait_ge(at_scores, s + 1)
                    if s >= 2:
                        dve.wait_ge(at_probs, s - 1)
                    steps.did(dve.scalar_tensor_tensor(out=scores[:, s % 2, :], in0=pst[:, s % 2, 0:3 * P],
                                                       scalar=HD1 ** -0.5, in1=log_mask[:], op0=ALU.mult, op1=ALU.add))
                    steps.settle()
                    for h, (a, b) in enumerate(((0, P), (P, 3 * P))):
                        ins = dve.tensor_reduce(row_inv[:, 2 * s + h:2 * s + h + 1], scores[:, s % 2, a:b],
                                                X_AXIS, ALU.max)
                    steps.did(ins)
                    steps.settle()
                    dve.tensor_scalar(row_max[:, 2 * s:2 * s + 2], row_inv[:, 2 * s:2 * s + 2], -1.0, None,
                                      ALU.mult).then_inc(at_max, 1)
                if s >= 2:
                    n = s - 2
                    dve.wait_ge(at_out, n + 1)
                    steps.did(dve.reciprocal(row_inv[:, 2 * n:2 * n + 2], row_sum[:, 2 * n:2 * n + 2]))
                    steps.settle()
                    dve.tensor_tensor(att[:, :, n * HD1:(n + 1) * HD1],
                                      acc[:, 0, n % 2, 0:2 * HD1].rearrange("p (h e) -> p h e", h=2),
                                      row_inv[:, 2 * n:2 * n + 2].unsqueeze(2).broadcast_to([P, 2, HD1]),
                                      ALU.mult).then_inc(at_fetched, 1)

        LDT, LR, LI, DT, LRDT, TH, MAG, N_, RED, SINH, SIN, COS, LRE, LIM, NR, DEN, FRE, FIM, T0, T1 = range(20)

        def pr(n):
            return par_[:, n, :]

        def ssm_params_act(act):
            act.wait_ge(ssm_consts, 16 * 7)
            act.activation(pr(DT), pr(LDT), ACT.Exp).then_inc(sp_step, 1)
            act.wait_ge(sp_dve, 1)
            act.activation(pr(MAG), pr(LRDT), ACT.Exp).then_inc(sp_step, 1)
            act.wait_ge(sp_dve, 2)
            act.activation(pr(SINH), pr(RED), ACT.Sin, scale=0.5).then_inc(sp_step, 1)
            act.activation(pr(SIN), pr(RED), ACT.Sin).then_inc(sp_step, 1)

        def ssm_params_dve(dve):
            def tt(o, a, b, op):
                steps.did(dve.tensor_tensor(o, a, b, op))

            def ts(o, a, s1, op0, s2=None, op1=None):
                if s2 is None:
                    steps.did(dve.tensor_scalar(o, a, s1, None, op0))
                else:
                    steps.did(dve.tensor_scalar(o, a, s1, s2, op0, op1))
            M, A_, S = ALU.mult, ALU.add, ALU.subtract
            dve.wait_ge(ssm_consts, 16 * 7)
            dve.wait_ge(sp_step, 1)
            tt(pr(TH), pr(LI), pr(DT), M)
            dve.tensor_tensor(pr(LRDT), pr(LR), pr(DT), M).then_inc(sp_dve, 1)
            steps.settle()
            magic = 1.5 * 2.0 ** 23
            ts(pr(N_), pr(TH), 1.0 / TWO_PI, M, magic, A_)
            steps.settle()
            ts(pr(T0), pr(N_), magic, S)
            steps.settle()
            c1 = 6.28125
            c2 = 0.0019350051879882812
            c3 = TWO_PI - c1 - c2
            src = TH
            for c, dst in ((c1, T1), (c2, RED), (c3, T1)):
                steps.did(dve.scalar_tensor_tensor(out=pr(dst), in0=pr(T0), scalar=-c, in1=pr(src), op0=M, op1=A_))
                steps.settle()
                src = dst
            dve.tensor_scalar(pr(RED), pr(T1), 3.1415925, -3.1415925, ALU.min, ALU.max).then_inc(sp_dve, 1)
            dve.wait_ge(sp_step, 4)
            tt(pr(T0), pr(SINH), pr(SINH), M)
            tt(pr(LIM), pr(MAG), pr(SIN), M)
            tt(pr(DEN), pr(LR), pr(LR), M)
            tt(pr(T1), pr(LI), pr(LI), M)
            steps.settle()
            ts(pr(COS), pr(T0), -2.0, M, 1.0, A_)
            tt(pr(DEN), pr(DEN), pr(T1), A_)
            steps.settle()
            tt(pr(LRE), pr(MAG), pr(COS), M)
            steps.did(dve.reciprocal(pr(DEN), pr(DEN)))
            steps.did(dve.tensor_copy(rot_cos[:, :, 0:1], pr(COS).unsqueeze(2)))
            steps.did(dve.tensor_copy(rot_sin[:, :, 0:1], pr(SIN).unsqueeze(2)))
            steps.settle()
            ts(pr(NR), pr(LRE), 1.0, S)
            steps.settle()
            tt(pr(FRE), pr(NR), pr(LR), M)
            tt(pr(T0), pr(LIM), pr(LI), M)
            tt(pr(FIM), pr(LIM), pr(LR), M)
            tt(pr(T1), pr(NR), pr(LI), M)
            steps.settle()
            tt(pr(FRE), pr(FRE), pr(T0), A_)
            tt(pr(FIM), pr(FIM), pr(T1), S)
            steps.settle()
            tt(pr(FRE), pr(FRE), pr(DEN), M)
            tt(pr(FIM), pr(FIM), pr(DEN), M)
            steps.settle()
            wide = [P, ST, 2 * GROUP]
            fr, fi = pr(FRE).unsqueeze(2).broadcast_to(wide), pr(FIM).unsqueeze(2).broadcast_to(wide)
            tmp = turn_tmp[:, :, 0:2 * GROUP]
            tt(cf_re[:], c_re[:], fr, M)
            tt(tmp, c_im[:], fi, M)
            steps.settle()
            tt(cf_re[:], cf_re[:], tmp, S)
            tt(cf_im[:], c_re[:], fi, M)
            steps.settle()
            tt(tmp, c_im[:], fr, M)
            steps.settle()
            steps.did(dve.scalar_tensor_tensor(out=cf_im[:], in0=cf_im[:], scalar=-1.0, in1=tmp, op0=M, op1=S))
            steps.settle()
            dve.sem_inc(sp_dve, 1)
            w = 1
            while w < FRAME:
                shape = [P, ST, w]
                ec = rot_cos[:, :, w - 1:w].broadcast_to(shape)
                es = rot_sin[:, :, w - 1:w].broadcast_to(shape)
                co, si = rot_cos[:, :, 0:w], rot_sin[:, :, 0:w]
                nc_, ns_ = rot_cos[:, :, w:2 * w], rot_sin[:, :, w:2 * w]
                tmp = turn_tmp[:, :, 0:w]
                tt(nc_, co, ec, M)
                tt(ns_, co, es, M)
                tt(tmp, si, es, M)
                steps.settle()
                tt(nc_, nc_, tmp, S)
                steps.settle()
                tt(tmp, si, ec, M)
                steps.settle()
                tt(ns_, ns_, tmp, A_)
                steps.settle()
                w *= 2

        def ssm_pe(pe):
            def out_of(i):
                pe.wait_ge(ssm_s, i + 1)
                g, o = i // 16, GROUP * 2 * (i % 16)
                for h in range(2):
                    dst = acc[:, g, h, o:o + 2 * GROUP]
                    pe.matmul(dst, st_s[:, i % 2, 0, h * P:(h + 1) * P], cf_re[:, i, :], start=True, stop=False)
                    mm = pe.matmul(dst, st_s[:, i % 2, 1, h * P:(h + 1) * P], cf_im[:, i, :], start=False, stop=True)
                mm.then_inc(ssm_y_done, 1)
            pe.wait_ge(at_fetched, N_HEADS1)
            pe.wait_ge(at_copied, N_HEADS1)
            pe.wait_ge(ssm_consts, 16 * 7)
            for i in range(ST):
                if i >= 2:
                    pe.wait_ge(ssm_b_read, i - 1)
                c, j = i // 4, 32 * (i % 4)
                for part, b in enumerate((b_re, b_im)):
                    mm = pe.matmul(pst[:, i % 2, part * SEQ:(part + 1) * SEQ], b[j:j + 32, c, :],
                                   u_t[j:j + 32, c, :], start=True, stop=True)
                mm.then_inc(ssm_b, 1)
                if i >= 1:
                    out_of(i - 1)
            out_of(ST - 1)

        def ssm_dve(dve):
            M, A_, S = ALU.mult, ALU.add, ALU.subtract

            def framed(x):
                return x.rearrange("p (f j) -> p f j", f=2)
            for i in range(ST):
                dve.wait_ge(ssm_b, i + 1)
                if i >= 1:
                    dve.wait_ge(ssm_s, i)
                bu_re, bu_im = framed(pst[:, i % 2, 0:SEQ]), framed(pst[:, i % 2, SEQ:2 * SEQ])
                co = rot_cos[:, i, :].unsqueeze(1).broadcast_to([P, 2, FRAME])
                si = rot_sin[:, i, :].unsqueeze(1).broadcast_to([P, 2, FRAME])
                dve.tensor_tensor(framed(prod[:, 0, :]), bu_re, co, M)
                dve.tensor_tensor(framed(prod[:, 1, :]), bu_im, si, M)
                dve.tensor_tensor(framed(prod[:, 2, :]), bu_im, co, M)
                steps.did(dve.tensor_tensor(framed(prod[:, 3, :]), bu_re, si, M))
                steps.settle()
                dve.sem_inc(ssm_b_read, 1)
                dve.tensor_tensor(prod[:, 0, :], prod[:, 0, :], prod[:, 1, :], A_)
                steps.did(dve.tensor_tensor(prod[:, 2, :], prod[:, 2, :], prod[:, 3, :], S))
                steps.settle()
                if i >= 2:
                    dve.wait_ge(ssm_y_done, i - 1)
                mag = par_[:, MAG, i:i + 1].broadcast_to([P, FRAME])
                for f in range(2):
                    a, b = f * FRAME, (f + 1) * FRAME
                    for part in range(2):
                        init = 0.0 if f == 0 else st_s[:, i % 2, part, a - 1:a]
                        ins = dve.tensor_tensor_scan(st_z[:, part, a:b], mag, prod[:, 2 * part, a:b], init, M, A_)
                    steps.did(ins)
                    steps.settle()
                    co, si = rot_cos[:, i, :], rot_sin[:, i, :]
                    zr, zi = st_z[:, 0, a:b], st_z[:, 1, a:b]
                    dve.tensor_tensor(prod[:, 0, a:b], zr, co, M)
                    dve.tensor_tensor(prod[:, 1, a:b], zi, si, M)
                    dve.tensor_tensor(prod[:, 2, a:b], zr, si, M)
                    steps.did(dve.tensor_tensor(prod[:, 3, a:b], zi, co, M))
                    steps.settle()
                    dve.tensor_tensor(st_s[:, i % 2, 0, a:b], prod[:, 0, a:b], prod[:, 1, a:b], S)
                    ins = dve.tensor_tensor(st_s[:, i % 2, 1, a:b], prod[:, 2, a:b], prod[:, 3, a:b], A_)
                    if f == 0:
                        steps.did(ins)
                        steps.settle()
                    else:
                        ins.then_inc(ssm_s, 1)
                if i % 16 == 15:
                    g = i // 16
                    if g == 0:
                        dve.wait_ge(row_ready, 32)
                        for h in range(2):
                            ins = dve.tensor_tensor(u_nat[:, h, :], u_nat[:, h, :], row_d[:], M)
                        steps.did(ins)
                        steps.settle()
                    dve.wait_ge(ssm_y_done, i + 1)
                    dve.tensor_tensor(ssm_y[:, :, g * BLK:(g + 1) * BLK], acc[:, g, :, :],
                                      u_nat[:, :, g * BLK:(g + 1) * BLK], A_).then_inc(ssm_y_read, 1)

        def ssm_act(act):
            for g in range(2):
                act.wait_ge(ssm_y_read, g + 1)
                y = ssm_y[:, :, g * BLK:(g + 1) * BLK]
                act.activation(y, y, ACT.Gelu_apprx_tanh).then_inc(ssm_gelu, 1)

        def glu_fetch_dve(dve):
            def fetch(m, blk, p):
                cs = slice(m * BLK, (m + 1) * BLK)
                dve.tensor_tensor(spare[:, :, cs], acc[:, m, :, :],
                                  row_bglu[:, cs].unsqueeze(1).broadcast_to([P, 2, BLK]), ALU.add).then_inc(fetched[m], 1)
            return fetch

        def fetch_residual(dve):
            def fetch(m, blk, p):
                o = resid[:, :, bass.ds(blk * BLK, BLK)]
                dve.tensor_tensor(o, acc[:, m, :, :], o, ALU.add).then_inc(fetched[m], 1)
            return fetch

        def glu_act(act):
            for m in range(2):
                act.wait_ge(fetched[m], AT["w_out"][1] + 1)
                o = spare[:, :, m * BLK:(m + 1) * BLK]
                act.activation(o, o, ACT.Sigmoid).then_inc(glu_sig, 1)

        def glu_dve(dve):
            for m in range(2):
                dve.wait_ge(glu_sig, m + 1)
                o = ssm_y[:, :, m * BLK:(m + 1) * BLK]
                dve.tensor_tensor(o, o, spare[:, :, m * BLK:(m + 1) * BLK], ALU.mult).then_inc(glu_out, 1)

        top2 = stage0 + 4 * (2 * FT * SEQ + 4 * BLK)
        r = Region(top2)
        gate_w_hi, gate_w_lo = r("gate_w_hi", [P, KT, 4 * NH_A], F32R), r("gate_w_lo", [P, KT, 4 * NH_A], F32R)
        neg_mask = at("neg_mask_sb", [P, 2, 2, SEQ], offset=top2)
        gate_w = r("gate_w", [P, KT, 4 * NH_A])
        c_col = r("c_col", [P, 2, KT])
        b_mod_col = r("b_mod_col", [P, 3 * KT])
        mod_col = r("mod_col", [P, 3 * KT, 2])
        conv_w, conv_b = r("conv_w_sb", [P, KT, 3]), r("conv_b_sb", [P, KT])
        b_if_row = r("b_if_row", [P, 4 * NH_A])
        mh_col = r("mh_col", [P, KT])
        q_gain, k_gain = r("q_gain", [P, HD_B]), r("k_gain", [P, HD_B])
        rope = r("rope_sb", [P, 2, 2, 2, 32])
        m_rows = [r(f"m_rows{d}", [NH_A, SEQ + 1]) for d in range(2)]
        ones_row = r("ones_row", [NH_A, SEQ])
        gate_pre, gate_log, gate_tmp = (r(n, [P, 2, 4 * NH_A]) for n in ("gate_pre", "gate_log", "gate_tmp"))
        w_col = r("w_col", [P, 2, 2, NH_A])
        g_col, e_col = r("g_col", [P, 2, 2, NH_A]), r("e_col", [P, 2, 2, NH_A])
        row_s = [r(f"row_s{d}", [NH_A, 4]) for d in range(2)]
        r = Region(stage0)
        keys_t, vals = r("keys_t", [P, NKV_B, 2 * SEQ]), r("vals", [P, 4, NKV_B * HD_B])
        ha = r("ha", [P, 2, D])
        qk_nat = at("qk_nat", [P, 2, D], offset=stage0 + 4 * 2 * 4 * BLK)
        region2 = r.o
        assert region2 == stage0 + 4 * (2 * 4 * BLK + 2 * D)
        c0 = r("c0", [P, 2 * NH_A, VA])
        region3 = r.o
        mod_nat = at("mod_nat", [P, 3 * D], offset=stage0 + 4 * 2 * 4 * BLK)
        ck_nat = at("ck_nat", [P, 2, HALF], offset=stage0 + 4 * 2 * 4 * BLK)
        ckb_nat = at("ckb_nat", [P, 2, BLK], offset=stage0 + 4 * 2 * 4 * BLK + 4 * D)
        conv_acc_c = at("conv_acc_c", [P, 4, SEQ], offset=stage0 + 4 * 2 * 4 * BLK + 4 * (D + 2 * BLK))
        cen = r("cen", [P, 2, D])
        cv_aug = r("cv_aug", [P, 2, NH_A, VA])
        ck_t = r("ck_t", [P, NH_A, SEQ])
        kw = r("kw", [P, 2, 2, P])
        turn_tmp2 = at("turn_tmp2", [P, 2, SEQ], offset=r.o - 4 * 4 * P)
        rows_c = at("rows_c", [NH_A, 2, 4, SEQ], offset=r.o - 4 * (4 * P + NH_A * SEQ))
        fin_row = at("fin_row", [P, D], offset=region3 + 4 * 2 * D)
        r = Region(region3)
        v_aug = r("v_aug", [P, 2, NH_A, VA])
        q_c, k_c = r("q_c", [P, NH_A, SEQ]), r("k_c", [P, NH_A, SEQ])
        kb_nat = r("kb_nat", [P, 2, NKV_B * HD_B])
        work = r.o
        conv_acc_x = at("conv_acc_x", [P, 4, SEQ], offset=work)
        rows_of = (rows_c, at("rows_x", [NH_A, 2, 4, SEQ], offset=work))
        m_bc, q_in, decay = r("m_bc", [P, 2, SEQ + 1]), r("q_in", [P, 2, SEQ]), r("decay", [P, 2, 2, SEQ])
        assert r.o <= top2, (r.o, top2)
        den = stat[:, 60:64].rearrange("p (a b) -> p a b", a=2)
        r = Region(region2)
        qb_nat, qb_t = r("qb_nat", [P, 2, D]), r("qb_t", [P, NH_B, SEQ])
        sg = at("sg", [P, 2, 2 * D], offset=region2)
        ob = r("ob", [P, 2, D])
        probs2, probs2_t = r("probs2", [P, 2, BLK]), r("probs2_t", [P, 2, BLK])
        rope_tmp = r("rope_tmp", [P, NH_B, 2, 32])
        hn = r("hn", [P, 3, 2 * NH_B])
        row2 = r("row2", [P, 3, 2 * NH_B])
        assert r.o <= top2, (r.o, top2)
        gated_tmp = at("gated_tmp", [P, 2, 2, BLK], offset=region2 + 4 * 6 * D)
        r = Region(stage0)
        gate_row, ln_w_row, ln_b_row = (r(n, [P, D]) for n in ("gate_row", "ln_w_row", "ln_b_row"))
        diag_g, ones_full = r("diag_g", [P, 4, P]), r("ones_full", [P, P])

        b2_consts, ctx_loaded, fin_loaded, mask_loaded, ln_loaded = (
            sem(n) for n in ("b2_consts", "ctx_loaded", "fin_loaded", "mask_loaded", "ln_loaded"))
        mod_sum, mod_turned, mod_done = sem("mod_sum"), sem("mod_turned"), sem("mod_done")
        c_hi, c_lo = sem("c_hi"), sem("c_lo")
        cen_done, fin_sq, fin_ms, fin_root, x1_done = (sem(n) for n in ("cen_done", "fin_sq", "fin_ms", "fin_root", "x1_done"))
        gw_hi, gw_lo = sem("gw_hi"), sem("gw_lo")
        gt_prod, gt_pre, gt_ln, gt_log, gt_rows, gt_exp_in, gt_exp, gt_w, gt_cols, gt_done = (
            sem("gt_" + n) for n in ("prod", "pre", "ln", "log", "rows", "exp_in", "exp", "w", "cols", "done"))
        cv_turned, cv_acc, cv_silu = sem("cv_turned"), sem("cv_acc"), sem("cv_silu")
        ones_set = sem("ones_set")
        ks_turned, ks_scaled, ks_prod, ks_done = (sem("ks_" + n) for n in ("turned", "scaled", "prod", "done"))
        ml_s, ml_m, ml_copy, ml_a, ml_mask, ml_exp, ml_ws, ml_num, ml_out = (
            sem("ml_" + n) for n in ("s", "m", "copy", "a", "mask", "exp", "ws", "num", "out"))
        hn_sq, hn_ms, hn_root, hn_turnable, hn_turned, hn_stored = (
            sem("hn_" + n) for n in ("sq", "ms", "root", "turnable", "turned", "stored"))
        gate_used = sem("gate_used")
        a2_scores, a2_max, a2_probs, a2_turned, a2_out, a2_fetched = (
            sem("a2_" + n) for n in ("scores", "max", "probs", "turned", "out", "fetched"))
        a2_copied = [sem("a2_copied_act"), sem("a2_copied_dve")]
        gr_diag, gr_row, gr_done = sem("gr_diag"), sem("gr_row"), sem("gr_done")
        end_sq, end_ms, end_root, end_done, end_sum = (sem("end_" + n) for n in ("sq", "ms", "root", "done", "sum"))
        hr_sq, hr_ms, hr_root, hr_done = (sem("hr_" + n) for n in ("sq", "ms", "root", "done"))
        M_, A_, S_ = ALU.mult, ALU.add, ALU.subtract

        def mod_act(act):
            act.wait_ge(b2_consts, 16 * N_B2)
            act.activation(c_col[:], c_col[:], ACT.Silu).then_inc(c_hi, 1)
            act.wait_ge(c_hi, 1)
            act.wait_ge(w_used, AT["mod"][0])
            for v in range(2):
                act.activation(act_hi[:, :, 64 * v:64 * v + 64],
                               c_col[:, v, :].unsqueeze(2).broadcast_to([P, KT, 64]), ACT.Copy).then_inc(c_hi, 1)

        def mod_dve(dve):
            dve.wait_ge(c_hi, 3)
            for v in range(2):
                dve.tensor_tensor(act_lo[:, :, 64 * v:64 * v + 64],
                                  c_col[:, v, :].unsqueeze(2).broadcast_to([P, KT, 64]),
                                  act_hi[:, :, 64 * v:64 * v + 64].bitcast(F32), S_).then_inc(c_lo, 1)

        def mod_fetch(act):
            def fetch(m, blk, p):
                act.activation(mod_nat[:, bass.ds(blk * BLK, BLK)], acc[:, m, 0, :], ACT.Copy).then_inc(fetched[m], 1)
            return fetch

        def mod_pe(pe):
            pe.wait_ge(c_lo, 2)
            stream_pe(pe, "mod", (0,))
            for m in range(2):
                pe.wait_ge(fetched[m], AT["ctx_k"][1] + 1)
            for t in range(3 * KT):
                mm = pe.matmul(pst[:, 0, 2 * t:2 * t + 2], mod_nat[:, t * P:(t + 1) * P], ident[:, 0:65:64],
                               start=True, stop=True)
            mm.then_inc(mod_turned, 1)

        def mod_col_dve(dve):
            dve.wait_ge(mod_turned, 1)
            steps.did(dve.tensor_tensor(mod_col[:], pst[:, 0, 0:6 * KT].rearrange("p (t v) -> p t v", v=2),
                                        b_mod_col[:].unsqueeze(2).broadcast_to([P, 3 * KT, 2]), A_))
            steps.settle()
            dve.tensor_scalar(mod_col[:, KT:2 * KT, :], mod_col[:, KT:2 * KT, :], 1.0, None, A_).then_inc(mod_done, 1)

        def centre_dve(dve, dst, src):
            steps.did(dve.tensor_reduce(stat[:, 8:10], src[:], X_AXIS, A_))
            steps.settle()
            steps.did(dve.tensor_scalar(stat[:, 10:12], stat[:, 8:10], 1.0 / D, None, M_))
            steps.settle()
            for h in range(2):
                ins = dve.tensor_scalar(dst[:, h, :], src[:, h, :], stat[:, 10 + h:11 + h], None, S_)
            return ins

        def final_norm_act(act):
            act.wait_ge(fetched[1], AT["mod"][1] + 1)
            for h in range(2):
                ins = act.activation(junk_full[:, h, :], resid[:, h, :], ACT.Square, accum_out=stat[:, 12 + h:13 + h])
            ins.then_inc(fin_sq, 1)
            act.wait_ge(fin_ms, 1)
            act.activation(stat[:, 16:18], stat[:, 14:16], ACT.Sqrt).then_inc(fin_root, 1)

        def final_norm_dve(dve):
            dve.wait_ge(fin_sq, 1)
            dve.tensor_scalar(stat[:, 14:16], stat[:, 12:14], 1.0 / D, EPS, M_, A_).then_inc(fin_ms, 1)
            dve.wait_ge(fin_root, 1)
            steps.did(dve.reciprocal(stat[:, 18:20], stat[:, 16:18]))
            steps.settle()
            dve.wait_ge(fin_loaded, 16)
            for h in range(2):
                ins = dve.scalar_tensor_tensor(out=resid[:, h, :], in0=resid[:, h, :], scalar=stat[:, 18 + h:19 + h],
                                               in1=fin_row[:], op0=M_, op1=M_)
            ins.then_inc(x1_done, 1)
            dve.wait_ge(x1_done, 1)

        def gates_pe_product(pe, n_use):
            pe.wait_ge(gw_lo, 1)
            if n_use:
                pe.wait_ge(hn_stored, 2)
                pe.wait_ge(ks_scaled, NH_A)
            for h in range(2):
                for k in range(KT):
                    xh, xl = act_hi[:, k, h * P:(h + 1) * P], act_lo[:, k, h * P:(h + 1) * P]
                    o = pst[:, 0, h * 32:(h + 1) * 32]
                    pe.matmul(o, xh, gate_w_hi[:, k, :], start=k == 0, stop=False)
                    pe.matmul(o, xh, gate_w_lo[:, k, :], start=False, stop=False)
                    mm = pe.matmul(o, xl, gate_w_hi[:, k, :], start=False, stop=k == KT - 1)
            mm.then_inc(gt_prod, 1)

        def gates_pe_rows(pe, n_use):
            pe.wait_ge(gt_log, n_use + 1)
            for d in range(2):
                for f, src in ((0, gate_pre), (1, gate_log)):
                    for h in range(2):
                        c = 16 * d + 8 * f
                        mm = pe.matmul(pst[0:NH_A, 1 + d, f * SEQ + h * P:f * SEQ + (h + 1) * P],
                                       src[:, h, c:c + NH_A], ident[:], start=True, stop=True)
            mm.then_inc(gt_rows, 1)

        def gates_pe_cols(pe, n_use):
            pe.wait_ge(gt_w, n_use + 1)
            for d in range(2):
                for q, slot in ((0, 3), (1, 1)) if n_use else ((0, 3),):
                    for h in range(2):
                        mm = pe.matmul(pst[:, 3, 32 * q + 16 * h + 8 * d:32 * q + 16 * h + 8 * d + 8],
                                       rows_of[n_use][:, d, slot, h * P:(h + 1) * P], ident[0:NH_A, 0:NH_A],
                                       start=True, stop=True)
            mm.then_inc(gt_cols, 1)

        def gates_act_log(act, n_use):
            act.wait_ge(gt_pre, n_use + 1)
            act.activation(gate_tmp[:], gate_pre[:], ACT.Abs).then_inc(gt_ln, 1)
            act.wait_ge(gt_ln, 3 * n_use + 1)
            act.activation(gate_tmp[:], gate_tmp[:], ACT.Exp, scale=-1.0).then_inc(gt_ln, 1)
            act.wait_ge(gt_ln, 3 * n_use + 2)
            act.activation(gate_tmp[:], gate_tmp[:], ACT.Ln, bias=1.0).then_inc(gt_ln, 1)

        def gates_act_exp(act, n_use):
            act.wait_ge(gt_exp_in, n_use + 1)
            for d in range(2):
                if n_use == 0:
                    ins = act.activation(rows_of[0][:, d, 3, :], rows_of[0][:, d, 1, :], ACT.Exp, bias=row_s[d][:, 1:2])
                else:
                    ins = act.activation(rows_of[1][:, d, 3, :], rows_of[1][:, d, 2, :], ACT.Exp, scale=-1.0)
            ins.then_inc(gt_exp, 1)

        def gates_dve_pre(dve, n_use):
            if n_use == 0:
                dve.memset(ones_row[:], 1.0).then_inc(ones_set, 1)
                dve.wait_ge(ones_set, 1)
            dve.wait_ge(gt_prod, n_use + 1)
            dve.tensor_tensor(gate_pre[:], pst[:, 0, 0:64].rearrange("p (h c) -> p h c", h=2),
                              b_if_row[:].unsqueeze(1).broadcast_to([P, 2, 32]), A_).then_inc(gt_pre, 1)

        def gates_dve_log(dve, n_use):
            dve.wait_ge(gt_ln, 3 * n_use + 3)
            dve.wait_ge(gt_pre, n_use + 1)
            dve.scalar_tensor_tensor(out=gate_log[:], in0=gate_pre[:], scalar=0.0, in1=gate_tmp[:],
                                     op0=ALU.min, op1=S_).then_inc(gt_log, 1)

        def run(x, d):
            return x if d == 0 else x[:, ::-1]

        def gates_dve_scan(dve, n_use):
            rw = rows_of[n_use]
            dve.wait_ge(gt_rows, n_use + 1)
            for d in range(2):
                f_row = pst[0:NH_A, 1 + d, SEQ:2 * SEQ]
                steps.did(dve.tensor_tensor_scan(run(rw[:, d, 0, :], d), run(ones_row[:], d), run(f_row, d), 0.0, M_, A_))
            steps.settle()
            for d in range(2):
                steps.did(dve.tensor_tensor(rw[:, d, 1, :], pst[0:NH_A, 1 + d, 0:SEQ], rw[:, d, 0, :], S_))
            steps.settle()
            if n_use == 0:
                for d in range(2):
                    steps.did(dve.tensor_reduce(row_s[d][:, 0:1], rw[:, d, 1, :], X_AXIS, ALU.max))
                steps.settle()
                for d in range(2):
                    last = 0 if d else SEQ - 1
                    steps.did(dve.tensor_tensor(row_s[d][:, 2:3], row_s[d][:, 0:1], rw[:, d, 0, last:last + 1], A_))
                    ins = dve.tensor_scalar(row_s[d][:, 1:2], row_s[d][:, 0:1], -1.0, None, M_)
                ins.then_inc(gt_exp_in, 1)
                dve.wait_ge(gt_exp, 1)
                for d in range(2):
                    ins = dve.tensor_scalar(rw[:, d, 3, :], rw[:, d, 3, :], DK_A ** -0.5, None, M_)
                ins.then_inc(gt_w, 1)
            else:
                for d in range(2):
                    steps.did(dve.tensor_copy(m_rows[d][:, SEQ:SEQ + 1], row_s[d][:, 2:3]))
                    steps.did(dve.tensor_tensor_scan(run(m_rows[d][:, 0:SEQ], d), run(ones_row[:], d),
                                                     run(rw[:, d, 1, :], d), row_s[d][:, 2:3], M_, ALU.max))
                steps.settle()
                for d in range(2):
                    ins = dve.tensor_tensor(rw[:, d, 2, :], rw[:, d, 0, :], m_rows[d][:, 0:SEQ], A_)
                ins.then_inc(gt_exp_in, 1)
                dve.wait_ge(gt_exp, 2)
                dve.sem_inc(gt_w, 1)

        def gates_dve_cols(dve, n_use):
            dve.wait_ge(gt_cols, n_use + 1)
            if n_use == 0:
                dve.tensor_copy(w_col[:].rearrange("p h d n -> p (h d n)"), pst[:, 3, 0:32]).then_inc(gt_done, 1)
            else:
                dve.tensor_copy(e_col[:].rearrange("p h d n -> p (h d n)"), pst[:, 3, 0:32])
                dve.tensor_copy(g_col[:].rearrange("p h d n -> p (h d n)"), pst[:, 3, 32:64]).then_inc(gt_done, 1)

        def conv_pe(pe, src, g0, n, first):
            for g in range(n):
                if g0 + g >= 1 and not (g == 0 and first):
                    pe.wait_ge(cv_acc, g0 + g)
                for t in range(4):
                    for h in range(2):
                        c = (4 * g + t) * P
                        mm = pe.transpose(pst[:, t, h * P:(h + 1) * P], src[:, h, c:c + P], ident[:])
                mm.then_inc(cv_turned, 1)

        def conv_dve(dve, conv_acc, w0, g0, n):
            for g in range(n):
                dve.wait_ge(cv_turned, g0 + g + 1)
                if g0 + g >= 1:
                    dve.wait_ge(cv_silu, g0 + g)
                for tap in range(3):
                    for t in range(4):
                        k = w0 + 4 * g + t
                        ps, w = pst[:, t, 0:SEQ], conv_w[:, k, :]
                        if tap == 0:
                            ins = dve.tensor_scalar(conv_acc[:, t, :], ps, w[:, 1:2], conv_b[:, k:k + 1], M_, A_)
                        elif tap == 1:
                            o = conv_acc[:, t, 1:SEQ]
                            ins = dve.scalar_tensor_tensor(out=o, in0=ps[:, 0:SEQ - 1], scalar=w[:, 0:1], in1=o, op0=M_, op1=A_)
                        else:
                            o = conv_acc[:, t, 0:SEQ - 1]
                            ins = dve.scalar_tensor_tensor(out=o, in0=ps[:, 1:SEQ], scalar=w[:, 2:3], in1=o, op0=M_, op1=A_)
                    if tap < 2:
                        steps.did(ins)
                        steps.settle()
                ins.then_inc(cv_acc, 1)

        def conv_act(act, conv_acc, dsts, g0):
            for g, dst in enumerate(dsts):
                act.wait_ge(cv_acc, g0 + g + 1)
                act.activation(dst, conv_acc[:], ACT.Silu).then_inc(cv_silu, 1)

        def state_pe(pe):
            pe.wait_ge(cv_silu, 2)
            pe.wait_ge(gt_done, 1)
            for s in range(NH_A + 1):
                if s < NH_A:
                    if s >= 2:
                        pe.wait_ge(ks_scaled, s - 1)
                    for h in range(2):
                        mm = pe.transpose(pst[:, s % 2, h * P:(h + 1) * P], ck_t[:, s, h * P:(h + 1) * P], ident[:])
                    mm.then_inc(ks_turned, 1)
                if s >= 1:
                    n = s - 1
                    pe.wait_ge(ks_scaled, n + 1)
                    if n >= 1:
                        pe.wait_ge(ks_done, n)
                    for d in range(2):
                        for h in range(2):
                            mm = pe.matmul(acc[:, 0, d, 0:VA], kw[:, d, h, :], cv_aug[:, h, n, :],
                                           start=h == 0, stop=h == 1)
                    mm.then_inc(ks_prod, 1)

        def state_act(act):
            act.wait_ge(gt_done, 1)
            for s in range(NH_A):
                act.wait_ge(ks_turned, s + 1)
                if s >= 1:
                    act.wait_ge(ks_prod, s)
                for d in range(2):
                    for h in range(2):
                        ins = act.activation(kw[:, d, h, :], pst[:, s % 2, h * P:(h + 1) * P], ACT.Copy,
                                             scale=w_col[:, h, d, s:s + 1])
                ins.then_inc(ks_scaled, 1)

        def state_dve(dve):
            for s in range(NH_A):
                dve.wait_ge(ks_prod, s + 1)
                dve.tensor_copy(c0[:, 2 * s:2 * s + 2, :], acc[:, 0, :, 0:VA]).then_inc(ks_done, 1)

        NU = 2 * NH_A

        def mlstm_pe(pe):
            pe.wait_ge(gt_done, 2)
            for m in range(2):
                pe.wait_ge(fetched[m], AT["x_o"][1] + 1)
            pe.wait_ge(cv_silu, 6)
            for s in range(NU + 2):
                if s < NU:
                    head, d = s // 2, s % 2
                    if d == 0:
                        if head >= 2:
                            pe.wait_ge(ml_ws, 2 * (head - 1))
                        for st in range(2):
                            mm = pe.matmul(pst[:, head % 2, st * SEQ:(st + 1) * SEQ],
                                           k_c[:, head, st * P:(st + 1) * P], q_c[:, head, :], start=True, stop=True)
                        mm.then_inc(ml_s, 1)
                    if s >= 2:
                        pe.wait_ge(ml_copy, s - 1)
                    pe.matmul(pst[:, 2 + s % 2, 0:SEQ + 1], ident[0:NH_A, head:head + 1].broadcast_to([NH_A, P]),
                              m_rows[d][:], start=True, stop=True).then_inc(ml_m, 1)
                if s >= 2:
                    n = s - 2
                    head, d = n // 2, n % 2
                    pe.wait_ge(ml_ws, n + 1)
                    if n >= 2:
                        pe.wait_ge(ml_out, n - 1)
                    for th in range(2):
                        o = acc[:, n % 2, th, 0:VA]
                        for j, st in enumerate([0, 1] if th != d else [th]):
                            pe.matmul(o, decay[:, n % 2, st, th * P:(th + 1) * P], v_aug[:, st, head, :],
                                      start=j == 0, stop=False)
                        mm = pe.matmul(o, q_in[:, n % 2, th * P:(th + 1) * P], c0[:, n, :], start=False, stop=True)
                    mm.then_inc(ml_num, 1)

        def mlstm_act(act):
            for s in range(NU + 1):
                if s < NU:
                    act.wait_ge(ml_m, s + 1)
                    if s >= 2:
                        act.wait_ge(ml_mask, s - 1)
                        act.wait_ge(ml_a, s - 1)
                    act.activation(m_bc[:, s % 2, :], pst[:, 2 + s % 2, 0:SEQ + 1], ACT.Copy).then_inc(ml_copy, 1)
                    act.wait_ge(ml_copy, s + 1)
                    if s >= 2:
                        act.wait_ge(ml_num, s - 1)
                    act.activation(q_in[:, s % 2, :], m_bc[:, s % 2, 0:SEQ], ACT.Exp, scale=-1.0,
                                   bias=m_bc[:, s % 2, SEQ:SEQ + 1]).then_inc(ml_a, 1)
                if s >= 1:
                    n = s - 1
                    act.wait_ge(ml_mask, n + 1)
                    for st in range(2):
                        o = decay[:, n % 2, st, :]
                        ins = act.activation(o, o, ACT.Exp, bias=g_col[:, st, n % 2, n // 2:n // 2 + 1])
                    ins.then_inc(ml_exp, 1)

        def mlstm_dve(dve):
            dve.wait_ge(mask_loaded, 16)
            for s in range(NU + 3):
                if s < NU:
                    dve.wait_ge(ml_copy, s + 1)
                    if s >= 2:
                        dve.wait_ge(ml_num, s - 1)
                    dve.tensor_tensor(decay[:, s % 2, :, :], neg_mask[:, s % 2, :, :],
                                      m_bc[:, s % 2, 0:SEQ].unsqueeze(1).broadcast_to([P, 2, SEQ]), S_).then_inc(ml_mask, 1)
                if 1 <= s <= NU:
                    n = s - 1
                    dve.wait_ge(ml_a, n + 1)
                    dve.wait_ge(ml_s, n // 2 + 1)
                    dve.tensor_tensor(q_in[:, n % 2, :], q_in[:, n % 2, :], q_c[:, n // 2, :], M_)
                    dve.wait_ge(ml_exp, n + 1)
                    o = decay[:, n % 2, :, :]
                    dve.scalar_tensor_tensor(out=o, in0=pst[:, (n // 2) % 2, :].rearrange("p (a t) -> p a t", a=2),
                                             scalar=DK_A ** -0.5, in1=o, op0=M_, op1=M_).then_inc(ml_ws, 1)
                if s >= 3:
                    n = s - 3
                    head, d = n // 2, n % 2
                    dve.wait_ge(ml_num, n + 1)
                    if n >= 1:
                        dve.wait_ge(ml_out, n)
                    total = acc[:, n % 2, :, VA - 1]
                    steps.did(dve.scalar_tensor_tensor(out=den[:, 0, :], in0=total, scalar=-1.0,
                                                       in1=e_col[:, :, d, head], op0=M_, op1=ALU.max))
                    steps.settle()
                    steps.did(dve.tensor_tensor(den[:, 0, :], total, den[:, 0, :], ALU.max))
                    steps.settle()
                    steps.did(dve.reciprocal(den[:, 1, :], den[:, 0, :]))
                    steps.settle()
                    for th in range(2):
                        o = ha[:, th, head * DV_A:(head + 1) * DV_A]
                        x = acc[:, n % 2, th, 0:DV_A]
                        if d == 0:
                            ins = dve.tensor_scalar(o, x, den[:, 1, th:th + 1], None, M_)
                        else:
                            ins = dve.scalar_tensor_tensor(out=o, in0=x, scalar=den[:, 1, th:th + 1], in1=o, op0=M_, op1=A_)
                    ins.then_inc(ml_out, 1)

        def head_norm_act(act):
            act.wait_ge(ml_out, NU)
            for h in range(2):
                for n in range(NH_A):
                    ins = act.activation(v_aug[:, h, n, 0:DV_A], ha[:, h, n * DV_A:(n + 1) * DV_A], ACT.Square,
                                         accum_out=stat[:, 20 + 8 * h + n:21 + 8 * h + n])
            ins.then_inc(hr_sq, 1)
            act.wait_ge(hr_ms, 1)
            act.activation(stat[:, 36:52], stat[:, 36:52], ACT.Sqrt).then_inc(hr_root, 1)

        def head_norm_dve(dve):
            dve.wait_ge(hr_sq, 1)
            dve.tensor_scalar(stat[:, 36:52], stat[:, 20:36], 1.0 / DV_A, EPS, M_, A_).then_inc(hr_ms, 1)
            dve.wait_ge(hr_root, 1)
            steps.did(dve.reciprocal(stat[:, 36:52], stat[:, 36:52]))
            steps.settle()
            x = ha[:].rearrange("p h (n v) -> p (h n) v", v=DV_A)
            dve.tensor_tensor(x, x, stat[:, 36:52].unsqueeze(2).broadcast_to([P, 16, DV_A]), M_).then_inc(hr_done, 1)
            dve.wait_ge(hr_done, 1)

        def gated_act(act, func, base):
            def fetch(m, blk, p):
                act.wait_ge(gate_used, blk + (base + 1))
                act.activation(gated_tmp[:, m, :, :], acc[:, m, :, :], func).then_inc(fetched[m], 1)
            return fetch

        def gated_dve(dve, dst):
            def fetch(m, blk, p):
                dve.wait_ge(fetched[m], p + 2)
                o = dst[:, :, bass.ds(blk * BLK, BLK)]
                dve.tensor_tensor(o, o, gated_tmp[:, m, :, :], M_).then_inc(gate_used, 1)
            return fetch

        def qk_norm(use):
            src, gain, n = ((ckb_nat, k_gain, NKV_B), (kb_nat, k_gain, NKV_B), (qb_nat, q_gain, NH_B))[use]
            return src, gain, n, ob if use else ckb_nat

        def qk_norm_act(act, use):
            n = qk_norm(use)[2]
            act.wait_ge(hn_ms, use + 1)
            act.activation(hn[:, 1, 0:2 * n], hn[:, 0, 0:2 * n], ACT.Sqrt).then_inc(hn_root, 1)

        def qk_norm_dve(dve, use):
            src, gain, n, dst = qk_norm(use)
            for m in range(2):
                dve.wait_ge(fetched[m], AT[("x_qk", "x_o", "x_zb")[use]][1] + 1)
            x = src[:].rearrange("p h (n e) -> p (h n) e", e=HD_B)
            y = ob[:, :, 0:n * HD_B] if use else ck_nat[:, :, 0:n * HD_B]
            if n == NH_B:
                for h in range(2):
                    steps.did(dve.tensor_tensor(ob[:, h, :], src[:, h, :], src[:, h, :], M_))
            else:
                steps.did(dve.tensor_tensor(y, src[:], src[:], M_))
            steps.settle()
            for h in range(2):
                steps.did(dve.tensor_reduce(hn[:, 0, h * n:(h + 1) * n], y[:, h, :].rearrange("p (n e) -> p n e", e=HD_B),
                                            X_AXIS, A_))
            steps.settle()
            dve.tensor_scalar(hn[:, 0, 0:2 * n], hn[:, 0, 0:2 * n], 1.0 / HD_B, EPS, M_, A_).then_inc(hn_ms, 1)
            dve.wait_ge(hn_root, use + 1)
            steps.did(dve.reciprocal(hn[:, 2, 0:2 * n], hn[:, 1, 0:2 * n]))
            steps.settle()
            steps.did(dve.tensor_tensor(x, x, hn[:, 2, 0:2 * n].unsqueeze(2).broadcast_to([P, 2 * n, HD_B]), M_))
            steps.settle()
            last = dve.tensor_tensor(x, x, gain[:].unsqueeze(1).broadcast_to([P, 2 * n, HD_B]), M_)
            if use:
                steps.did(last)
                steps.settle()
                for h in range(2):
                    xv = src[:, h, :].rearrange("p (n r s e) -> p n r s e", r=2, s=2, e=32)
                    yv = ob[:, h, 0:n * HD_B].rearrange("p (n r s e) -> p n r s e", r=2, s=2, e=32)
                    x1, x2, y1, y2 = xv[:, :, :, 0, :], xv[:, :, :, 1, :], yv[:, :, :, 0, :], yv[:, :, :, 1, :]
                    shape = [P, n, 2, 32]
                    co = rope[:, 0, h, :, :].unsqueeze(1).broadcast_to(shape)
                    si = rope[:, 1, h, :, :].unsqueeze(1).broadcast_to(shape)
                    t = rope_tmp[:, 0:n, :, :]
                    dve.tensor_tensor(y1, x1, co, M_)
                    dve.tensor_tensor(y2, x1, si, M_)
                    steps.did(dve.tensor_tensor(t, x2, si, M_))
                    steps.settle()
                    steps.did(dve.tensor_tensor(y1, y1, t, S_))
                    steps.settle()
                    steps.did(dve.tensor_tensor(t, x2, co, M_))
                    steps.settle()
                    last = dve.tensor_tensor(y2, y2, t, A_)
                    if h == 0:
                        steps.did(last)
                        steps.settle()
            last.then_inc(hn_turnable, 1)

        TURN_BANKS = (0, 2, 4, 12)

        def qk_turn_pe(pe, use):
            n, dst = qk_norm(use)[2:]
            pe.wait_ge(hn_turnable, use + 1)
            for b in range(n // 2):
                done = TURN_BANKS[use] + b
                if done >= 2:
                    pe.wait_ge(hn_stored, done - 1)
                for t in range(2):
                    for h in range(2):
                        mm = pe.transpose(pst[:, done % 2, t * SEQ + h * P:t * SEQ + (h + 1) * P],
                                          dst[:, h, (2 * b + t) * HD_B:(2 * b + t + 1) * HD_B], ident[:])
                mm.then_inc(hn_turned, 1)

        def qk_store_act(act, use):
            n = qk_norm(use)[2]
            for b in range(n // 2):
                done = TURN_BANKS[use] + b
                act.wait_ge(hn_turned, done + 1)
                x = pst[:, done % 2, :].rearrange("p (t s) -> p t s", t=2)
                o = qb_t[:, 2 * b:2 * b + 2, :] if use == 2 else keys_t[:, 2 * b:2 * b + 2, use * SEQ:(use + 1) * SEQ]
                act.activation(o, x, ACT.Copy).then_inc(hn_stored, 1)

        NQ = 2 * NH_B
        SCALE_B = HD_B ** -0.5

        def attention2_pe(pe):
            pe.wait_ge(hn_stored, TURN_BANKS[3])
            for m in range(2):
                pe.wait_ge(fetched[m], AT["x_zb"][1] + 1)
            for s in range(NQ + 2):
                if s < NQ:
                    if s >= 2:
                        pe.wait_ge(a2_probs, s - 1)
                    head, h = s // 2, s % 2
                    pe.matmul(pst[:, s % 2, :], qb_t[:, head, h * P:(h + 1) * P], keys_t[:, head // 4, :],
                              start=True, stop=True).then_inc(a2_scores, 1)
                if 1 <= s <= NQ:
                    u = s - 1
                    pe.wait_ge(a2_probs, u + 1)
                    if u >= 2:
                        pe.wait_ge(a2_copied[u % 2], u // 2)
                    for b in range(4):
                        mm = pe.transpose(pst[:, 2 + u % 2, b * P:(b + 1) * P], probs2[:, u % 2, b * P:(b + 1) * P], ident[:])
                    mm.then_inc(a2_turned, 1)
                if s >= 2:
                    u = s - 2
                    head = u // 2
                    pe.wait_ge(a2_copied[u % 2], u // 2 + 1)
                    if u >= 2:
                        pe.wait_ge(a2_fetched, u - 1)
                    kv = head // 4
                    for b in range(4):
                        mm = pe.matmul(acc[:, 0, u % 2, 0:HD_B], probs2_t[:, u % 2, b * P:(b + 1) * P],
                                       vals[:, b, kv * HD_B:(kv + 1) * HD_B], start=b == 0, stop=b == 3)
                    mm.then_inc(a2_out, 1)

        def attention2_copy(eng, par, u, copy):
            eng.wait_ge(a2_turned, u + 1)
            if u >= 2:
                eng.wait_ge(a2_out, u - 1)
            copy(probs2_t[:, par, :], pst[:, 2 + par, :]).then_inc(a2_copied[par], 1)

        def attention2_act(act):
            for s in range(NQ + 1):
                if s < NQ:
                    act.wait_ge(a2_max, s + 1)
                    if s >= 2:
                        act.wait_ge(a2_turned, s - 1)
                    act.activation(probs2[:, s % 2, :], pst[:, s % 2, :], ACT.Exp, scale=SCALE_B,
                                   bias=row2[:, 0, s:s + 1], accum_out=row2[:, 1, s:s + 1]).then_inc(a2_probs, 1)
                if s >= 1 and (s - 1) % 2 == 0:
                    attention2_copy(act, 0, s - 1, lambda o, i: act.activation(o, i, ACT.Copy))

        def attention2_dve(dve):
            for s in range(NQ + 2):
                if s < NQ:
                    dve.wait_ge(a2_scores, s + 1)
                    steps.did(dve.tensor_reduce(row2[:, 2, s:s + 1], pst[:, s % 2, :], X_AXIS, ALU.max))
                    steps.settle()
                    dve.tensor_scalar(row2[:, 0, s:s + 1], row2[:, 2, s:s + 1], -SCALE_B, None, M_).then_inc(a2_max, 1)
                if s >= 1 and s <= NQ and (s - 1) % 2 == 1:
                    attention2_copy(dve, 1, s - 1, dve.tensor_copy)
                if s >= 2:
                    u = s - 2
                    head, h = u // 2, u % 2
                    dve.wait_ge(a2_out, u + 1)
                    dve.wait_ge(a2_max, u + 1)
                    steps.did(dve.reciprocal(row2[:, 2, u:u + 1], row2[:, 1, u:u + 1]))
                    steps.settle()
                    dve.tensor_scalar(ob[:, h, head * HD_B:(head + 1) * HD_B], acc[:, 0, u % 2, 0:HD_B],
                                      row2[:, 2, u:u + 1], None, M_).then_inc(a2_fetched, 1)

        def sg_fetch(act):
            def fetch(m, blk, p):
                act.activation(sg[:, :, bass.ds(blk * BLK, BLK)], acc[:, m, :, :], ACT.Sigmoid).then_inc(fetched[m], 1)
            return fetch

        def ba_fetch(dve):
            def fetch(m, blk, p):
                o = sg[:, :, bass.ds(blk * BLK, BLK)]
                dve.tensor_tensor(o, o, acc[:, m, :, :], M_).then_inc(fetched[m], 1)
            return fetch

        bb_prod = sem("bb_prod")

        def bb_fetch(dve):
            def fetch(m, blk, p):
                o, g = sg[:, :, bass.ds(blk * BLK, BLK)], sg[:, :, bass.ds(blk * BLK + D, BLK)]
                dve.tensor_tensor(g, g, acc[:, m, :, :], M_).then_inc(bb_prod, 1)
                dve.wait_ge(bb_prod, blk + 1)
                dve.tensor_tensor(o, o, g, A_).then_inc(fetched[m], 1)
            return fetch

        def gate_row_dve(dve):
            dve.wait_ge(nt_turned, turns["ob"][0] + 16)
            dve.memset(ones_full[:], 1.0)
            for g in range(4):
                if g:
                    dve.wait_ge(gr_row, g)
                for t in range(4):
                    ins = dve.tensor_scalar(diag_g[:, t, :], ident[:], mod_col[:, 2 * KT + 4 * g + t, 0:1], None, M_)
                ins.then_inc(gr_diag, 1)
                dve.wait_ge(gr_row, g + 1)
                ins = dve.tensor_copy(gate_row[:, g * BLK:(g + 1) * BLK], pst[:, g % 2, :])
                ins.then_inc(gr_done, 1)

        def gate_row_pe(pe):
            for g in range(4):
                pe.wait_ge(gr_diag, g + 1)
                if g >= 2:
                    pe.wait_ge(gr_done, g - 1)
                for t in range(4):
                    mm = pe.matmul(pst[:, g % 2, t * P:(t + 1) * P], ones_full[:], diag_g[:, t, :], start=True, stop=True)
                mm.then_inc(gr_row, 1)


        wo_prod = sem("wo_prod")

        def wo_fetch(dve):
            def fetch(m, blk, p):
                t = sg[:, :, bass.ds(blk * BLK + D, BLK)]
                o = resid[:, :, bass.ds(blk * BLK, BLK)]
                g = gate_row[:, bass.ds(blk * BLK, BLK)].unsqueeze(1).broadcast_to([P, 2, BLK])
                dve.tensor_tensor(t, acc[:, m, :, :], g, M_).then_inc(wo_prod, 1)
                dve.wait_ge(wo_prod, blk + 1)
                dve.scalar_tensor_tensor(out=o, in0=o, scalar=ALPHA, in1=t, op0=M_, op1=A_).then_inc(fetched[m], 1)
            return fetch

        def end_act(act):
            act.wait_ge(end_sum, 1)
            for h in range(2):
                ins = act.activation(junk_full[:, h, :], resid[:, h, :], ACT.Square, accum_out=stat[:, 52 + h:53 + h])
            ins.then_inc(end_sq, 1)
            act.wait_ge(end_ms, 1)
            act.activation(stat[:, 56:58], stat[:, 54:56], ACT.Sqrt).then_inc(end_root, 1)

        def end_dve(dve):
            for m in range(2):
                dve.wait_ge(fetched[m], AT["end"][1] + 1)
            centre_dve(dve, resid, resid).then_inc(end_sum, 1)
            dve.wait_ge(end_sq, 1)
            dve.tensor_scalar(stat[:, 54:56], stat[:, 52:54], 1.0 / D, EPS, M_, A_).then_inc(end_ms, 1)
            dve.wait_ge(end_root, 1)
            steps.did(dve.reciprocal(stat[:, 58:60], stat[:, 56:58]))
            steps.settle()
            dve.wait_ge(ln_loaded, 32)
            for h in range(2):
                steps.did(dve.scalar_tensor_tensor(out=resid[:, h, :], in0=resid[:, h, :], scalar=stat[:, 58 + h:59 + h],
                                                   in1=ln_w_row[:], op0=M_, op1=M_))
                steps.settle()
                dve.tensor_tensor(resid[:, h, :], resid[:, h, :], ln_b_row[:], A_).then_inc(end_done, 1)

        B2_LOADS = ((gate_w[:], "gate_w"), (c_col[:], "c_col"), (b_mod_col[:], "b_mod_col"), (conv_w[:], "conv_w"),
                    (conv_b[:], "conv_b"), (mh_col[:], "mh_col"), (rope[:], "rope"))
        B2_ROWS = ((b_if_row[:], "b_if_2"), (q_gain[:], "q_norm_w_2"), (k_gain[:], "k_norm_w_2"))
        N_B2 = len(B2_LOADS) + len(B2_ROWS)

        block = ctx.enter_context(nc.Block())

        @block.sync
        def _(sp):
            sp.dma_start(resid[:], A["x"].rearrange("(h p) d -> p h d", p=P)).then_inc(x_ready, 16)
            sp.dma_start(ident[:], A["ident"]).then_inc(consts_ready, 16)
            sp.dma_start(gains[:].rearrange("p a k -> p (a k)"), A["gains"]).then_inc(consts_ready, 16)
            ffn_sp(sp, "ffn1", A["ffn1_w_gate"], A["ffn1_w_up"], A["ffn1_w_down"])
            stream_sp(sp, "w_in", A["w_in"], 0)
            stream_sp(sp, "glu", A["ssm_w_glu"], 0)
            stream_sp(sp, "w_out", A["w_out"], 0)
            ffn_sp(sp, "ffn2", A["ffn2_w_gate"], A["ffn2_w_up"], A["ffn2_w_down"])
            win2 = A["w_in_2"]
            stream_sp(sp, "mod", A["w_mod_2"], 0)
            for name, col in (("ctx_k", DK_A * NH_A), ("ctx_v", 2 * DK_A * NH_A), ("ctx_kv", KB0), ("x_qk", 0),
                              ("x_v", 2 * DK_A * NH_A), ("x_kv", KB0)) + tuple(
                    (n, KB0 + BLK * b) for n, b in (("x_o", 2), ("x_z", 6), ("x_q", 10), ("x_zb", 14), ("x_g", 18))):
                stream_sp(sp, name, win2, col)
            stream_sp(sp, "ba", A["w_branch_a_2"], 0)
            stream_sp(sp, "bb", A["w_branch_b_2"], 0)
            stream_sp(sp, "wo", A["w_out_2"], 0)
            for h in range(2):
                sp.wait_ge(end_done, h + 1)
                sp.dma_start(out.rearrange("(h p) d -> p h d", p=P)[:, h, :], resid[:, h, :]).then_inc(out_done, 16)
            sp.wait_ge(out_done, 32)

        @block.scalar
        def _(act):
            for j in range(LEAD):
                round_chunk(act, j)
            act.wait_ge(x_ready, 16)
            act.wait_ge(consts_ready, 32)
            turn_act(act, "ffn1", resid, gains[:, 0, :], junk=junk_full)
            ffn_act(act, "ffn1", 0)
            act.wait_ge(fetched[1], AT["w_in"][1] + 1)
            turn_act(act, "mix", resid, gains[:, 1, :], junk=junk_full)
            fp = fetch_prj(act)
            stream_split(act, "w_in", lambda m, blk, p: fp(m, blk, p, 0))
            turn_qku_fetch(act, 0, lambda o, i: act.activation(o, i, ACT.Copy))
            attention1_act(act)
            ssm_params_act(act)
            ssm_act(act)
            turn_act(act, "y", ssm_y)
            stream_split(act, "glu")
            glu_act(act)
            act.wait_ge(glu_out, 2)
            turn_act(act, "ssm", ssm_y, gains[:, 2, 0:8], junk=junk_low)
            turn_act(act, "att", att, gains[:, 2, 8:16], junk=junk_high, dst=8)
            stream_split(act, "w_out")
            act.wait_ge(fetched[1], AT["ffn2"][1] + 1)
            turn_act(act, "ffn2", resid, gains[:, 3, :], junk=junk_full)
            ffn_act(act, "ffn2", 1)
            final_norm_act(act)
            mod_act(act)
            act.activation(gate_w_hi[:], gate_w[:], ACT.Copy).then_inc(gw_hi, 1)
            stream_split(act, "mod", mod_fetch(act))
            act.wait_ge(cen_done, 1)
            act.wait_ge(mod_done, 1)
            turn_act(act, "u_ctx", cen, mod_col[:, KT:2 * KT, 1], junk=junk_full, bias=mod_col[:, 0:KT, 1])

            def store(place):
                def fetch(m, blk, p):
                    act.activation(place(blk), acc[:, m, :, :], ACT.Copy).then_inc(fetched[m], 1)
                return fetch

            def store_values(dst):
                def fetch(m, blk, p):
                    act.activation(dst[:, :, bass.ds(blk * 2, 2), 0:DV_A],
                                   acc[:, m, :, :].rearrange("p h (n v) -> p h n v", v=DV_A), ACT.Copy).then_inc(fetched[m], 1)
                return fetch
            stream_split(act, "ctx_k", store(lambda blk: ck_nat[:, :, bass.ds(blk * BLK, BLK)]))
            gates_act_log(act, 0)
            stream_split(act, "ctx_v", store_values(cv_aug))
            gates_act_exp(act, 0)
            stream_split(act, "ctx_kv", store(lambda blk: vals[:, 0:2, :] if blk else ckb_nat[:]))
            conv_act(act, conv_acc_c, (ck_t[:, 0:4, :], ck_t[:, 4:8, :]), 0)
            state_act(act)
            qk_norm_act(act, 0)
            qk_store_act(act, 0)
            turn_act(act, "u_x", cen, mod_col[:, KT:2 * KT, 0], junk=junk_full, bias=mod_col[:, 0:KT, 0])
            stream_split(act, "x_qk", store(lambda blk: qk_nat[:, :, bass.ds(blk * BLK, BLK)]))
            gates_act_log(act, 1)
            stream_split(act, "x_v", store_values(v_aug))
            gates_act_exp(act, 1)
            stream_split(act, "x_kv", store(lambda blk: vals[:, 2:4, :] if blk else kb_nat[:]))
            conv_act(act, conv_acc_x, (q_c[:, 0:4, :], q_c[:, 4:8, :], k_c[:, 0:4, :], k_c[:, 4:8, :]), 2)
            mlstm_act(act)
            head_norm_act(act)
            qk_norm_act(act, 1)
            qk_store_act(act, 1)
            stream_split(act, "x_o", gated_act(act, ACT.Sigmoid, 0))
            stream_split(act, "x_z", gated_act(act, ACT.Silu, 4))
            stream_split(act, "x_q", store(lambda blk: qb_nat[:, :, bass.ds(blk * BLK, BLK)]))
            qk_norm_act(act, 2)
            qk_store_act(act, 2)
            attention2_act(act)
            stream_split(act, "x_zb", gated_act(act, ACT.Silu, 8))
            stream_split(act, "x_g", sg_fetch(act))
            turn_act(act, "ha", ha, mh_col)
            stream_split(act, "ba")
            turn_act(act, "ob", ob)
            stream_split(act, "bb")
            turn_act(act, "merge", sg)
            stream_split(act, "wo")
            end_act(act)

        @block.vector
        def _(dve):
            nonlocal steps
            steps = Steps(dve, dve_steps)
            dve.sem_inc(fetched[0], 1)
            dve.sem_inc(fetched[1], 1)
            dve.sem_inc(g_lo_done, 1)
            dve.sem_inc(gate_used, 2)
            for j in range(LEAD):
                rest_chunk(dve, j)
            dve.wait_ge(consts_ready, 32)
            turn_dve(dve, "ffn1", gains[:, 0, :])
            ffn_dve(dve, "ffn1", 0)
            turn_dve(dve, "mix", gains[:, 1, :])
            stream_split(dve, "w_in")
            turn_qku_fetch(dve, 1, dve.tensor_copy)
            attention1_dve(dve)
            ssm_params_dve(dve)
            ssm_dve(dve)
            turn_dve(dve, "y")
            stream_split(dve, "glu", glu_fetch_dve(dve))
            glu_dve(dve)
            turn_dve(dve, "ssm", gains[:, 2, 0:8], width=HALF)
            turn_dve(dve, "att", gains[:, 2, 8:16], width=HALF, dst=8)
            stream_split(dve, "w_out", fetch_residual(dve))
            turn_dve(dve, "ffn2", gains[:, 3, :])
            ffn_dve(dve, "ffn2", 1)
            final_norm_dve(dve)
            mod_dve(dve)
            dve.wait_ge(gw_hi, 1)
            dve.tensor_tensor(gate_w_lo[:], gate_w[:], gate_w_hi[:].bitcast(F32), ALU.subtract).then_inc(gw_lo, 1)
            stream_split(dve, "mod")
            mod_col_dve(dve)
            dve.wait_ge(ctx_loaded, 16)
            centre_dve(dve, cen, cen).then_inc(cen_done, 1)
            turn_dve(dve, "u_ctx", mod_col[:, KT:2 * KT, 1], bias=mod_col[:, 0:KT, 1], tmp=turn_tmp2)
            centre_dve(dve, cen, resid).then_inc(cen_done, 1)
            dve.memset(cv_aug[:, :, :, DV_A:VA], 1.0)
            gates_dve_pre(dve, 0)
            stream_split(dve, "ctx_k")
            gates_dve_log(dve, 0)
            stream_split(dve, "ctx_v")
            gates_dve_scan(dve, 0)
            stream_split(dve, "ctx_kv")
            gates_dve_cols(dve, 0)
            conv_dve(dve, conv_acc_c, NH_A, 0, 2)
            state_dve(dve)
            qk_norm_dve(dve, 0)
            turn_dve(dve, "u_x", mod_col[:, KT:2 * KT, 0], bias=mod_col[:, 0:KT, 0], tmp=turn_tmp2)
            dve.memset(v_aug[:, :, :, DV_A:VA], 1.0)
            gates_dve_pre(dve, 1)
            stream_split(dve, "x_qk")
            gates_dve_log(dve, 1)
            stream_split(dve, "x_v")
            gates_dve_scan(dve, 1)
            stream_split(dve, "x_kv")
            gates_dve_cols(dve, 1)
            conv_dve(dve, conv_acc_x, 0, 2, 4)
            mlstm_dve(dve)
            head_norm_dve(dve)
            qk_norm_dve(dve, 1)
            stream_split(dve, "x_o", gated_dve(dve, ha))
            stream_split(dve, "x_z", gated_dve(dve, ha))
            stream_split(dve, "x_q")
            qk_norm_dve(dve, 2)
            attention2_dve(dve)
            stream_split(dve, "x_zb", gated_dve(dve, ob))
            stream_split(dve, "x_g")
            turn_dve(dve, "ha", mh_col)
            stream_split(dve, "ba", ba_fetch(dve))
            turn_dve(dve, "ob")
            gate_row_dve(dve)
            stream_split(dve, "bb", bb_fetch(dve))
            turn_dve(dve, "merge")
            stream_split(dve, "wo", wo_fetch(dve))
            end_dve(dve)

        @block.tensor
        def _(pe):
            pe.wait_ge(x_ready, 16)
            turn_pe(pe, "ffn1", resid)
            turned(pe, "ffn1")
            ffn_pe(pe, "ffn1", 0)
            turn_pe(pe, "mix", resid)
            turned(pe, "mix")
            stream_pe(pe, "w_in")
            turn_qku_pe(pe)
            attention1_pe(pe)
            ssm_pe(pe)
            pe.wait_ge(ssm_gelu, 2)
            turn_pe(pe, "y", ssm_y)
            turned(pe, "y")
            stream_pe(pe, "glu")
            turn_pe(pe, "ssm", ssm_y)
            turn_pe(pe, "att", att)
            turned(pe, "att")
            stream_pe(pe, "w_out")
            turn_pe(pe, "ffn2", resid)
            turned(pe, "ffn2")
            ffn_pe(pe, "ffn2", 1)
            mod_pe(pe)
            turn_pe(pe, "u_ctx", cen)
            turned(pe, "u_ctx")
            gates_pe_product(pe, 0)
            stream_pe(pe, "ctx_k")
            stream_pe(pe, "ctx_v")
            gates_pe_rows(pe, 0)
            stream_pe(pe, "ctx_kv")
            gates_pe_cols(pe, 0)
            pe.wait_ge(gt_done, 1)
            conv_pe(pe, ck_nat, 0, 2, True)
            state_pe(pe)
            qk_turn_pe(pe, 0)
            pe.wait_ge(hn_stored, TURN_BANKS[1])
            turn_pe(pe, "u_x", cen)
            turned(pe, "u_x")
            gates_pe_product(pe, 1)
            stream_pe(pe, "x_qk")
            stream_pe(pe, "x_v")
            gates_pe_rows(pe, 1)
            stream_pe(pe, "x_kv")
            gates_pe_cols(pe, 1)
            pe.wait_ge(gt_done, 2)
            conv_pe(pe, qk_nat, 2, 4, True)
            mlstm_pe(pe)
            qk_turn_pe(pe, 1)
            stream_pe(pe, "x_o")
            stream_pe(pe, "x_z")
            stream_pe(pe, "x_q")
            qk_turn_pe(pe, 2)
            attention2_pe(pe)
            pe.wait_ge(a2_fetched, NQ)
            stream_pe(pe, "x_zb")
            stream_pe(pe, "x_g")
            pe.wait_ge(a2_copied[0], NH_B)
            pe.wait_ge(a2_copied[1], NH_B)
            turn_pe(pe, "ha", ha)
            turned(pe, "ha")
            stream_pe(pe, "ba")
            turn_pe(pe, "ob", ob)
            turned(pe, "ob")
            gate_row_pe(pe)
            stream_pe(pe, "bb")
            turn_pe(pe, "merge", sg)
            turned(pe, "merge")
            stream_pe(pe, "wo")

        @block.gpsimd
        def _(pool):
            pool.wait_ge(w_used, AT["w_in"][0])
            pool.dma_start(log_mask[:], A["log_mask"]).then_inc(att_consts, 16)
            pool.wait_ge(at_fetched, N_HEADS1)
            for dst, name in ((pr(LDT), "ssm_log_dt"), (pr(LR), "ssm_a_re"), (pr(LI), "ssm_a_im"),
                              (c_re[:], "ssm_c_re"), (c_im[:], "ssm_c_im"), (b_re[:], "ssm_b_re"), (b_im[:], "ssm_b_im")):
                pool.dma_start(dst, A[name]).then_inc(ssm_consts, 16)
            pool.wait_ge(sp_dve, 3)
            pool.dma_start(row_d[:], A["ssm_d"].partition_broadcast(P)).then_inc(row_ready, 16)
            pool.dma_start(row_bglu[:], A["ssm_b_glu"].partition_broadcast(P)).then_inc(row_ready, 16)
            pool.wait_ge(w_used, AT["ffn2"][0])
            for dst, name in B2_LOADS:
                pool.dma_start(dst, A[name]).then_inc(b2_consts, 16)
            for dst, name in B2_ROWS:
                pool.dma_start(dst, A[name].partition_broadcast(P)).then_inc(b2_consts, 16)
            pool.wait_ge(w_used, AT["mod"][0])
            pool.dma_start(fin_row[:], A["final_norm"].partition_broadcast(P)).then_inc(fin_loaded, 16)
            pool.dma_start(cen[:], A["ctx_2"].rearrange("(h p) d -> p h d", p=P)).then_inc(ctx_loaded, 16)
            pool.wait_ge(gt_prod, 2)
            pool.dma_start(neg_mask[:], A["neg_mask"]).then_inc(mask_loaded, 16)
            pool.wait_ge(nt_turned, turns["ha"][0] + 16)
            pool.dma_start(ln_w_row[:], A["ln_w_2"].partition_broadcast(P)).then_inc(ln_loaded, 16)
            pool.dma_start(ln_b_row[:], A["ln_b_2"].partition_broadcast(P)).then_inc(ln_loaded, 16)


def lay_out(inputs):
    def a(name):
        return np.ascontiguousarray(inputs[name])

    def by_feature(v):
        return np.ascontiguousarray(v.reshape(-1, P).T)

    o = {"x": a("x")[0]}
    for n in ("ffn1_w_gate", "ffn1_w_up", "ffn1_w_down"):
        o[n] = a(n)[0]
    o["gains"] = np.concatenate([by_feature(a("ffn1_norm")), by_feature(a("mix_norm")),
                                 np.concatenate([by_feature(a("ssm_out_norm")), by_feature(a("attn_out_norm"))], 1),
                                 by_feature(a("ffn2_norm"))], axis=1)
    for n in ("w_in", "ssm_w_glu", "w_out", "ffn2_w_gate", "ffn2_w_up", "ffn2_w_down"):
        o[n] = a(n)[0]
    for n in ("ssm_a_re", "ssm_a_im"):
        o[n] = np.ascontiguousarray(a(n)[0].reshape(ST, P).T)
    o["ssm_log_dt"] = np.ascontiguousarray(np.repeat(a("ssm_log_dt")[0], STATE).reshape(ST, P).T)
    for n in ("ssm_c_re", "ssm_c_im"):
        c = a(n)[0].reshape(ST, 2, GROUP, STATE)
        o[n] = np.zeros((P, ST, 2 * GROUP), np.float32)
        for g in range(2):
            o[n][STATE * g:STATE * (g + 1), :, GROUP * g:GROUP * (g + 1)] = c[:, g].transpose(2, 0, 1)
    for n in ("ssm_b_re", "ssm_b_im"):
        b = a(n)[0].reshape(8, 4, 2, STATE, GROUP)
        o[n] = np.zeros((P, 8, P), np.float32)
        for j in range(4):
            for g in range(2):
                q = 32 * j + GROUP * g
                o[n][q:q + GROUP, :, STATE * g:STATE * (g + 1)] = b[:, j, g].transpose(2, 0, 1)
    o["ssm_d"] = a("ssm_d").reshape(-1)
    o["ssm_b_glu"] = a("ssm_b_glu").reshape(-1)
    for n in ("w_mod_2", "w_in_2", "w_branch_a_2", "w_branch_b_2", "w_out_2"):
        o[n] = a(n)[0]
    o["ctx_2"] = a("ctx_2")[0]
    for n in ("final_norm", "b_if_2", "q_norm_w_2", "k_norm_w_2", "ln_w_2", "ln_b_2"):
        o[n] = a(n).reshape(-1)
    o["c_col"] = np.stack([by_feature(a("c_2").reshape(-1)), by_feature(a("c_ctx_2").reshape(-1))], axis=1)
    o["b_mod_col"] = by_feature(a("b_mod_2").reshape(-1))
    o["conv_w"] = np.ascontiguousarray(a("conv_w_2")[0].reshape(3, KT, P).transpose(2, 1, 0))
    o["conv_b"] = by_feature(a("conv_b_2").reshape(-1))
    o["mh_col"] = by_feature(a("mh_norm_w_2").reshape(-1))
    o["gate_w"] = np.ascontiguousarray(a("w_in_2")[0][:, GATE0:KB0].reshape(KT, P, KB0 - GATE0).transpose(1, 0, 2))
    half = HD_B // 4
    inv = 10000.0 ** (-np.arange(0, 2 * half, 2) / (2 * half))
    tok = np.arange(SEQ)
    angle = np.stack([(tok // GRID_W)[:, None] * inv, (tok % GRID_W)[:, None] * inv], axis=1)
    o["rope"] = np.ascontiguousarray(np.stack([np.cos(angle), np.sin(angle)]).reshape(2, 2, P, 2, half)
                                     .transpose(2, 0, 1, 3, 4).astype(np.float32))
    key, query = np.arange(SEQ)[:, None], np.arange(SEQ)[None, :]
    seen = np.stack([key <= query, key >= query])
    o["neg_mask"] = np.ascontiguousarray(np.where(seen, 0.0, BIG_NEG).astype(np.float32)
                                         .reshape(2, 2, P, SEQ).transpose(2, 0, 1, 3))
    t, s = np.arange(SEQ)[:, None], np.arange(SEQ)[None, :]
    n_branches = sum((t >= s) & (t - s <= w) & ((t - s) % d == 0) for w, d in ((128, 1), (512, 4), (2048, 16)))
    log_n = np.where(n_branches > 0, np.log(np.maximum(n_branches, 1)), BIG_NEG).astype(np.float32)
    o["log_mask"] = np.concatenate([log_n[:P, :P], log_n[P:, :]], axis=1)
    o["ident"] = np.eye(P, dtype=np.float32)
    return o


def kernel(**inputs):
    from concourse import bacc
    from concourse.bass_utils import run_bass_kernel_spmd

    nc = bacc.Bacc("TRN2", target_bir_lowering=False, num_devices=1)
    arrays, A = {}, {}
    for name, a in lay_out({k: np.asarray(v) for k, v in inputs.items()}).items():
        arrays[f"in_{name}"] = a
        A[name] = nc.dram_tensor(f"in_{name}", a.shape, mybir.dt.from_np(a.dtype), kind="ExternalInput").ap()
    out = nc.dram_tensor("out_x", (SEQ, D), F32, kind="ExternalOutput").ap()
    build(nc, A, out)
    r = run_bass_kernel_spmd(nc, [arrays], core_ids=[0])
    return r.results[0]["out_x"].reshape(1, SEQ, D)
```

```python
from contextlib import ExitStack

import numpy as np

import concourse.bass as bass
from concourse import mybir

F32 = mybir.dt.float32
F32R = mybir.dt.float32r
I32 = mybir.dt.int32
ALU = mybir.AluOpType
ACT = mybir.ActivationFunctionType
X_AXIS = mybir.AxisListType.X

P = 128
SEQ = 256
D = 2048
KT = D // P
D_FF = 5504
FT = D_FF // P
BLK = 512
HALF = D // 2
N_HEADS1, HD1 = 16, 64
GROUP, STATE = 16, 64
ST = 32
FRAME = 128
EPS = 1e-6
SLOTS = 4
LEAD = 4
BIG_NEG = -1e30
TWO_PI = 6.283185307179586
NH_A, DK_A, DV_A = 8, 128, 256
VA = DV_A + 1
NH_B, NKV_B, HD_B = 16, 4, 128
GRID_W = 64
ALPHA = 2.0 ** 0.25
N_IN = 17440
GATE0 = 2 * NH_A * DK_A + NH_A * DV_A
KB0 = GATE0 + 4 * NH_A

JOBS = [("ffn1", None, None), ("w_u", 8, 2), ("w_qkv", 8, 6), ("mod", 8, 8), ("glu", 4, 2), ("w_out", 8, 4), ("ffn2", None, None),
        ("mod_gate", 8, 4), ("ctx_k", 8, 2), ("ctx_v", 8, 4), ("ctx_kv", 8, 2),
        ("x_qk", 8, 4), ("x_v", 8, 4), ("x_kv", 8, 2), ("x_o", 8, 4), ("x_q", 8, 4), ("x_z", 8, 4),
        ("x_ga", 8, 4), ("x_zb", 8, 4), ("x_gb", 8, 4), ("ba", 8, 4), ("bb", 8, 4), ("wo", 8, 4)]
DOWN_CHUNKS = 44
FFN_CHUNKS = 11 * 16 + 2 * DOWN_CHUNKS


def plan():
    chunk, pair, where = 0, 0, {}
    for name, nch, nb in JOBS:
        where[name] = (chunk, pair)
        chunk += FFN_CHUNKS if nch is None else nch * nb
        pair += 13 if nch is None else nb // 2
    where["end"] = (chunk, pair)
    return where


AT = plan()
TOTAL_CHUNKS = AT["end"][0]


class Steps:

    def __init__(self, eng, sem):
        self.eng, self.sem, self.n = eng, sem, 0

    def did(self, ins):
        self.n += 1
        ins.then_inc(self.sem, 1)
        return self.n

    def settle(self):
        self.eng.wait_ge(self.sem, self.n)


def build(nc, A, out):
    ctx = ExitStack()
    with ctx:
        def sem(name):
            return ctx.enter_context(nc.semaphore(name))

        top = [16512]

        def at(name, shape, dt=F32, offset=None):
            size = 4 * int(np.prod(shape[1:]))
            if offset is None:
                offset = top[0]
                top[0] += -(-size // 32) * 32
            assert offset + size <= 229344, (name, offset, size)
            return nc.alloc_sbuf_tensor_at(name, shape, dt, offset=offset)

        class Region:
            def __init__(self, offset):
                self.o = offset

            def __call__(self, name, shape, dt=F32):
                t = at(name, shape, dt, offset=self.o)
                self.o += -(-4 * int(np.prod(shape[1:])) // 32) * 32
                return t

        resid = at("resid", [P, 2, D])
        act_hi = at("act_hi", [P, KT, SEQ], F32R)
        act_lo = at("act_lo", [P, KT, SEQ], F32R)
        junk_full = at("junk_full", [P, 2, D], offset=16512 + 4 * 2 * D)
        junk_low = at("junk_low", [P, 2, HALF], offset=16512 + 4 * 2 * D)
        junk_high = at("junk_high", [P, 2, HALF], offset=16512 + 4 * 2 * D + 4 * 2 * HALF)
        w_raw = at("w_raw", [P, SLOTS, 2 * BLK])
        w_hi = at("w_hi", [P, SLOTS, 2 * BLK], F32R)
        w_lo = at("w_lo", [P, SLOTS, 2 * BLK], F32R)
        ident = at("ident_sb", [P, P])
        gains = at("gains_sb", [P, 4, KT])
        stat = at("stat", [P, 64])
        dscale = at("dscale", [P, 2, P])
        stage0 = top[0]

        r = Region(stage0)
        g_hi = r("g_hi", [P, FT, SEQ], F32R)
        g_lo = r("g_lo", [P, FT, SEQ], F32R)
        silu_gate = r("silu_gate", [P, 2, BLK])
        gated = r("gated", [P, 2, BLK])

        acc = ctx.enter_context(nc.psum_tensor("acc", [P, 2, 2, BLK], F32))
        pst = ctx.enter_context(nc.psum_tensor("pst", [P, 4, BLK], F32))

        w_raw_ready = [sem(f"w_raw_ready{s}") for s in range(SLOTS)]
        w_hi_done, w_lo_done, w_used = sem("w_hi_done"), sem("w_lo_done"), sem("w_used")
        fetched = [sem("fetched_a"), sem("fetched_b")]
        consts_ready, x_ready = sem("consts_ready"), sem("x_ready")
        act_steps, dve_steps = sem("act_steps"), sem("dve_steps")
        nt_square, nt_mean, nt_root, nt_diag = sem("nt_square"), sem("nt_mean"), sem("nt_root"), sem("nt_diag")
        nt_turned, nt_hi, nt_lo = sem("nt_turned"), sem("nt_hi"), sem("nt_lo")
        g_turned, g_hi_done, g_lo_done = sem("g_turned"), sem("g_hi_done"), sem("g_lo_done")
        steps = None
        out_done = sem("out_done")

        def cols(w, k0, col, n=BLK):
            return w.rearrange("(k p) n -> p k n", p=P)[:, k0:k0 + 2, bass.ds(col, n)]

        def load_chunk(sp, s, src, c=None):
            c = s if c is None else c
            if not isinstance(c, int) or c >= SLOTS:
                sp.wait_ge(w_lo_done, c - SLOTS + 1)
            view = w_raw[:, s % SLOTS, :]
            if len(src.shape) == 3:
                view = view.rearrange("p (k n) -> p k n", k=src.shape[1])
            sp.dma_start(view, src).then_inc(w_raw_ready[s % SLOTS], 16)

        def round_chunk(act, s, c=None, q=None):
            if s >= TOTAL_CHUNKS:
                return
            act.wait_ge(w_raw_ready[s % SLOTS], 16 * ((s // SLOTS if q is None else q) + 1))
            c = s if c is None else c
            if not isinstance(c, int) or c >= SLOTS:
                act.wait_ge(w_used, c - SLOTS + 1)
            act.activation(w_hi[:, s % SLOTS, :], w_raw[:, s % SLOTS, :], ACT.Copy).then_inc(w_hi_done, 1)

        def rest_chunk(dve, s, c=None):
            if s >= TOTAL_CHUNKS:
                return
            dve.wait_ge(w_hi_done, (s if c is None else c) + 1)
            dve.tensor_tensor(w_lo[:, s % SLOTS, :], w_raw[:, s % SLOTS, :],
                              w_hi[:, s % SLOTS, :].bitcast(F32), ALU.subtract).then_inc(w_lo_done, 1)

        def split_ahead(eng, s0, k, i, nch, first=LEAD, last=None):
            for j in range(first, nch + LEAD if last is None else last):
                s = s0 + j
                c = None if i is None else i * k + s
                if eng is nc_act:
                    round_chunk(eng, s, c, None if i is None else i * (k // SLOTS) + s // SLOTS)
                else:
                    rest_chunk(eng, s, c)

        nc_act, nc_dve = nc.scalar, nc.vector

        def block_product(pe, s0, c0, hi, lo, par, nch, pair, halves=(0, 1), between=None):
            pe.wait_ge(fetched[par], pair + 1)
            for j in range(nch):
                pe.wait_ge(w_lo_done, c0 + j + 1)
                slot = (s0 + j) % SLOTS
                for kk in range(2):
                    k = 2 * j + kk
                    wh = w_hi[:, slot, kk * BLK:(kk + 1) * BLK]
                    wl = w_lo[:, slot, kk * BLK:(kk + 1) * BLK]
                    for h in halves:
                        xh, xl = hi[:, k, h * P:(h + 1) * P], lo[:, k, h * P:(h + 1) * P]
                        o = acc[:, par, h, :]
                        pe.matmul(o, xh, wh, start=k == 0, stop=False)
                        pe.matmul(o, xh, wl, start=False, stop=False)
                        mm = pe.matmul(o, xl, wh, start=False, stop=k == 2 * nch - 1)
                mm.then_inc(w_used, 1)
                if between is not None:
                    between()

        turns = {}
        turn_count = [0, 0, 0]

        def plan_turn(name, n, normed):
            turns[name] = (turn_count[0], turn_count[1], n, normed)
            turn_count[0] += n
            turn_count[1] += int(normed)

        for name, n, normed in (("ffn1", 16, True), ("mix", 16, True), ("y", 8, False), ("ssm", 8, True),
                                ("att", 8, True), ("ffn2", 16, True), ("u_ctx", 16, True), ("u_x", 16, True),
                                ("ha", 16, False), ("ob", 16, False), ("merge", 16, False)):
            plan_turn(name, n, normed)

        def turn_act(act, name, src, gain=None, junk=None, width=D, dst=0, bias=None):
            t0, c0, n, normed = turns[name]
            if normed:
                for h in range(2):
                    act.activation(junk[:, h, :], src[:, h, :], ACT.Square,
                                   accum_out=stat[:, h:h + 1]).then_inc(nt_square, 1)
                act.wait_ge(nt_mean, c0 + 1)
                act.activation(stat[:, 4:6], stat[:, 2:4], ACT.Sqrt).then_inc(nt_root, 1)
            for k in range(n):
                act.wait_ge(nt_turned, t0 + k + 1)
                o, i = act_hi[:, dst + k, :], pst[:, (t0 + k) % 4, 0:SEQ]
                if bias is not None:
                    ins = act.activation(o, i, ACT.Identity, scale=gain[:, k:k + 1], bias=bias[:, k:k + 1])
                elif gain is not None:
                    ins = act.activation(o, i, ACT.Copy, scale=gain[:, k:k + 1])
                else:
                    ins = act.activation(o, i, ACT.Copy)
                ins.then_inc(nt_hi, 1)

        def turn_dve(dve, name, gain=None, width=D, dst=0, bias=None, tmp=None):
            t0, c0, n, normed = turns[name]
            if normed:
                dve.wait_ge(nt_square, 2 * (c0 + 1))
                dve.tensor_scalar(stat[:, 2:4], stat[:, 0:2], 1.0 / width, EPS, ALU.mult, ALU.add).then_inc(nt_mean, 1)
                dve.wait_ge(nt_root, c0 + 1)
                steps.did(dve.reciprocal(stat[:, 6:8], stat[:, 4:6]))
                steps.settle()
                for h in range(2):
                    dve.tensor_scalar(dscale[:, h, :], ident[:], stat[:, 6 + h:7 + h], None,
                                      ALU.mult).then_inc(nt_diag, 1)
            for k in range(n):
                dve.wait_ge(nt_hi, t0 + k + 1)
                o, i = act_lo[:, dst + k, :], pst[:, (t0 + k) % 4, 0:SEQ]
                hi = act_hi[:, dst + k, :].bitcast(F32)
                if bias is not None:
                    steps.did(dve.tensor_scalar(tmp[:, k % 2, :], i, gain[:, k:k + 1], bias[:, k:k + 1],
                                                ALU.mult, ALU.add))
                    steps.settle()
                    ins = dve.tensor_tensor(o, tmp[:, k % 2, :], hi, ALU.subtract)
                elif gain is not None:
                    ins = dve.scalar_tensor_tensor(out=o, in0=i, scalar=gain[:, k:k + 1], in1=hi,
                                                   op0=ALU.mult, op1=ALU.subtract)
                else:
                    ins = dve.tensor_tensor(o, i, hi, ALU.subtract)
                ins.then_inc(nt_lo, 1)

        def turn_pe(pe, name, src):
            t0, c0, n, normed = turns[name]
            if normed:
                pe.wait_ge(nt_diag, 2 * (c0 + 1))
            for k in range(n):
                if t0 + k >= 4:
                    pe.wait_ge(nt_lo, t0 + k - 3)
                for h in range(2):
                    o = pst[:, (t0 + k) % 4, h * P:(h + 1) * P]
                    lhs = src[:, h, k * P:(k + 1) * P]
                    if normed:
                        mm = pe.matmul(o, lhs, dscale[:, h, :], start=True, stop=True)
                    else:
                        mm = pe.transpose(o, lhs, ident[:])
                mm.then_inc(nt_turned, 1)

        def turned(eng, name):
            t0, _, n, _ = turns[name]
            eng.wait_ge(nt_lo, t0 + n)

        NB = 11

        def ffn_iterations(eng, name, it):
            s0, p0 = AT[name]
            it(0, s0, s0, p0, None)
            with eng.Fori(1, NB - 1) as i:
                it(i, s0, i * 16 + s0, i + p0, i)
            it(NB - 1, s0 + 16 * (NB - 1), s0 + 16 * (NB - 1), p0 + NB - 1, None)

        def first(b):
            return isinstance(b, int) and b == 0

        def ffn_sp(sp, name, w_gate, w_up, w_down):
            def it(b, s, c, p, i):
                col = D_FF - BLK if isinstance(b, int) and b == NB - 1 else b * BLK
                for m, w in enumerate((w_gate, w_up)):
                    for j in range(8):
                        load_chunk(sp, s + 8 * m + j, cols(w, 2 * j, col), c + 8 * m + j)
            ffn_iterations(sp, name, it)
            s1 = AT[name][0] + 16 * NB
            wd = w_down.rearrange("(k p) n -> p k n", p=P)
            with sp.Fori(0, 2) as i:
                for j in range(DOWN_CHUNKS):
                    load_chunk(sp, s1 + j, wd[:, min(j, FT - 1), bass.ds(i * 1024, 1024)],
                               i * DOWN_CHUNKS + s1 + j)

        def tiles_of(b):
            return slice(FT - 4, FT) if isinstance(b, int) and b == NB - 1 else (
                slice(4 * b, 4 * b + 4) if isinstance(b, int) else bass.ds(b * 4, 4))

        turned_tiles = pst[:, 0:2, :].rearrange("p a (b t) -> p (a b) t", b=2)

        def ffn_act(act, name, n_use):
            b0 = NB * n_use

            def hi_tiles(b):
                act.wait_ge(g_turned, b + (b0 + 1))
                act.activation(g_hi[:, tiles_of(b), :], turned_tiles, ACT.Copy).then_inc(g_hi_done, 1)

            def it(b, s, c, p, i):
                split_ahead(act, s, 16, i, 16, LEAD, 8 + LEAD)
                act.wait_ge(w_used, c + 8)
                act.wait_ge(fetched[1], p + 1)
                act.activation(silu_gate[:], acc[:, 0, :, :], ACT.Silu).then_inc(fetched[0], 1)
                if not first(b):
                    hi_tiles(b - 1)
                split_ahead(act, s, 16, i, 16, 8 + LEAD, 16 + LEAD)
            ffn_iterations(act, name, it)
            hi_tiles(NB - 1)
            s1 = AT[name][0] + 16 * NB
            with act.Fori(0, 2) as i:
                split_ahead(act, s1, DOWN_CHUNKS, i, DOWN_CHUNKS)

        def ffn_dve(dve, name, n_use):
            b0 = NB * n_use

            def lo_tiles(b):
                dve.wait_ge(g_hi_done, b + (b0 + 1))
                dve.tensor_tensor(g_lo[:, tiles_of(b), :], turned_tiles,
                                  g_hi[:, tiles_of(b), :].bitcast(F32), ALU.subtract).then_inc(g_lo_done, 1)

            def it(b, s, c, p, i):
                split_ahead(dve, s, 16, i, 16, LEAD, 8 + LEAD)
                if not first(b):
                    lo_tiles(b - 1)
                split_ahead(dve, s, 16, i, 16, 8 + LEAD, 16 + LEAD)
                dve.wait_ge(w_used, c + 16)
                dve.wait_ge(fetched[0], p + 2)
                if not first(b):
                    dve.wait_ge(g_turned, b + b0)
                dve.tensor_tensor(gated[:], silu_gate[:], acc[:, 1, :, :], ALU.mult).then_inc(fetched[1], 1)
            ffn_iterations(dve, name, it)
            lo_tiles(NB - 1)
            s1 = AT[name][0] + 16 * NB
            with dve.Fori(0, 2) as i:
                split_ahead(dve, s1, DOWN_CHUNKS, i, DOWN_CHUNKS)
                dve.wait_ge(w_used, i * DOWN_CHUNKS + (s1 + DOWN_CHUNKS))
                for par in range(2):
                    o = resid[:, :, bass.ds(i * 1024 + par * BLK, BLK)]
                    dve.scalar_tensor_tensor(out=o, in0=acc[:, par, :, :], scalar=0.5, in1=o,
                                             op0=ALU.mult, op1=ALU.add).then_inc(fetched[par], 1)

        def ffn_pe(pe, name, n_use):
            b0 = NB * n_use

            def turn_gated(b, p):
                pe.wait_ge(fetched[1], p + 2)
                pe.wait_ge(g_lo_done, b + (b0 + 1))
                for t in range(4):
                    for h in range(2):
                        mm = pe.transpose(turned_tiles[:, t, h * P:(h + 1) * P],
                                          gated[:, h, t * P:(t + 1) * P], ident[:])
                mm.then_inc(g_turned, 1)

            def it(b, s, c, p, i):
                block_product(pe, s, c, act_hi, act_lo, 0, 8, p)
                if not first(b):
                    turn_gated(b - 1, p - 1)
                block_product(pe, s + 8, c + 8, act_hi, act_lo, 1, 8, p)
            ffn_iterations(pe, name, it)
            s0, p0 = AT[name]
            turn_gated(NB - 1, p0 + NB - 1)
            s1 = s0 + 16 * NB
            pe.wait_ge(g_lo_done, NB + b0 + 1)
            with pe.Fori(0, 2) as i:
                for par in range(2):
                    pe.wait_ge(fetched[par], i + (p0 + NB + 1))
                for j in range(FT):
                    pe.wait_ge(w_lo_done, i * DOWN_CHUNKS + (s1 + j + (1 if j < FT - 1 else 2)))
                    slot = (s1 + j) % SLOTS
                    for par in range(2):
                        wh = w_hi[:, slot, par * BLK:(par + 1) * BLK]
                        wl = w_lo[:, slot, par * BLK:(par + 1) * BLK]
                        for h in range(2):
                            gh, gl = g_hi[:, j, h * P:(h + 1) * P], g_lo[:, j, h * P:(h + 1) * P]
                            o = acc[:, par, h, :]
                            pe.matmul(o, gh, wh, start=j == 0, stop=False)
                            pe.matmul(o, gh, wl, start=False, stop=False)
                            mm = pe.matmul(o, gl, wh, start=False, stop=j == FT - 1)
                    mm.then_inc(w_used, 1 if j < FT - 1 else 2)

        def job(name):
            nch, nb = next((n, b) for j, n, b in JOBS if j == name)
            return AT[name] + (nch, nb)

        def pairs(eng, name, body, unrolled=False):
            s0, p0, nch, nb = job(name)
            if nb == 2 or unrolled or name == JOBS[-1][0]:
                for i in range(nb // 2):
                    s = s0 + 2 * nch * i
                    body(i, s, s, p0 + i)
            else:
                with eng.Fori(0, nb // 2) as i:
                    body(i, s0, i * (2 * nch) + s0, i + p0)

        def stream_sp(sp, name, w, col0):
            nch = job(name)[2]

            def body(i, s, c, p):
                for m in range(2):
                    for j in range(nch):
                        load_chunk(sp, s + nch * m + j, cols(w, 2 * j, (i * 2 + m) * BLK + col0), c + nch * m + j)
            pairs(sp, name, body)

        def stream_pe(pe, name, halves=(0, 1), between=None):
            nch = job(name)[2]

            def body(i, s, c, p):
                for m in range(2):
                    block_product(pe, s + nch * m, c + nch * m, act_hi, act_lo, m, nch, p, halves, between)
            pairs(pe, name, body, between is not None)

        def stream_split(eng, name, fetch=None, between=None, unrolled=False):
            nch = job(name)[2]

            def body(i, s, c, p):
                for m in range(2):
                    if between is None:
                        split_ahead(eng, s + nch * m, 2 * nch, None if isinstance(i, int) else i, nch)
                    else:
                        for j in range(nch):
                            between()
                            split_ahead(eng, s + nch * m, 2 * nch, None, nch, j + LEAD, j + LEAD + 1)
                    if fetch is not None:
                        eng.wait_ge(w_used, c + nch * (m + 1))
                        fetch(m, i * 2 + m, p)
            pairs(eng, name, body, between is not None or unrolled)

        def spread(step, eng, steps, *names):
            chunks = sum(job(name)[2] * job(name)[3] for name in names)
            state = [0, 0]

            def between():
                state[0] += 1
                while state[1] < state[0] * steps // chunks:
                    step(eng, state[1])
                    state[1] += 1
            return between

        r = Region(stage0)
        prj = r("prj", [P, 2, 4 * HALF])
        q_nat, k_nat, v_nat, u_nat = (prj[:, :, n * HALF:(n + 1) * HALF] for n in range(4))
        att, spare, ssm_y = q_nat, k_nat, u_nat
        u_t = r("u_t", [P, 8, SEQ])
        mix_x = r.o
        rot_cos, rot_sin = r("rot_cos", [P, ST, FRAME]), r("rot_sin", [P, ST, FRAME])
        b_re, b_im = (r(n, [P, 8, P]) for n in ("b_re", "b_im"))
        ssm_temps = r.o
        turn_tmp = Region(ssm_temps)("turn_tmp", [P, ST, FRAME // 2])
        prod = r("prod", [P, 2, SEQ])
        st_z = r("st_z", [P, 2, 2, SEQ])
        r = Region(stage0 + 4 * (2 * FT * SEQ + 4 * BLK))
        par_ = r("ssm_par", [P, 22, ST])
        cf_re, cf_im = (r(n, [P, ST, 2 * GROUP]) for n in ("cf_re", "cf_im"))
        cf_tmp = r("cf_tmp", [P, 3, ST // 8, 2 * GROUP])
        frame_init = r("frame_init", [P, 2, 2])
        c_col = r("c_col", [P, 2, KT])
        pick = r("pick", [P, 2])
        assert r.o <= 229344
        r = Region(ssm_temps + 4 * 6 * SEQ)
        z_prod = r("z_prod", [P, 2, SEQ])
        st_s = r("st_s", [P, 3, 2, SEQ])
        assert r.o <= stage0 + 4 * (2 * FT * SEQ + 4 * BLK), (r.o, stage0 + 4 * (2 * FT * SEQ + 4 * BLK))
        r = Region(mix_x)
        q_t, k_t = r("q_t", [P, 8, SEQ]), r("k_t", [P, 8, SEQ])
        log_mask = r("log_mask", [P, 3 * P])
        scores, probs, probs_t = (r(n, [P, 2, 3 * P]) for n in ("scores", "probs", "probs_t"))
        row_max, row_sum, row_inv = (r(n, [P, 2 * N_HEADS1]) for n in ("row_max", "row_sum", "row_inv"))
        row_bglu = r("row_bglu", [P, HALF])
        mod_nat = r("mod_nat", [P, 2 * D])
        assert r.o <= stage0 + 4 * (2 * FT * SEQ + 4 * BLK)
        row_d = at("row_d", [P, HALF], offset=ssm_temps + 4 * 8 * SEQ)

        att_consts, ssm_consts, row_ready = sem("att_consts"), sem("ssm_consts"), sem("row_ready")
        b_ready = sem("b_ready")
        tq_turned, tq_fetched = sem("tq_turned"), [sem("tq_fetched_act"), sem("tq_fetched_dve")]
        at_scores, at_max, at_probs, at_turned, at_copied, at_out, at_fetched = (
            sem("at_" + n) for n in ("scores", "max", "probs", "turned", "copied", "out", "fetched"))
        sp_act, sp_ready, sp_recip, tables_ready = (sem("sp_" + n) for n in ("act", "ready", "recip", "tables"))
        pool_steps, ssm_z = sem("pool_steps"), sem("ssm_z")
        ssm_b, ssm_b_read, ssm_s, ssm_y_done, ssm_y_read, ssm_gelu = (
            sem(n) for n in ("ssm_b", "ssm_b_read", "ssm_s", "ssm_y_done", "ssm_y_read", "ssm_gelu"))
        glu_pre, glu_sig, glu_out = sem("glu_pre"), sem("glu_sig"), sem("glu_out")

        def fetch_prj(act, first):
            def fetch(m, blk, p):
                act.activation(prj[:, :, bass.ds((first + blk) * BLK, BLK)], acc[:, m, :, :],
                               ACT.Copy).then_inc(fetched[m], 1)
            return fetch

        TQ = [(u_t, 3 * HALF, n) for n in range(4)] + [(q_t, 0, n) for n in range(4)] + [(k_t, HALF, n) for n in range(4)]

        def turn_qku_pe(pe, first, last, after):
            for m in range(2):
                pe.wait_ge(fetched[m], AT[after][1] + 1)
            for n, (dst, col, t) in list(enumerate(TQ))[first:last]:
                if n >= 4:
                    pe.wait_ge(tq_fetched[n % 2], (n - 4) // 2 + 1)
                for tt in range(2):
                    for h in range(2):
                        c = col + (2 * t + tt) * P
                        mm = pe.transpose(pst[:, n % 4, tt * SEQ + h * P:tt * SEQ + (h + 1) * P],
                                          prj[:, h, c:c + P], ident[:])
                mm.then_inc(tq_turned, 1)

        def turn_qku_fetch(eng, par, first, last, copy):
            for n, (dst, col, t) in enumerate(TQ):
                if n % 2 == par and first <= n < last:
                    eng.wait_ge(tq_turned, n + 1)
                    copy(dst[:, 2 * t:2 * t + 2, :], pst[:, n % 4, :].rearrange("p (a t) -> p a t", a=2)).then_inc(
                        tq_fetched[par], 1)

        def head_rows(n):
            return slice(64 * (n % 2), 64 * (n % 2) + 64), n // 2

        def attention1_step_pe(pe, s):
            if s < N_HEADS1:
                if s >= 2:
                    pe.wait_ge(at_max, s - 1)
                rows, t = head_rows(s)
                pe.matmul(pst[:, s % 2, 0:P], q_t[rows, t, 0:P], k_t[rows, t, 0:P], start=True, stop=True)
                pe.matmul(pst[:, s % 2, P:3 * P], q_t[rows, t, P:SEQ], k_t[rows, t, :],
                          start=True, stop=True).then_inc(at_scores, 1)
            if 1 <= s <= N_HEADS1:
                n = s - 1
                pe.wait_ge(at_probs, n + 1)
                if n >= 2:
                    pe.wait_ge(at_copied, n - 1)
                for b in range(3):
                    mm = pe.transpose(pst[:, 2 + n % 2, b * P:(b + 1) * P],
                                      probs[:, n % 2, b * P:(b + 1) * P], ident[:])
                mm.then_inc(at_turned, 1)
            if s >= 2:
                n = s - 2
                pe.wait_ge(at_copied, n + 1)
                if n >= 2:
                    pe.wait_ge(at_fetched, n - 1)
                o = acc[:, n % 2, 1, :]
                v = v_nat[:, :, n * HD1:(n + 1) * HD1]
                pe.matmul(o[:, 0:HD1], probs_t[:, n % 2, 0:P], v[:, 0, :], start=True, stop=True)
                pe.matmul(o[:, HD1:2 * HD1], probs_t[:, n % 2, P:2 * P], v[:, 0, :], start=True, stop=False)
                pe.matmul(o[:, HD1:2 * HD1], probs_t[:, n % 2, 2 * P:3 * P], v[:, 1, :],
                          start=False, stop=True).then_inc(at_out, 1)

        def attention1_step_act(act, s):
            if s < N_HEADS1:
                act.wait_ge(at_max, s + 1)
                if s >= 2:
                    act.wait_ge(at_turned, s - 1)
                for h, (a, b) in enumerate(((0, P), (P, 3 * P))):
                    ins = act.activation(probs[:, s % 2, a:b], scores[:, s % 2, a:b], ACT.Exp,
                                         bias=row_max[:, 2 * s + h:2 * s + h + 1],
                                         accum_out=row_sum[:, 2 * s + h:2 * s + h + 1])
                ins.then_inc(at_probs, 1)
            if 1 <= s <= N_HEADS1:
                n = s - 1
                act.wait_ge(at_turned, n + 1)
                if n >= 2:
                    act.wait_ge(at_out, n - 1)
                act.activation(probs_t[:, n % 2, :], pst[:, 2 + n % 2, 0:3 * P], ACT.Copy).then_inc(at_copied, 1)

        def attention1_step_dve(dve, s):
            if s < N_HEADS1:
                dve.wait_ge(at_scores, s + 1)
                if s >= 2:
                    dve.wait_ge(at_probs, s - 1)
                steps.did(dve.scalar_tensor_tensor(out=scores[:, s % 2, :], in0=pst[:, s % 2, 0:3 * P],
                                                   scalar=HD1 ** -0.5, in1=log_mask[:], op0=ALU.mult, op1=ALU.add))
                steps.settle()
                for h, (a, b) in enumerate(((0, P), (P, 3 * P))):
                    ins = dve.tensor_reduce(row_inv[:, 2 * s + h:2 * s + h + 1], scores[:, s % 2, a:b],
                                            X_AXIS, ALU.max)
                steps.did(ins)
                steps.settle()
                dve.tensor_scalar(row_max[:, 2 * s:2 * s + 2], row_inv[:, 2 * s:2 * s + 2], -1.0, None,
                                  ALU.mult).then_inc(at_max, 1)
            if s >= 2:
                n = s - 2
                dve.wait_ge(at_out, n + 1)
                steps.did(dve.reciprocal(row_inv[:, 2 * n:2 * n + 2], row_sum[:, 2 * n:2 * n + 2]))
                steps.settle()
                dve.tensor_tensor(att[:, :, n * HD1:(n + 1) * HD1],
                                  acc[:, n % 2, 1, 0:2 * HD1].rearrange("p (h e) -> p h e", h=2),
                                  row_inv[:, 2 * n:2 * n + 2].unsqueeze(2).broadcast_to([P, 2, HD1]),
                                  ALU.mult).then_inc(at_fetched, 1)

        LDT, LR, LI, DT, LRDT, TH, MAG, N_, RED, SINH, SIN, COS, LRE, LIM, NR, DEN, FRE, FIM, T0, T1 = range(20)

        def pr(n):
            return par_[:, n, :]

        def ssm_params_act(act, part):
            if part == 0:
                act.wait_ge(ssm_consts, 16 * 5)
                act.activation(pr(DT), pr(LDT), ACT.Exp).then_inc(sp_act, 1)
            else:
                act.wait_ge(sp_ready, 1)
                act.activation(pr(MAG), pr(LRDT), ACT.Exp).then_inc(sp_act, 1)
                act.activation(pr(SINH), pr(RED), ACT.Sin, scale=0.5).then_inc(sp_act, 1)
                act.activation(pr(SIN), pr(RED), ACT.Sin).then_inc(sp_act, 1)

        def ssm_params_pool(pool, steps):
            M, A_, S = ALU.mult, ALU.add, ALU.subtract

            def tt(o, a, b, op):
                steps.did(pool.tensor_tensor(o, a, b, op))

            def ts(o, a, s1, op0, s2=None, op1=None):
                if s2 is None:
                    steps.did(pool.tensor_scalar(o, a, s1, None, op0))
                else:
                    steps.did(pool.tensor_scalar(o, a, s1, s2, op0, op1))
            pool.wait_ge(sp_act, 1)
            tt(pr(TH), pr(LI), pr(DT), M)
            tt(pr(LRDT), pr(LR), pr(DT), M)
            steps.settle()
            magic = 1.5 * 2.0 ** 23
            ts(pr(N_), pr(TH), 1.0 / TWO_PI, M, magic, A_)
            steps.settle()
            ts(pr(T0), pr(N_), magic, S)
            steps.settle()
            c1 = 6.28125
            c2 = 0.0019350051879882812
            c3 = TWO_PI - c1 - c2
            src = TH
            for c, dst in ((c1, T1), (c2, RED), (c3, T1)):
                ts(pr(N_), pr(T0), c, M)
                steps.settle()
                tt(pr(dst), pr(src), pr(N_), S)
                steps.settle()
                src = dst
            pool.tensor_scalar(pr(RED), pr(T1), 3.1415925, -3.1415925, ALU.min, ALU.max).then_inc(sp_ready, 1)
            pool.wait_ge(sp_act, 4)
            tt(pr(T0), pr(SINH), pr(SINH), M)
            tt(pr(LIM), pr(MAG), pr(SIN), M)
            tt(pr(DEN), pr(LR), pr(LR), M)
            tt(pr(T1), pr(LI), pr(LI), M)
            steps.settle()
            ts(pr(COS), pr(T0), -2.0, M, 1.0, A_)
            pool.tensor_tensor(pr(DEN), pr(DEN), pr(T1), A_).then_inc(sp_ready, 1)
            steps.settle()
            tt(pr(LRE), pr(MAG), pr(COS), M)
            steps.settle()
            ts(pr(NR), pr(LRE), 1.0, S)
            steps.settle()
            tt(pr(FRE), pr(NR), pr(LR), M)
            tt(pr(T0), pr(LIM), pr(LI), M)
            tt(pr(FIM), pr(LIM), pr(LR), M)
            tt(pr(N_), pr(NR), pr(LI), M)
            steps.settle()
            tt(pr(FRE), pr(FRE), pr(T0), A_)
            tt(pr(FIM), pr(FIM), pr(N_), S)
            steps.settle()
            pool.wait_ge(sp_recip, 1)
            tt(pr(FRE), pr(FRE), pr(T1), M)
            tt(pr(FIM), pr(FIM), pr(T1), M)
            steps.settle()
            pool.wait_ge(ssm_consts, 16 * 5)
            n = ST // 8
            wide = [P, n, 2 * GROUP]
            for g in range(8):
                t = slice(g * n, (g + 1) * n)
                fr, fi = (par_[:, v, t].unsqueeze(2).broadcast_to(wide) for v in (FRE, FIM))
                re, im = cf_re[:, t, :], cf_im[:, t, :]
                tt(cf_tmp[:, 0], im, fi, M)
                tt(cf_tmp[:, 1], re, fi, M)
                tt(cf_tmp[:, 2], im, fr, M)
                tt(re, re, fr, M)
                steps.settle()
                tt(re, re, cf_tmp[:, 0], S)
                tt(cf_tmp[:, 1], cf_tmp[:, 1], cf_tmp[:, 2], A_)
                steps.settle()
                ts(im, cf_tmp[:, 1], -1.0, M)
                steps.settle()

        def ssm_tables_pool(pool, steps):
            M, A_, S = ALU.mult, ALU.add, ALU.subtract

            def tt(o, a, b, op):
                steps.did(pool.tensor_tensor(o, a, b, op))
            steps.did(pool.tensor_copy(rot_cos[:, :, 0:1], pr(COS).unsqueeze(2)))
            steps.did(pool.tensor_copy(rot_sin[:, :, 0:1], pr(SIN).unsqueeze(2)))
            steps.settle()
            w = 1
            while w < FRAME:
                shape = [P, ST, w]
                ec = rot_cos[:, :, w - 1:w].broadcast_to(shape)
                es = rot_sin[:, :, w - 1:w].broadcast_to(shape)
                co, si = rot_cos[:, :, 0:w], rot_sin[:, :, 0:w]
                nc_, ns_ = rot_cos[:, :, w:2 * w], rot_sin[:, :, w:2 * w]
                tmp = turn_tmp[:, :, 0:w]
                tt(nc_, co, ec, M)
                tt(ns_, co, es, M)
                tt(tmp, si, es, M)
                steps.settle()
                tt(nc_, nc_, tmp, S)
                steps.settle()
                tt(tmp, si, ec, M)
                steps.settle()
                tt(ns_, ns_, tmp, A_)
                steps.settle()
                w *= 2
            pool.sem_inc(tables_ready, 1)

        SSM_STEPS = ST + 5
        OUT_LAG = 3

        def ssm_input_pe(pe, i):
            if i >= 2:
                pe.wait_ge(ssm_b_read, i - 1)
            c, j = i // 4, 32 * (i % 4)
            for part, b in enumerate((b_re, b_im)):
                mm = pe.matmul(pst[:, i % 2, part * SEQ:(part + 1) * SEQ], b[j:j + 32, c, :],
                               u_t[j:j + 32, c, :], start=True, stop=True)
            mm.then_inc(ssm_b, 1)

        def ssm_step_pe(pe, i):
            if i + 1 < ST:
                ssm_input_pe(pe, i + 1)
            o = i - OUT_LAG
            if 0 <= o < ST:
                pe.wait_ge(ssm_s, o + 1)
                if o == ST // 2:
                    pe.wait_ge(ssm_y_read, 1)
                c = 2 * GROUP * (o % (ST // 2))
                for h in range(2):
                    dst = pst[:, 2 + h, c:c + 2 * GROUP]
                    pe.matmul(dst, st_s[:, o % 3, 0, h * P:(h + 1) * P], cf_re[:, o, :], start=True, stop=False)
                    mm = pe.matmul(dst, st_s[:, o % 3, 1, h * P:(h + 1) * P], cf_im[:, o, :], start=False, stop=True)
                mm.then_inc(ssm_y_done, 1)

        def ssm_step_dve(dve, i):
            M, A_, S = ALU.mult, ALU.add, ALU.subtract
            done = i - OUT_LAG - 1
            if done in (ST // 2 - 1, ST - 1):
                g = done // (ST // 2)
                dve.wait_ge(ssm_y_done, done + 1)
                o = ssm_y[:, :, g * BLK:(g + 1) * BLK]
                dve.tensor_tensor(o, pst[:, 2:4, :], o, A_).then_inc(ssm_y_read, 1)
            if i >= ST:
                return
            dve.wait_ge(ssm_b, i + 1)
            if i >= 2:
                dve.wait_ge(ssm_s, i - 1)

            def framed(x):
                return x.rearrange("p (f j) -> p f j", f=2)
            bu_re, bu_im = framed(pst[:, i % 2, 0:SEQ]), framed(pst[:, i % 2, SEQ:2 * SEQ])
            co = rot_cos[:, i, :].unsqueeze(1).broadcast_to([P, 2, FRAME])
            si = rot_sin[:, i, :].unsqueeze(1).broadcast_to([P, 2, FRAME])
            z = st_z[:, i % 2, :, :]
            dve.tensor_tensor(framed(z[:, 0, :]), bu_re, co, M)
            dve.tensor_tensor(framed(z[:, 1, :]), bu_im, co, M)
            dve.tensor_tensor(framed(prod[:, 0, :]), bu_im, si, M)
            dve.tensor_tensor(framed(prod[:, 1, :]), bu_re, si, M).then_inc(ssm_b_read, 1)
            dve.wait_ge(ssm_b_read, i + 1)
            dve.tensor_tensor(z[:, 0, :], z[:, 0, :], prod[:, 0, :], A_)
            steps.did(dve.tensor_tensor(z[:, 1, :], z[:, 1, :], prod[:, 1, :], S))
            steps.settle()
            mag = par_[:, MAG, i:i + 1].broadcast_to([P, FRAME])
            for part in range(2):
                ins = dve.tensor_tensor_scan(z[:, part, 0:FRAME], mag, z[:, part, 0:FRAME], 0.0, M, A_)
            steps.did(ins)
            steps.settle()
            zr, zi = z[:, 0, FRAME - 1:FRAME], z[:, 1, FRAME - 1:FRAME]
            ce, se = rot_cos[:, i, FRAME - 1:FRAME], rot_sin[:, i, FRAME - 1:FRAME]
            dve.tensor_tensor(frame_init[:, 1, 0:1], zi, se, M)
            steps.did(dve.tensor_tensor(frame_init[:, 1, 1:2], zr, se, M))
            steps.settle()
            dve.scalar_tensor_tensor(out=frame_init[:, 0, 0:1], in0=zr, scalar=ce, in1=frame_init[:, 1, 0:1], op0=M, op1=S)
            steps.did(dve.scalar_tensor_tensor(out=frame_init[:, 0, 1:2], in0=zi, scalar=ce, in1=frame_init[:, 1, 1:2],
                                               op0=M, op1=A_))
            steps.settle()
            for part in range(2):
                ins = dve.tensor_tensor_scan(z[:, part, FRAME:SEQ], mag, z[:, part, FRAME:SEQ],
                                             frame_init[:, 0, part:part + 1], M, A_)
            ins.then_inc(ssm_z, 1)

        def ssm_steps_pool(pool, steps):
            M, A_, S = ALU.mult, ALU.add, ALU.subtract

            def framed(x):
                return x.rearrange("p (f j) -> p f j", f=2)
            for i in range(ST):
                pool.wait_ge(ssm_z, i + 1)
                if i >= 3:
                    pool.wait_ge(ssm_y_done, i - 2)
                z, o = st_z[:, i % 2, :, :], st_s[:, i % 3, :, :]
                co = rot_cos[:, i, :].unsqueeze(1).broadcast_to([P, 2, FRAME])
                si = rot_sin[:, i, :].unsqueeze(1).broadcast_to([P, 2, FRAME])
                pool.tensor_tensor(framed(o[:, 0, :]), framed(z[:, 0, :]), co, M)
                pool.tensor_tensor(framed(o[:, 1, :]), framed(z[:, 1, :]), co, M)
                pool.tensor_tensor(framed(z_prod[:, 0, :]), framed(z[:, 1, :]), si, M)
                steps.did(pool.tensor_tensor(framed(z_prod[:, 1, :]), framed(z[:, 0, :]), si, M))
                steps.settle()
                pool.tensor_tensor(o[:, 0, :], o[:, 0, :], z_prod[:, 0, :], S)
                steps.did(pool.tensor_tensor(o[:, 1, :], o[:, 1, :], z_prod[:, 1, :], A_))
                steps.settle()
                pool.sem_inc(ssm_s, 1)

        def ssm_act(act):
            for g in range(2):
                act.wait_ge(ssm_y_read, g + 1)
                y = ssm_y[:, :, g * BLK:(g + 1) * BLK]
                act.activation(y, y, ACT.Gelu_apprx_tanh).then_inc(ssm_gelu, 1)

        def glu_fetch_dve(dve):
            dve.wait_ge(row_ready, 32)

            def fetch(m, blk, p):
                cs = slice(m * BLK, (m + 1) * BLK)
                dve.tensor_tensor(spare[:, :, cs], acc[:, m, :, :],
                                  row_bglu[:, cs].unsqueeze(1).broadcast_to([P, 2, BLK]), ALU.add).then_inc(fetched[m], 1)
            return fetch

        def fetch_residual(dve):
            def fetch(m, blk, p):
                o = resid[:, :, bass.ds(blk * BLK, BLK)]
                dve.tensor_tensor(o, acc[:, m, :, :], o, ALU.add).then_inc(fetched[m], 1)
            return fetch

        def glu_act(act):
            for m in range(2):
                act.wait_ge(fetched[m], AT["w_out"][1] + 1)
                o = spare[:, :, m * BLK:(m + 1) * BLK]
                act.activation(o, o, ACT.Sigmoid).then_inc(glu_sig, 1)

        def glu_dve(dve):
            for m in range(2):
                dve.wait_ge(glu_sig, m + 1)
                o = ssm_y[:, :, m * BLK:(m + 1) * BLK]
                dve.tensor_tensor(o, o, spare[:, :, m * BLK:(m + 1) * BLK], ALU.mult).then_inc(glu_out, 1)

        top2 = stage0 + 4 * (2 * FT * SEQ + 4 * BLK)
        r = Region(top2)
        gate_w_hi, gate_w_lo = r("gate_w_hi", [P, KT, 4 * NH_A], F32R), r("gate_w_lo", [P, KT, 4 * NH_A], F32R)
        neg_mask = at("neg_mask_sb", [P, 2, 2, SEQ], offset=top2)
        gate_w = r("gate_w", [P, KT, 4 * NH_A])
        b_mod_col = r("b_mod_col", [P, 3 * KT])
        mod_col = r("mod_col", [P, 3 * KT, 2])
        conv_w, conv_b = r("conv_w_sb", [P, KT, 3]), r("conv_b_sb", [P, KT])
        b_if_row = r("b_if_row", [P, 4 * NH_A])
        mh_col = r("mh_col", [P, KT])
        q_gain, k_gain = r("q_gain", [P, HD_B]), r("k_gain", [P, HD_B])
        rope = r("rope_sb", [P, 2, 2, 2, 32])
        m_rows = [r(f"m_rows{d}", [NH_A, SEQ + 1]) for d in range(2)]
        ones_row = r("ones_row", [NH_A, SEQ])
        gate_pre, gate_log, gate_tmp = (r(n, [P, 2, 4 * NH_A]) for n in ("gate_pre", "gate_log", "gate_tmp"))
        w_col = r("w_col", [P, 2, 2, NH_A])
        g_col, e_col = r("g_col", [P, 2, 2, NH_A]), r("e_col", [P, 2, 2, NH_A])
        row_s = [r(f"row_s{d}", [NH_A, 4]) for d in range(2)]
        r = Region(stage0)
        keys_t, vals = r("keys_t", [P, NKV_B, 2 * SEQ]), r("vals", [P, 4, NKV_B * HD_B])
        area1 = r.o
        q_c, k_c = r("q_c", [P, NH_A, SEQ]), r("k_c", [P, NH_A, SEQ])
        area2 = r.o
        c0 = r("c0", [P, 2 * NH_A, VA])
        area3 = r.o
        ha = r("ha", [P, 2, D])
        area4 = r.o
        va = r("va", [P, 2, NH_A, VA])
        area5 = r.o
        r = Region(area1)
        ck_nat, ckb_nat, conv_acc_c = r("ck_nat", [P, 2, HALF]), r("ckb_nat", [P, 2, BLK]), r("conv_acc_c", [P, 4, SEQ])
        assert r.o <= area2
        mod_nat_gate = at("mod_nat_gate", [P, D], offset=area1)
        cen, qk_nat = at("cen", [P, 2, D], offset=area3), at("qk_nat", [P, 2, D], offset=area3)
        fin_row = at("fin_row", [P, D], offset=area4)
        r = Region(area5)
        ck_t = r("ck_t", [P, NH_A, SEQ])
        rows_c = at("rows_c", [NH_A, 2, 4, SEQ], offset=area5)
        turn_tmp2 = at("turn_tmp2", [P, 2, SEQ], offset=r.o)
        kw = r("kw", [P, 2, 2, P])
        hn0 = r("hn0", [P, 3, 2 * NKV_B])
        assert r.o <= top2
        r = Region(area5)
        kb_nat = r("kb_nat", [P, 2, NKV_B * HD_B])
        conv_acc_x = at("conv_acc_x", [P, 4, SEQ], offset=r.o)
        rows_of = (rows_c, at("rows_x", [NH_A, 2, 4, SEQ], offset=r.o))
        m_bc, q_in, decay = r("m_bc", [P, 2, SEQ + 1]), r("q_in", [P, 2, SEQ]), r("decay", [P, 2, 2, SEQ])
        squares = r("squares", [P, DV_A])
        assert r.o <= top2, (r.o, top2)
        den = stat[:, 60:64].rearrange("p (a b) -> p a b", a=2)
        qb_nat, sg_a = at("qb_nat", [P, 2, D], offset=area1), at("sg_a", [P, 2, D], offset=area1)
        qb_t, sg_b = at("qb_t", [P, NH_B, SEQ], offset=area2), at("sg_b", [P, 2, D], offset=area2)
        ob = at("ob", [P, 2, D], offset=area4)
        r = Region(area5 + 4 * 2 * NKV_B * HD_B)
        rope_tmp = r("rope_tmp", [P, NH_B, 2, 32])
        hn = r("hn", [P, 3, 2 * NH_B])
        row2 = r("row2", [P, 3, 2 * NH_B])
        assert r.o <= top2
        probs2 = at("probs2", [P, 2, BLK], offset=area5)
        probs2_t = at("probs2_t", [P, 2, BLK], offset=r.o - 4 * 6 * 2 * NH_B - 4 * NH_B * 64)
        gate_row, ln_w_row = at("gate_row", [P, D], offset=stage0), at("ln_w_row", [P, D], offset=stage0 + 4 * D)
        r = Region(area3)
        ln_b_row, diag_g, ones_full = r("ln_b_row", [P, D]), r("diag_g", [P, 4, P]), r("ones_full", [P, P])

        b2_consts, ctx_loaded, fin_loaded, mask_loaded, ln_loaded = (
            sem(n) for n in ("b2_consts", "ctx_loaded", "fin_loaded", "mask_loaded", "ln_loaded"))
        c_loaded, mod_turned, mod_done = sem("c_loaded"), sem("mod_turned"), sem("mod_done")
        c_silu, c_hi, c_lo = sem("c_silu"), sem("c_hi"), sem("c_lo")
        cen_done, fin_sq, fin_ms, fin_root, x1_done = (sem(n) for n in ("cen_done", "fin_sq", "fin_ms", "fin_root", "x1_done"))
        gw_hi, gw_lo = sem("gw_hi"), sem("gw_lo")
        gt_prod, gt_pre, gt_ln, gt_log, gt_rows, gt_exp_in, gt_exp, gt_w, gt_cols, gt_done = (
            sem("gt_" + n) for n in ("prod", "pre", "ln", "log", "rows", "exp_in", "exp", "w", "cols", "done"))
        cv_turned, cv_acc, cv_silu = sem("cv_turned"), sem("cv_acc"), sem("cv_silu")
        ones_set = sem("ones_set")
        ks_turned, ks_scaled, ks_prod, ks_done = (sem("ks_" + n) for n in ("turned", "scaled", "prod", "done"))
        ml_s, ml_m, ml_copy, ml_a, ml_mask, ml_exp, ml_ws, ml_num, ml_out = (
            sem("ml_" + n) for n in ("s", "m", "copy", "a", "mask", "exp", "ws", "num", "out"))
        hn_sq, hn_ms, hn_root, hn_turnable, hn_turned, hn_stored = (
            sem("hn_" + n) for n in ("sq", "ms", "root", "turnable", "turned", "stored"))
        gate_ready = sem("gate_ready")
        a2_scores, a2_max, a2_probs, a2_turned, a2_out, a2_fetched = (
            sem("a2_" + n) for n in ("scores", "max", "probs", "turned", "out", "fetched"))
        a2_copied = sem("a2_copied")
        gr_diag, gr_row, gr_done = sem("gr_diag"), sem("gr_row"), sem("gr_done")
        end_sq, end_ms, end_root, end_done, end_sum = (sem("end_" + n) for n in ("sq", "ms", "root", "done", "sum"))
        hr_sq, hr_ms, hr_root, hr_done = (sem("hr_" + n) for n in ("sq", "ms", "root", "done"))
        M_, A_, S_ = ALU.mult, ALU.add, ALU.subtract

        MOD_TILES = (2 * KT, KT)

        def mod_act(act, use):
            act.wait_ge(b2_consts if use else c_loaded, 16 * N_B2 if use else 16)
            if use == 0:
                act.activation(c_col[:], c_col[:], ACT.Silu).then_inc(c_silu, 1)
                act.wait_ge(c_silu, 1)
            act.wait_ge(w_used, AT["mod_gate" if use else "mod"][0])
            for v in range(4):
                ins = act.activation(act_hi[:, :, 32 * v:32 * v + 32],
                                     c_col[:, v % 2, :].unsqueeze(2).broadcast_to([P, KT, 32]), ACT.Copy)
            ins.then_inc(c_hi, 1)

        def mod_dve(dve, use):
            if use == 0:
                for v in range(2):
                    steps.did(dve.tensor_tensor(pick[:, v:v + 1], ident[:, 32 * v:32 * v + 1],
                                                ident[:, 64 + 32 * v:65 + 32 * v], ALU.add))
            dve.wait_ge(c_hi, use + 1)
            for v in range(2):
                ins = dve.tensor_tensor(act_hi[:, :, 64 + 32 * v:96 + 32 * v],
                                        c_col[:, v, :].unsqueeze(2).broadcast_to([P, KT, 32]),
                                        act_hi[:, :, 32 * v:32 * v + 32].bitcast(F32), ALU.subtract)
            ins.then_inc(c_lo, 1)

        def mod_fetch(act, use):
            def fetch(m, blk, p):
                act.activation((mod_nat, mod_nat_gate)[use][:, bass.ds(blk * BLK, BLK)], acc[:, m, 0, :],
                               ACT.Copy).then_inc(fetched[m], 1)
            return fetch

        def mod_pe(pe, name, use, between=None):
            pe.wait_ge(c_lo, use + 1)
            nch = job(name)[2]

            def body(i, s, c, p):
                for m in range(2):
                    pe.wait_ge(fetched[m], p + 1)
                    for j in range(nch):
                        pe.wait_ge(w_lo_done, c + nch * m + j + 1)
                        slot = (s + nch * m + j) % SLOTS
                        for kk in range(2):
                            k = 2 * j + kk
                            x, o = act_hi[:, k, 0:P], acc[:, m, 0, :]
                            pe.matmul(o, x, w_hi[:, slot, kk * BLK:(kk + 1) * BLK], start=k == 0, stop=False)
                            mm = pe.matmul(o, x, w_lo[:, slot, kk * BLK:(kk + 1) * BLK], start=False, stop=k == KT - 1)
                        mm.then_inc(w_used, 1)
                        if between is not None:
                            between()
            pairs(pe, name, body, between is not None)

        def mod_turn_pe(pe, after, use):
            for m in range(2):
                pe.wait_ge(fetched[m], AT[after][1] + 1)
            src = (mod_nat, mod_nat_gate)[use]
            for t in range(MOD_TILES[use]):
                mm = pe.matmul(pst[:, 0, 2 * t:2 * t + 2], src[:, t * P:(t + 1) * P], pick[:], start=True, stop=True)
            mm.then_inc(mod_turned, 1)

        def mod_col_dve(dve, use):
            dve.wait_ge(mod_turned, use + 1)
            a, n = 2 * KT * use, MOD_TILES[use]
            dve.wait_ge(b2_consts, 16 * N_B2)
            steps.did(dve.tensor_tensor(mod_col[:, a:a + n, :], pst[:, 0, 0:2 * n].rearrange("p (t v) -> p t v", v=2),
                                        b_mod_col[:, a:a + n].unsqueeze(2).broadcast_to([P, n, 2]), ALU.add))
            steps.settle()
            if use == 0:
                steps.did(dve.tensor_scalar(mod_col[:, KT:2 * KT, :], mod_col[:, KT:2 * KT, :], 1.0, None, ALU.add))
                steps.settle()
            dve.sem_inc(mod_done, 1)

        def centre_dve(dve, dst, src):
            steps.did(dve.tensor_reduce(stat[:, 8:10], src[:], X_AXIS, A_))
            steps.settle()
            steps.did(dve.tensor_scalar(stat[:, 10:12], stat[:, 8:10], 1.0 / D, None, M_))
            steps.settle()
            for h in range(2):
                ins = dve.tensor_scalar(dst[:, h, :], src[:, h, :], stat[:, 10 + h:11 + h], None, S_)
            return ins

        def final_norm_act(act):
            act.wait_ge(fetched[1], AT["mod_gate"][1] + 1)
            for h in range(2):
                ins = act.activation(junk_full[:, h, :], resid[:, h, :], ACT.Square, accum_out=stat[:, 12 + h:13 + h])
            ins.then_inc(fin_sq, 1)
            act.wait_ge(fin_ms, 1)
            act.activation(stat[:, 16:18], stat[:, 14:16], ACT.Sqrt).then_inc(fin_root, 1)

        def final_norm_dve(dve):
            dve.wait_ge(fin_sq, 1)
            dve.tensor_scalar(stat[:, 14:16], stat[:, 12:14], 1.0 / D, EPS, M_, A_).then_inc(fin_ms, 1)
            dve.wait_ge(fin_root, 1)
            steps.did(dve.reciprocal(stat[:, 18:20], stat[:, 16:18]))
            steps.settle()
            dve.wait_ge(fin_loaded, 16)
            for h in range(2):
                ins = dve.scalar_tensor_tensor(out=resid[:, h, :], in0=resid[:, h, :], scalar=stat[:, 18 + h:19 + h],
                                               in1=fin_row[:], op0=M_, op1=M_)
            ins.then_inc(x1_done, 1)
            dve.wait_ge(x1_done, 1)

        def gates_pe_product(pe, n_use):
            pe.wait_ge(gw_lo, 1)
            for h in range(2):
                for k in range(KT):
                    xh, xl = act_hi[:, k, h * P:(h + 1) * P], act_lo[:, k, h * P:(h + 1) * P]
                    o = pst[:, 0, h * 32:(h + 1) * 32]
                    pe.matmul(o, xh, gate_w_hi[:, k, :], start=k == 0, stop=False)
                    pe.matmul(o, xh, gate_w_lo[:, k, :], start=False, stop=False)
                    mm = pe.matmul(o, xl, gate_w_hi[:, k, :], start=False, stop=k == KT - 1)
            mm.then_inc(gt_prod, 1)

        def gates_pe_rows(pe, n_use):
            pe.wait_ge(gt_log, n_use + 1)
            for d in range(2):
                for f, src in ((0, gate_pre), (1, gate_log)):
                    for h in range(2):
                        c = 16 * d + 8 * f
                        mm = pe.matmul(pst[0:NH_A, 1 + d, f * SEQ + h * P:f * SEQ + (h + 1) * P],
                                       src[:, h, c:c + NH_A], ident[:], start=True, stop=True)
            mm.then_inc(gt_rows, 1)

        def gates_pe_cols(pe, n_use):
            pe.wait_ge(gt_w, n_use + 1)
            for d in range(2):
                for q, slot in ((0, 3), (1, 1)) if n_use else ((0, 3),):
                    for h in range(2):
                        mm = pe.matmul(pst[:, 3, 32 * q + 16 * h + 8 * d:32 * q + 16 * h + 8 * d + 8],
                                       rows_of[n_use][:, d, slot, h * P:(h + 1) * P], ident[0:NH_A, 0:NH_A],
                                       start=True, stop=True)
            mm.then_inc(gt_cols, 1)

        def gates_act_log(act, n_use):
            act.wait_ge(gt_pre, n_use + 1)
            act.activation(gate_tmp[:], gate_pre[:], ACT.Abs).then_inc(gt_ln, 1)
            act.wait_ge(gt_ln, 3 * n_use + 1)
            act.activation(gate_tmp[:], gate_tmp[:], ACT.Exp, scale=-1.0).then_inc(gt_ln, 1)
            act.wait_ge(gt_ln, 3 * n_use + 2)
            act.activation(gate_tmp[:], gate_tmp[:], ACT.Ln, bias=1.0).then_inc(gt_ln, 1)

        def gates_act_exp(act, n_use):
            act.wait_ge(gt_exp_in, n_use + 1)
            for d in range(2):
                if n_use == 0:
                    ins = act.activation(rows_of[0][:, d, 3, :], rows_of[0][:, d, 1, :], ACT.Exp, bias=row_s[d][:, 1:2])
                else:
                    ins = act.activation(rows_of[1][:, d, 3, :], rows_of[1][:, d, 2, :], ACT.Exp, scale=-1.0)
            ins.then_inc(gt_exp, 1)

        def gates_dve_pre(dve, n_use):
            if n_use == 0:
                dve.memset(ones_row[:], 1.0).then_inc(ones_set, 1)
                dve.wait_ge(ones_set, 1)
            dve.wait_ge(gt_prod, n_use + 1)
            dve.tensor_tensor(gate_pre[:], pst[:, 0, 0:64].rearrange("p (h c) -> p h c", h=2),
                              b_if_row[:].unsqueeze(1).broadcast_to([P, 2, 32]), A_).then_inc(gt_pre, 1)

        def gates_dve_log(dve, n_use):
            dve.wait_ge(gt_ln, 3 * n_use + 3)
            dve.wait_ge(gt_pre, n_use + 1)
            dve.scalar_tensor_tensor(out=gate_log[:], in0=gate_pre[:], scalar=0.0, in1=gate_tmp[:],
                                     op0=ALU.min, op1=S_).then_inc(gt_log, 1)

        def run(x, d):
            return x if d == 0 else x[:, ::-1]

        def gates_dve_scan(dve, n_use):
            rw = rows_of[n_use]
            dve.wait_ge(gt_rows, n_use + 1)
            for d in range(2):
                f_row = pst[0:NH_A, 1 + d, SEQ:2 * SEQ]
                steps.did(dve.tensor_tensor_scan(run(rw[:, d, 0, :], d), run(ones_row[:], d), run(f_row, d), 0.0, M_, A_))
            steps.settle()
            for d in range(2):
                steps.did(dve.tensor_tensor(rw[:, d, 1, :], pst[0:NH_A, 1 + d, 0:SEQ], rw[:, d, 0, :], S_))
            steps.settle()
            if n_use == 0:
                for d in range(2):
                    steps.did(dve.tensor_reduce(row_s[d][:, 0:1], rw[:, d, 1, :], X_AXIS, ALU.max))
                steps.settle()
                for d in range(2):
                    last = 0 if d else SEQ - 1
                    steps.did(dve.tensor_tensor(row_s[d][:, 2:3], row_s[d][:, 0:1], rw[:, d, 0, last:last + 1], A_))
                    ins = dve.tensor_scalar(row_s[d][:, 1:2], row_s[d][:, 0:1], -1.0, None, M_)
                ins.then_inc(gt_exp_in, 1)
                dve.wait_ge(gt_exp, 1)
                for d in range(2):
                    ins = dve.tensor_scalar(rw[:, d, 3, :], rw[:, d, 3, :], DK_A ** -0.5, None, M_)
                ins.then_inc(gt_w, 1)
            else:
                for d in range(2):
                    steps.did(dve.tensor_copy(m_rows[d][:, SEQ:SEQ + 1], row_s[d][:, 2:3]))
                    steps.did(dve.tensor_tensor_scan(run(m_rows[d][:, 0:SEQ], d), run(ones_row[:], d),
                                                     run(rw[:, d, 1, :], d), row_s[d][:, 2:3], M_, ALU.max))
                steps.settle()
                for d in range(2):
                    ins = dve.tensor_tensor(rw[:, d, 2, :], rw[:, d, 0, :], m_rows[d][:, 0:SEQ], A_)
                ins.then_inc(gt_exp_in, 1)
                dve.wait_ge(gt_exp, 2)
                dve.sem_inc(gt_w, 1)

        def gates_dve_cols(dve, n_use):
            dve.wait_ge(gt_cols, n_use + 1)
            if n_use == 0:
                dve.tensor_copy(w_col[:].rearrange("p h d n -> p (h d n)"), pst[:, 3, 0:32]).then_inc(gt_done, 1)
            else:
                dve.tensor_copy(e_col[:].rearrange("p h d n -> p (h d n)"), pst[:, 3, 0:32])
                dve.tensor_copy(g_col[:].rearrange("p h d n -> p (h d n)"), pst[:, 3, 32:64]).then_inc(gt_done, 1)

        CONVS = ((NH_A, conv_acc_c, 2), (0, conv_acc_x, 4))

        def conv_step_pe(pe, use, g):
            n = 2 * use + g
            if n:
                pe.wait_ge(cv_acc, n)
            src = (ck_nat, qk_nat)[use]
            for t in range(4):
                for h in range(2):
                    c = (4 * g + t) * P
                    mm = pe.transpose(pst[:, t, h * P:(h + 1) * P], src[:, h, c:c + P], ident[:])
            mm.then_inc(cv_turned, 1)

        def conv_step_dve(dve, use, g):
            w0, conv_acc, _ = CONVS[use]
            n = 2 * use + g
            dve.wait_ge(cv_turned, n + 1)
            if n:
                dve.wait_ge(cv_silu, n)
            for tap in range(3):
                for t in range(4):
                    k = w0 + 4 * g + t
                    ps, w = pst[:, t, 0:SEQ], conv_w[:, k, :]
                    if tap == 0:
                        ins = dve.tensor_scalar(conv_acc[:, t, :], ps, w[:, 1:2], conv_b[:, k:k + 1], M_, A_)
                    elif tap == 1:
                        o = conv_acc[:, t, 1:SEQ]
                        ins = dve.scalar_tensor_tensor(out=o, in0=ps[:, 0:SEQ - 1], scalar=w[:, 0:1], in1=o, op0=M_, op1=A_)
                    else:
                        o = conv_acc[:, t, 0:SEQ - 1]
                        ins = dve.scalar_tensor_tensor(out=o, in0=ps[:, 1:SEQ], scalar=w[:, 2:3], in1=o, op0=M_, op1=A_)
                if tap < 2:
                    steps.did(ins)
                    steps.settle()
            ins.then_inc(cv_acc, 1)

        def conv_step_act(act, use, g):
            act.wait_ge(cv_acc, 2 * use + g + 1)
            dst = (ck_t, ck_t, q_c, k_c)[2 * use + g // 2][:, 4 * (g % 2):4 * (g % 2) + 4, :]
            act.activation(dst, CONVS[use][1][:], ACT.Silu).then_inc(cv_silu, 1)

        def state_step_pe(pe, s):
            if s == 0:
                pe.wait_ge(cv_silu, 2)
            if s < NH_A:
                if s >= 2:
                    pe.wait_ge(ks_scaled, s - 1)
                for h in range(2):
                    mm = pe.transpose(pst[:, s % 2, h * P:(h + 1) * P], ck_t[:, s, h * P:(h + 1) * P], ident[:])
                mm.then_inc(ks_turned, 1)
            if s >= 1:
                n = s - 1
                pe.wait_ge(ks_scaled, n + 1)
                if n >= 1:
                    pe.wait_ge(ks_done, n)
                for d in range(2):
                    for h in range(2):
                        mm = pe.matmul(pst[:, 2 + d, 0:VA], kw[:, d, h, :], va[:, h, n, :], start=h == 0, stop=h == 1)
                mm.then_inc(ks_prod, 1)

        def state_step_act(act, s):
            if s < NH_A:
                act.wait_ge(ks_turned, s + 1)
                if s >= 1:
                    act.wait_ge(ks_prod, s)
                for d in range(2):
                    for h in range(2):
                        ins = act.activation(kw[:, d, h, :], pst[:, s % 2, h * P:(h + 1) * P], ACT.Copy,
                                             scale=w_col[:, h, d, s:s + 1])
                ins.then_inc(ks_scaled, 1)

        def state_step_dve(dve, s):
            if s >= 1:
                dve.wait_ge(ks_prod, s)
                dve.tensor_copy(c0[:, 2 * s - 2:2 * s, :], pst[:, 2:4, 0:VA]).then_inc(ks_done, 1)

        CTX_STEPS = 2 + NH_A + 1 + 1

        def ctx_step_pe(pe, s):
            if s < 2:
                conv_step_pe(pe, 0, s)
            elif s < CTX_STEPS - 1:
                if s == 2:
                    pe.wait_ge(cv_acc, 2)
                state_step_pe(pe, s - 2)
            else:
                for b in range(NKV_B // 2):
                    qk_turn_pe(pe, 0, b)

        def ctx_step_act(act, s):
            if s < 2:
                conv_step_act(act, 0, s)
            elif s < CTX_STEPS - 1:
                state_step_act(act, s - 2)
            else:
                for h in range(2):
                    qk_root_act(act, 0, h)
                for b in range(NKV_B // 2):
                    qk_store_act(act, 0, b)

        def ctx_step_dve(dve, s):
            if s < 2:
                conv_step_dve(dve, 0, s)
            elif s < CTX_STEPS - 1:
                state_step_dve(dve, s - 2)
            else:
                for h in range(2):
                    for part in range(QK_PARTS):
                        qk_part_dve(dve, 0, h, part)

        XV_STEPS = 6

        def xv_step_pe(pe, s):
            if s < 4:
                conv_step_pe(pe, 1, s)
            elif s == 4:
                pe.wait_ge(cv_acc, 6)
                gates_pe_rows(pe, 1)
            else:
                gates_pe_cols(pe, 1)

        def xv_step_act(act, s):
            if s < 4:
                conv_step_act(act, 1, s)
            elif s == 4:
                gates_act_exp(act, 1)

        def xv_step_dve(dve, s):
            if s < 4:
                conv_step_dve(dve, 1, s)
            elif s == 4:
                dve.wait_ge(cv_silu, 6)
                gates_dve_scan(dve, 1)
            else:
                gates_dve_cols(dve, 1)

        NU = 2 * NH_A

        MLSTM_STEPS = NU + 4

        def mlstm_step_pe(pe, s):
            if s == 0:
                pe.wait_ge(gt_done, 2)
                pe.wait_ge(cv_silu, 6)
            if s < NU and s % 2 == 1:
                head = s // 2
                if s >= 2:
                    pe.wait_ge(ml_ws, s - 1)
                for st in range(2):
                    mm = pe.matmul(pst[:, 0, st * SEQ:(st + 1) * SEQ],
                                   k_c[:, head, st * P:(st + 1) * P], q_c[:, head, :], start=True, stop=True)
                mm.then_inc(ml_s, 1)
            if s < NU:
                if s >= 1:
                    pe.wait_ge(ml_copy, s)
                pe.matmul(pst[:, 1, 0:SEQ + 1], ident[0:NH_A, s // 2:s // 2 + 1].broadcast_to([NH_A, P]),
                          m_rows[s % 2][:], start=True, stop=True).then_inc(ml_m, 1)
            n = s - 2
            if 0 <= n < NU:
                head, d = n // 2, n % 2
                pe.wait_ge(ml_ws, n + 1)
                if n >= 1:
                    pe.wait_ge(ml_out, n)
                for th in range(2):
                    o = pst[:, 2 + th, 0:VA]
                    for j, st in enumerate([0, 1] if th != d else [th]):
                        pe.matmul(o, decay[:, n % 2, st, th * P:(th + 1) * P], va[:, st, head, :],
                                  start=j == 0, stop=False)
                    mm = pe.matmul(o, q_in[:, n % 2, th * P:(th + 1) * P], c0[:, n, :], start=False, stop=True)
                mm.then_inc(ml_num, 1)

        def mlstm_step_act(act, s):
            if s < NU:
                act.wait_ge(ml_m, s + 1)
                if s >= 2:
                    act.wait_ge(ml_mask, s - 1)
                    act.wait_ge(ml_a, s - 1)
                act.activation(m_bc[:, s % 2, :], pst[:, 1, 0:SEQ + 1], ACT.Copy).then_inc(ml_copy, 1)
                act.wait_ge(ml_copy, s + 1)
                if s >= 2:
                    act.wait_ge(ml_num, s - 1)
                act.activation(q_in[:, s % 2, :], m_bc[:, s % 2, 0:SEQ], ACT.Exp, scale=-1.0,
                               bias=m_bc[:, s % 2, SEQ:SEQ + 1]).then_inc(ml_a, 1)
            if 1 <= s <= NU:
                n = s - 1
                act.wait_ge(ml_mask, n + 1)
                for st in range(2):
                    o = decay[:, n % 2, st, :]
                    ins = act.activation(o, o, ACT.Exp, bias=g_col[:, st, n % 2, n // 2:n // 2 + 1])
                ins.then_inc(ml_exp, 1)
            if s >= 5 and s % 2 == 1:
                head = (s - 5) // 2
                act.wait_ge(ml_out, 2 * head + 2)
                for h in range(2):
                    act.activation(squares[:], ha[:, h, head * DV_A:(head + 1) * DV_A], ACT.Square,
                                   accum_out=stat[:, 20 + 8 * h + head:21 + 8 * h + head]).then_inc(hr_sq, 1)
                    act.wait_ge(hr_sq, 2 * head + h + 1)

        def mlstm_step_dve(dve, s):
            if s == 0:
                dve.wait_ge(mask_loaded, 16)
            n = s - 3
            if 0 <= n < NU:
                head, d = n // 2, n % 2
                dve.wait_ge(ml_num, n + 1)
                if n >= 1:
                    dve.wait_ge(ml_out, n)
                total = pst[:, 2:4, VA - 1]
                steps.did(dve.scalar_tensor_tensor(out=den[:, 0, :], in0=total, scalar=-1.0,
                                                   in1=e_col[:, :, d, head], op0=M_, op1=ALU.max))
                steps.settle()
                steps.did(dve.tensor_tensor(den[:, 0, :], total, den[:, 0, :], ALU.max))
                steps.settle()
                steps.did(dve.reciprocal(den[:, 1, :], den[:, 0, :]))
                steps.settle()
                for th in range(2):
                    o = ha[:, th, head * DV_A:(head + 1) * DV_A]
                    x = pst[:, 2 + th, 0:DV_A]
                    if d == 0:
                        ins = dve.tensor_scalar(o, x, den[:, 1, th:th + 1], None, M_)
                    else:
                        ins = dve.scalar_tensor_tensor(out=o, in0=x, scalar=den[:, 1, th:th + 1], in1=o, op0=M_, op1=A_)
                ins.then_inc(ml_out, 1)
            if s < NU:
                dve.wait_ge(ml_copy, s + 1)
                if s >= 2:
                    dve.wait_ge(ml_num, s - 1)
                dve.tensor_tensor(decay[:, s % 2, :, :], neg_mask[:, s % 2, :, :],
                                  m_bc[:, s % 2, 0:SEQ].unsqueeze(1).broadcast_to([P, 2, SEQ]), S_).then_inc(ml_mask, 1)
            if 1 <= s <= NU:
                n = s - 1
                dve.wait_ge(ml_a, n + 1)
                dve.wait_ge(ml_s, n // 2 + 1)
                dve.tensor_tensor(q_in[:, n % 2, :], q_in[:, n % 2, :], q_c[:, n // 2, :], M_)
                dve.wait_ge(ml_exp, n + 1)
                o = decay[:, n % 2, :, :]
                dve.scalar_tensor_tensor(out=o, in0=pst[:, 0, :].rearrange("p (a t) -> p a t", a=2),
                                         scalar=DK_A ** -0.5, in1=o, op0=M_, op1=M_).then_inc(ml_ws, 1)

        def head_norm_act(act):
            act.wait_ge(hr_ms, 1)
            act.activation(stat[:, 36:52], stat[:, 36:52], ACT.Sqrt).then_inc(hr_root, 1)

        def head_norm_dve(dve):
            dve.wait_ge(hr_sq, 2 * NH_A)
            dve.tensor_scalar(stat[:, 36:52], stat[:, 20:36], 1.0 / DV_A, EPS, M_, A_).then_inc(hr_ms, 1)
            dve.wait_ge(hr_root, 1)
            steps.did(dve.reciprocal(stat[:, 36:52], stat[:, 36:52]))
            steps.settle()

        def gated_act(act, func, base):
            def fetch(m, blk, p):
                act.activation(acc[:, m, :, :], acc[:, m, :, :], func).then_inc(gate_ready, 1)
            return fetch

        def gated_dve(dve, dst, base, kind=None):
            def fetch(m, blk, p):
                dve.wait_ge(gate_ready, blk + (base + 1))
                o = dst[:, :, bass.ds(blk * BLK, BLK)]
                if kind == "o":
                    dve.wait_ge(hr_sq, 4 * (blk + 1))
                if kind == "z":
                    for n in range(2 * blk, 2 * blk + 2):
                        for h in range(2):
                            o = dst[:, h, n * DV_A:(n + 1) * DV_A]
                            c = (n % 2) * DV_A
                            ins = dve.scalar_tensor_tensor(out=o, in0=o, scalar=stat[:, 36 + 8 * h + n:37 + 8 * h + n],
                                                           in1=acc[:, m, h, c:c + DV_A], op0=M_, op1=M_)
                else:
                    ins = dve.tensor_tensor(o, o, acc[:, m, :, :], M_)
                ins.then_inc(fetched[m], 1)
            return fetch

        QK_PARTS = 6

        def qk_norm(use):
            src, gain, n = ((ckb_nat, k_gain, NKV_B), (kb_nat, k_gain, NKV_B), (qb_nat, q_gain, NH_B))[use]
            return src, gain, n, ob if use else ckb_nat, hn if use else hn0

        def qk_root_act(act, use, h):
            n, hs = qk_norm(use)[2], qk_norm(use)[4]
            act.wait_ge(hn_ms, 2 * use + h + 1)
            act.activation(hs[:, 1, h * n:(h + 1) * n], hs[:, 0, h * n:(h + 1) * n], ACT.Sqrt).then_inc(hn_root, 1)

        def qk_part_dve(dve, use, h, part):
            src, gain, n, dst, hs = qk_norm(use)
            x = src[:, h, :].rearrange("p (n e) -> p n e", e=HD_B)
            y = (ob if use else ck_nat)[:, h, 0:n * HD_B]
            sums, roots, scales = (hs[:, v, h * n:(h + 1) * n] for v in range(3))
            if part == 0:
                for m in range(2):
                    dve.wait_ge(fetched[m], AT[("x_qk", "x_o", "x_z")[use]][1] + 1)
                if use == 2:
                    dve.wait_ge(hn_turned, TURN_BANKS[2])
                steps.did(dve.tensor_tensor(y, src[:, h, :], src[:, h, :], M_))
                steps.settle()
            elif part == 1:
                steps.did(dve.tensor_reduce(sums, y.rearrange("p (n e) -> p n e", e=HD_B), X_AXIS, A_))
                steps.settle()
                dve.tensor_scalar(sums, sums, 1.0 / HD_B, EPS, M_, A_).then_inc(hn_ms, 1)
            elif part == 2:
                dve.wait_ge(hn_root, 2 * use + h + 1)
                steps.did(dve.reciprocal(scales, roots))
                steps.settle()
                steps.did(dve.tensor_tensor(x, x, scales.unsqueeze(2).broadcast_to([P, n, HD_B]), M_))
                steps.settle()
            elif part == 3:
                steps.did(dve.tensor_tensor(x, x, gain[:].unsqueeze(1).broadcast_to([P, n, HD_B]), M_))
                steps.settle()
            elif use:
                xv = src[:, h, :].rearrange("p (n r s e) -> p n r s e", r=2, s=2, e=32)
                yv = ob[:, h, 0:n * HD_B].rearrange("p (n r s e) -> p n r s e", r=2, s=2, e=32)
                x1, x2, y1, y2 = xv[:, :, :, 0, :], xv[:, :, :, 1, :], yv[:, :, :, 0, :], yv[:, :, :, 1, :]
                shape = [P, n, 2, 32]
                co = rope[:, 0, h, :, :].unsqueeze(1).broadcast_to(shape)
                si = rope[:, 1, h, :, :].unsqueeze(1).broadcast_to(shape)
                t = rope_tmp[:, 0:n, :, :]
                a, b, o, op = (co, si, y1, S_) if part == 4 else (si, co, y2, A_)
                steps.did(dve.tensor_tensor(o, x1, a, M_))
                steps.did(dve.tensor_tensor(t, x2, b, M_))
                steps.settle()
                steps.did(dve.tensor_tensor(o, o, t, op))
                steps.settle()
            if part == 5:
                dve.sem_inc(hn_turnable, 1)

        TURN_BANKS = (0, 2, 4, 12)

        def qk_turn_pe(pe, use, b):
            dst = qk_norm(use)[3]
            pe.wait_ge(hn_turnable, 2 * use + 2)
            done = TURN_BANKS[use] + b
            if done >= 2:
                pe.wait_ge(hn_stored, done - 1)
            for t in range(2):
                for h in range(2):
                    mm = pe.transpose(pst[:, done % 2, t * SEQ + h * P:t * SEQ + (h + 1) * P],
                                      dst[:, h, (2 * b + t) * HD_B:(2 * b + t + 1) * HD_B], ident[:])
            mm.then_inc(hn_turned, 1)

        def qk_store_act(act, use, b):
            done = TURN_BANKS[use] + b
            act.wait_ge(hn_turned, done + 1)
            x = pst[:, done % 2, :].rearrange("p (t s) -> p t s", t=2)
            o = qb_t[:, 2 * b:2 * b + 2, :] if use == 2 else keys_t[:, 2 * b:2 * b + 2, use * SEQ:(use + 1) * SEQ]
            act.activation(o, x, ACT.Copy).then_inc(hn_stored, 1)

        XZ_STEPS = 2 + 2 * QK_PARTS + NH_B // 2

        def xz_step_pe(pe, s):
            if s == 2:
                for b in range(NKV_B // 2):
                    qk_turn_pe(pe, 1, b)
            elif s >= 2 + 2 * QK_PARTS:
                qk_turn_pe(pe, 2, s - 2 - 2 * QK_PARTS)

        def xz_step_act(act, s):
            if s < 2:
                qk_root_act(act, 1, s)
            elif s >= 2 + 2 * QK_PARTS:
                qk_store_act(act, 2, s - 2 - 2 * QK_PARTS)
            else:
                if s == 2:
                    for b in range(NKV_B // 2):
                        qk_store_act(act, 1, b)
                if (s - 2) % QK_PARTS == 1:
                    qk_root_act(act, 2, (s - 2) // QK_PARTS)

        def xz_step_dve(dve, s):
            if s < 2:
                for part in range(QK_PARTS):
                    qk_part_dve(dve, 1, s, part)
            elif s < 2 + 2 * QK_PARTS:
                qk_part_dve(dve, 2, (s - 2) // QK_PARTS, (s - 2) % QK_PARTS)

        NQ = 2 * NH_B
        SCALE_B = HD_B ** -0.5
        ATT2_STEPS = NQ + 4

        def attention2_step_pe(pe, s):
            if s == 0:
                pe.wait_ge(hn_stored, TURN_BANKS[3])
            if s < NQ:
                if s >= 2:
                    pe.wait_ge(a2_probs, s - 1)
                head, h = s // 2, s % 2
                pe.matmul(pst[:, s % 2, :], qb_t[:, head, h * P:(h + 1) * P], keys_t[:, head // 4, :],
                          start=True, stop=True).then_inc(a2_scores, 1)
            u = s - 2
            if 0 <= u < NQ:
                pe.wait_ge(a2_probs, u + 1)
                if u >= 1:
                    pe.wait_ge(a2_copied, u)
                for b in range(4):
                    mm = pe.transpose(pst[:, 2, b * P:(b + 1) * P], probs2[:, u % 2, b * P:(b + 1) * P], ident[:])
                mm.then_inc(a2_turned, 1)
            u = s - 3
            if 0 <= u < NQ:
                head = u // 2
                pe.wait_ge(a2_copied, u + 1)
                if u >= 1:
                    pe.wait_ge(a2_fetched, u)
                kv = head // 4
                for b in range(4):
                    mm = pe.matmul(pst[:, 3, 0:HD_B], probs2_t[:, u % 2, b * P:(b + 1) * P],
                                   vals[:, b, kv * HD_B:(kv + 1) * HD_B], start=b == 0, stop=b == 3)
                mm.then_inc(a2_out, 1)

        def attention2_step_act(act, s):
            u = s - 1
            if 0 <= u < NQ:
                act.wait_ge(a2_max, u + 1)
                if u >= 2:
                    act.wait_ge(a2_turned, u - 1)
                act.activation(probs2[:, u % 2, :], pst[:, u % 2, :], ACT.Exp, scale=SCALE_B,
                               bias=row2[:, 0, u:u + 1], accum_out=row2[:, 1, u:u + 1]).then_inc(a2_probs, 1)
            u = s - 2
            if 0 <= u < NQ:
                act.wait_ge(a2_turned, u + 1)
                if u >= 2:
                    act.wait_ge(a2_out, u - 1)
                act.activation(probs2_t[:, u % 2, :], pst[:, 2, :], ACT.Copy).then_inc(a2_copied, 1)

        def attention2_step_dve(dve, s):
            u = s - 4
            if 0 <= u < NQ:
                head, h = u // 2, u % 2
                dve.wait_ge(a2_out, u + 1)
                steps.did(dve.reciprocal(row2[:, 2, u:u + 1], row2[:, 1, u:u + 1]))
                steps.settle()
                dve.tensor_scalar(ob[:, h, head * HD_B:(head + 1) * HD_B], pst[:, 3, 0:HD_B],
                                  row2[:, 2, u:u + 1], None, M_).then_inc(a2_fetched, 1)
            if s < NQ:
                dve.wait_ge(a2_scores, s + 1)
                steps.did(dve.tensor_reduce(row2[:, 2, s:s + 1], pst[:, s % 2, :], X_AXIS, ALU.max))
                steps.settle()
                dve.tensor_scalar(row2[:, 0, s:s + 1], row2[:, 2, s:s + 1], -SCALE_B, None, M_).then_inc(a2_max, 1)

        def sg_fetch(act, sg):
            def fetch(m, blk, p):
                act.activation(sg[:, :, bass.ds(blk * BLK, BLK)], acc[:, m, :, :], ACT.Sigmoid).then_inc(fetched[m], 1)
            return fetch

        def ba_fetch(dve):
            def fetch(m, blk, p):
                o = sg_a[:, :, bass.ds(blk * BLK, BLK)]
                dve.tensor_tensor(o, o, acc[:, m, :, :], M_).then_inc(fetched[m], 1)
            return fetch

        bb_prod = sem("bb_prod")

        def bb_fetch(dve):
            def fetch(m, blk, p):
                o, g = (x[:, :, bass.ds(blk * BLK, BLK)] for x in (sg_a, sg_b))
                dve.tensor_tensor(g, g, acc[:, m, :, :], M_).then_inc(bb_prod, 1)
                dve.wait_ge(bb_prod, blk + 1)
                dve.tensor_tensor(o, o, g, A_).then_inc(fetched[m], 1)
            return fetch

        def gate_row_dve(dve):
            dve.wait_ge(nt_turned, turns["ob"][0] + 16)
            dve.memset(ones_full[:], 1.0)
            for g in range(4):
                if g:
                    dve.wait_ge(gr_row, g)
                for t in range(4):
                    ins = dve.tensor_scalar(diag_g[:, t, :], ident[:], mod_col[:, 2 * KT + 4 * g + t, 0:1], None, M_)
                ins.then_inc(gr_diag, 1)
                dve.wait_ge(gr_row, g + 1)
                ins = dve.tensor_copy(gate_row[:, g * BLK:(g + 1) * BLK], pst[:, g % 2, :])
                ins.then_inc(gr_done, 1)

        def gate_row_pe(pe):
            for g in range(4):
                pe.wait_ge(gr_diag, g + 1)
                if g >= 2:
                    pe.wait_ge(gr_done, g - 1)
                for t in range(4):
                    mm = pe.matmul(pst[:, g % 2, t * P:(t + 1) * P], ones_full[:], diag_g[:, t, :], start=True, stop=True)
                mm.then_inc(gr_row, 1)


        wo_prod = sem("wo_prod")

        def wo_fetch(dve):
            def fetch(m, blk, p):
                t = sg_b[:, :, bass.ds(blk * BLK, BLK)]
                o = resid[:, :, bass.ds(blk * BLK, BLK)]
                g = gate_row[:, bass.ds(blk * BLK, BLK)].unsqueeze(1).broadcast_to([P, 2, BLK])
                dve.tensor_tensor(t, acc[:, m, :, :], g, M_).then_inc(wo_prod, 1)
                dve.wait_ge(wo_prod, blk + 1)
                dve.scalar_tensor_tensor(out=o, in0=o, scalar=ALPHA, in1=t, op0=M_, op1=A_).then_inc(fetched[m], 1)
            return fetch

        def end_act(act):
            act.wait_ge(end_sum, 1)
            for h in range(2):
                ins = act.activation(junk_full[:, h, :], resid[:, h, :], ACT.Square, accum_out=stat[:, 52 + h:53 + h])
            ins.then_inc(end_sq, 1)
            act.wait_ge(end_ms, 1)
            act.activation(stat[:, 56:58], stat[:, 54:56], ACT.Sqrt).then_inc(end_root, 1)

        def end_dve(dve):
            for m in range(2):
                dve.wait_ge(fetched[m], AT["end"][1] + 1)
            centre_dve(dve, resid, resid).then_inc(end_sum, 1)
            dve.wait_ge(end_sq, 1)
            dve.tensor_scalar(stat[:, 54:56], stat[:, 52:54], 1.0 / D, EPS, M_, A_).then_inc(end_ms, 1)
            dve.wait_ge(end_root, 1)
            steps.did(dve.reciprocal(stat[:, 58:60], stat[:, 56:58]))
            steps.settle()
            dve.wait_ge(ln_loaded, 32)
            for h in range(2):
                steps.did(dve.scalar_tensor_tensor(out=resid[:, h, :], in0=resid[:, h, :], scalar=stat[:, 58 + h:59 + h],
                                                   in1=ln_w_row[:], op0=M_, op1=M_))
                steps.settle()
                dve.tensor_tensor(resid[:, h, :], resid[:, h, :], ln_b_row[:], A_).then_inc(end_done, 1)

        B2_LOADS = ((gate_w[:], "gate_w"), (b_mod_col[:], "b_mod_col"), (conv_w[:], "conv_w"),
                    (conv_b[:], "conv_b"), (mh_col[:], "mh_col"), (rope[:], "rope"))
        B2_ROWS = ((b_if_row[:], "b_if_2"), (q_gain[:], "q_norm_w_2"), (k_gain[:], "k_norm_w_2"))
        N_B2 = len(B2_LOADS) + len(B2_ROWS)

        block = ctx.enter_context(nc.Block())

        @block.sync
        def _(sp):
            sp.dma_start(resid[:], A["x"].rearrange("(h p) d -> p h d", p=P)).then_inc(x_ready, 16)
            sp.dma_start(ident[:], A["ident"]).then_inc(consts_ready, 16)
            sp.dma_start(gains[:].rearrange("p a k -> p (a k)"), A["gains"]).then_inc(consts_ready, 16)
            ffn_sp(sp, "ffn1", A["ffn1_w_gate"], A["ffn1_w_up"], A["ffn1_w_down"])
            stream_sp(sp, "w_u", A["w_in"], 3 * HALF)
            stream_sp(sp, "w_qkv", A["w_in"], 0)
            stream_sp(sp, "mod", A["w_mod_2"], 0)
            stream_sp(sp, "glu", A["ssm_w_glu"], 0)
            stream_sp(sp, "w_out", A["w_out"], 0)
            ffn_sp(sp, "ffn2", A["ffn2_w_gate"], A["ffn2_w_up"], A["ffn2_w_down"])
            win2 = A["w_in_2"]
            stream_sp(sp, "mod_gate", A["w_mod_2"], 2 * D)
            for name, col in (("ctx_k", DK_A * NH_A), ("ctx_v", 2 * DK_A * NH_A), ("ctx_kv", KB0), ("x_qk", 0),
                              ("x_v", 2 * DK_A * NH_A), ("x_kv", KB0)) + tuple(
                    (n, KB0 + BLK * b) for n, b in (("x_o", 2), ("x_q", 10), ("x_z", 6), ("x_ga", 18), ("x_zb", 14), ("x_gb", 22))):
                stream_sp(sp, name, win2, col)
            stream_sp(sp, "ba", A["w_branch_a_2"], 0)
            stream_sp(sp, "bb", A["w_branch_b_2"], 0)
            stream_sp(sp, "wo", A["w_out_2"], 0)
            for h in range(2):
                sp.wait_ge(end_done, h + 1)
                sp.dma_start(out.rearrange("(h p) d -> p h d", p=P)[:, h, :], resid[:, h, :]).then_inc(out_done, 16)
            sp.wait_ge(out_done, 32)

        @block.scalar
        def _(act):
            for j in range(LEAD):
                round_chunk(act, j)
            ssm_params_act(act, 0)
            act.wait_ge(x_ready, 16)
            act.wait_ge(consts_ready, 32)
            turn_act(act, "ffn1", resid, gains[:, 0, :], junk=junk_full)
            ssm_params_act(act, 1)
            ffn_act(act, "ffn1", 0)
            act.wait_ge(fetched[1], AT["w_u"][1] + 1)
            turn_act(act, "mix", resid, gains[:, 1, :], junk=junk_full)
            stream_split(act, "w_u", fetch_prj(act, 6))
            turn_qku_fetch(act, 0, 0, 4, lambda o, i: act.activation(o, i, ACT.Copy))
            stream_split(act, "w_qkv", fetch_prj(act, 0), unrolled=True)
            ssm_act(act)
            turn_qku_fetch(act, 0, 4, 12, lambda o, i: act.activation(o, i, ACT.Copy))
            mod_act(act, 0)
            stream_split(act, "mod", mod_fetch(act, 0), between=spread(attention1_step_act, act, N_HEADS1 + 2, "mod"))
            turn_act(act, "y", ssm_y)
            stream_split(act, "glu")
            glu_act(act)
            act.wait_ge(glu_out, 2)
            turn_act(act, "ssm", ssm_y, gains[:, 2, 0:8], junk=junk_low)
            turn_act(act, "att", att, gains[:, 2, 8:16], junk=junk_high, dst=8)
            stream_split(act, "w_out")
            act.wait_ge(fetched[1], AT["ffn2"][1] + 1)
            turn_act(act, "ffn2", resid, gains[:, 3, :], junk=junk_full)
            ffn_act(act, "ffn2", 1)
            final_norm_act(act)
            mod_act(act, 1)
            act.activation(gate_w_hi[:], gate_w[:], ACT.Copy).then_inc(gw_hi, 1)
            stream_split(act, "mod_gate", mod_fetch(act, 1))
            act.wait_ge(cen_done, 1)
            act.wait_ge(mod_done, 2)
            turn_act(act, "u_ctx", cen, mod_col[:, KT:2 * KT, 1], junk=junk_full, bias=mod_col[:, 0:KT, 1])

            def store(place):
                def fetch(m, blk, p):
                    act.activation(place(blk), acc[:, m, :, :], ACT.Copy).then_inc(fetched[m], 1)
                return fetch

            def store_values(dst):
                def fetch(m, blk, p):
                    act.activation(dst[:, :, bass.ds(blk * 2, 2), 0:DV_A],
                                   acc[:, m, :, :].rearrange("p h (n v) -> p h n v", v=DV_A), ACT.Copy).then_inc(fetched[m], 1)
                return fetch
            stream_split(act, "ctx_k", store(lambda blk: ck_nat[:, :, blk * BLK:(blk + 1) * BLK]))
            gates_act_log(act, 0)
            stream_split(act, "ctx_v", store_values(va))
            gates_act_exp(act, 0)
            stream_split(act, "ctx_kv", store(lambda blk: vals[:, 0:2, :] if blk else ckb_nat[:]))
            act.wait_ge(cen_done, 2)
            turn_act(act, "u_x", cen, mod_col[:, KT:2 * KT, 0], junk=junk_full, bias=mod_col[:, 0:KT, 0])
            stream_split(act, "x_qk", store(lambda blk: qk_nat[:, :, blk * BLK:(blk + 1) * BLK]),
                         spread(ctx_step_act, act, CTX_STEPS, "x_qk"))
            gates_act_log(act, 1)
            act.wait_ge(ks_prod, NH_A)
            stream_split(act, "x_v", store_values(va), spread(xv_step_act, act, XV_STEPS, "x_v"))
            between = spread(mlstm_step_act, act, MLSTM_STEPS, "x_kv", "x_o")
            stream_split(act, "x_kv", store(lambda blk: vals[:, 2:4, :] if blk else kb_nat[:]), between)
            stream_split(act, "x_o", gated_act(act, ACT.Sigmoid, 0), between)
            head_norm_act(act)
            stream_split(act, "x_q", store(lambda blk: qb_nat[:, :, bass.ds(blk * BLK, BLK)]))
            stream_split(act, "x_z", gated_act(act, ACT.Silu, 4), spread(xz_step_act, act, XZ_STEPS, "x_z"))
            stream_split(act, "x_ga", sg_fetch(act, sg_a), spread(attention2_step_act, act, ATT2_STEPS, "x_ga"))
            stream_split(act, "x_zb", gated_act(act, ACT.Silu, 8))
            stream_split(act, "x_gb", sg_fetch(act, sg_b))
            turn_act(act, "ha", ha, mh_col)
            stream_split(act, "ba")
            turn_act(act, "ob", ob)
            stream_split(act, "bb")
            turn_act(act, "merge", sg_a)
            stream_split(act, "wo")
            end_act(act)

        @block.vector
        def _(dve):
            nonlocal steps
            steps = Steps(dve, dve_steps)
            dve.sem_inc(fetched[0], 1)
            dve.sem_inc(fetched[1], 1)
            dve.sem_inc(g_lo_done, 1)
            for j in range(LEAD):
                rest_chunk(dve, j)
            dve.wait_ge(consts_ready, 32)
            turn_dve(dve, "ffn1", gains[:, 0, :])
            dve.wait_ge(sp_ready, 2)
            dve.reciprocal(pr(T1), pr(DEN)).then_inc(sp_recip, 1)
            ffn_dve(dve, "ffn1", 0)
            turn_dve(dve, "mix", gains[:, 1, :])
            stream_split(dve, "w_u")
            turn_qku_fetch(dve, 1, 0, 4, dve.tensor_copy)
            dve.wait_ge(tq_turned, 4)
            dve.wait_ge(row_ready, 16)
            for h in range(2):
                steps.did(dve.tensor_tensor(u_nat[:, h, :], u_nat[:, h, :], row_d[:], ALU.mult))
            dve.wait_ge(tables_ready, 1)
            steps.settle()
            stream_split(dve, "w_qkv", between=spread(ssm_step_dve, dve, SSM_STEPS, "w_qkv"))
            turn_qku_fetch(dve, 1, 4, 12, dve.tensor_copy)
            mod_dve(dve, 0)
            dve.wait_ge(att_consts, 16)
            stream_split(dve, "mod", between=spread(attention1_step_dve, dve, N_HEADS1 + 2, "mod"))
            mod_col_dve(dve, 0)
            turn_dve(dve, "y")
            stream_split(dve, "glu", glu_fetch_dve(dve))
            glu_dve(dve)
            turn_dve(dve, "ssm", gains[:, 2, 0:8], width=HALF)
            turn_dve(dve, "att", gains[:, 2, 8:16], width=HALF, dst=8)
            stream_split(dve, "w_out", fetch_residual(dve))
            turn_dve(dve, "ffn2", gains[:, 3, :])
            ffn_dve(dve, "ffn2", 1)
            final_norm_dve(dve)
            mod_dve(dve, 1)
            dve.wait_ge(gw_hi, 1)
            dve.tensor_tensor(gate_w_lo[:], gate_w[:], gate_w_hi[:].bitcast(F32), ALU.subtract).then_inc(gw_lo, 1)
            stream_split(dve, "mod_gate")
            mod_col_dve(dve, 1)
            dve.wait_ge(ctx_loaded, 16)
            centre_dve(dve, cen, cen).then_inc(cen_done, 1)
            turn_dve(dve, "u_ctx", mod_col[:, KT:2 * KT, 1], bias=mod_col[:, 0:KT, 1], tmp=turn_tmp2)
            centre_dve(dve, cen, resid).then_inc(cen_done, 1)
            dve.memset(va[:, :, :, DV_A:VA], 1.0)
            gates_dve_pre(dve, 0)
            stream_split(dve, "ctx_k")
            gates_dve_log(dve, 0)
            stream_split(dve, "ctx_v")
            gates_dve_scan(dve, 0)
            stream_split(dve, "ctx_kv")
            gates_dve_cols(dve, 0)
            turn_dve(dve, "u_x", mod_col[:, KT:2 * KT, 0], bias=mod_col[:, 0:KT, 0], tmp=turn_tmp2)
            gates_dve_pre(dve, 1)
            stream_split(dve, "x_qk", between=spread(ctx_step_dve, dve, CTX_STEPS, "x_qk"))
            gates_dve_log(dve, 1)
            stream_split(dve, "x_v", between=spread(xv_step_dve, dve, XV_STEPS, "x_v"))
            between = spread(mlstm_step_dve, dve, MLSTM_STEPS, "x_kv", "x_o")
            stream_split(dve, "x_kv", between=between)
            stream_split(dve, "x_o", gated_dve(dve, ha, 0, "o"), between)
            head_norm_dve(dve)
            stream_split(dve, "x_q")
            stream_split(dve, "x_z", gated_dve(dve, ha, 4, "z"), spread(xz_step_dve, dve, XZ_STEPS, "x_z"))
            stream_split(dve, "x_ga", between=spread(attention2_step_dve, dve, ATT2_STEPS, "x_ga"))
            stream_split(dve, "x_zb", gated_dve(dve, ob, 8))
            stream_split(dve, "x_gb")
            turn_dve(dve, "ha", mh_col)
            stream_split(dve, "ba", ba_fetch(dve))
            turn_dve(dve, "ob")
            gate_row_dve(dve)
            stream_split(dve, "bb", bb_fetch(dve))
            turn_dve(dve, "merge")
            stream_split(dve, "wo", wo_fetch(dve))
            end_dve(dve)

        @block.tensor
        def _(pe):
            pe.wait_ge(x_ready, 16)
            turn_pe(pe, "ffn1", resid)
            turned(pe, "ffn1")
            ffn_pe(pe, "ffn1", 0)
            turn_pe(pe, "mix", resid)
            turned(pe, "mix")
            stream_pe(pe, "w_u")
            turn_qku_pe(pe, 0, 4, "w_qkv")
            for par in range(2):
                pe.wait_ge(tq_fetched[par], 2)
            pe.wait_ge(b_ready, 32)
            ssm_input_pe(pe, 0)
            stream_pe(pe, "w_qkv", between=spread(ssm_step_pe, pe, SSM_STEPS, "w_qkv"))
            pe.wait_ge(ssm_y_read, 2)
            turn_qku_pe(pe, 4, 12, "mod")
            for par in range(2):
                pe.wait_ge(tq_fetched[par], 6)
            mod_pe(pe, "mod", 0, spread(attention1_step_pe, pe, N_HEADS1 + 2, "mod"))
            mod_turn_pe(pe, "glu", 0)
            pe.wait_ge(mod_done, 1)
            pe.wait_ge(ssm_gelu, 2)
            turn_pe(pe, "y", ssm_y)
            turned(pe, "y")
            stream_pe(pe, "glu")
            turn_pe(pe, "ssm", ssm_y)
            turn_pe(pe, "att", att)
            turned(pe, "att")
            stream_pe(pe, "w_out")
            turn_pe(pe, "ffn2", resid)
            turned(pe, "ffn2")
            ffn_pe(pe, "ffn2", 1)
            mod_pe(pe, "mod_gate", 1)
            mod_turn_pe(pe, "ctx_k", 1)
            turn_pe(pe, "u_ctx", cen)
            turned(pe, "u_ctx")
            gates_pe_product(pe, 0)
            stream_pe(pe, "ctx_k")
            stream_pe(pe, "ctx_v")
            gates_pe_rows(pe, 0)
            stream_pe(pe, "ctx_kv")
            gates_pe_cols(pe, 0)
            pe.wait_ge(gt_done, 1)
            turn_pe(pe, "u_x", cen)
            turned(pe, "u_x")
            gates_pe_product(pe, 1)
            pe.wait_ge(gt_pre, 2)
            stream_pe(pe, "x_qk", between=spread(ctx_step_pe, pe, CTX_STEPS, "x_qk"))
            pe.wait_ge(hn_stored, TURN_BANKS[1])
            for m in range(2):
                pe.wait_ge(fetched[m], AT["x_v"][1] + 1)
            stream_pe(pe, "x_v", between=spread(xv_step_pe, pe, XV_STEPS, "x_v"))
            between = spread(mlstm_step_pe, pe, MLSTM_STEPS, "x_kv", "x_o")
            stream_pe(pe, "x_kv", between=between)
            stream_pe(pe, "x_o", between=between)
            stream_pe(pe, "x_q")
            stream_pe(pe, "x_z", between=spread(xz_step_pe, pe, XZ_STEPS, "x_z"))
            stream_pe(pe, "x_ga", between=spread(attention2_step_pe, pe, ATT2_STEPS, "x_ga"))
            stream_pe(pe, "x_zb")
            stream_pe(pe, "x_gb")
            turn_pe(pe, "ha", ha)
            turned(pe, "ha")
            stream_pe(pe, "ba")
            turn_pe(pe, "ob", ob)
            turned(pe, "ob")
            gate_row_pe(pe)
            stream_pe(pe, "bb")
            turn_pe(pe, "merge", sg_a)
            turned(pe, "merge")
            stream_pe(pe, "wo")

        @block.gpsimd
        def _(pool):
            steps = Steps(pool, pool_steps)
            for dst, name in ((pr(LDT), "ssm_log_dt"), (pr(LR), "ssm_a_re"), (pr(LI), "ssm_a_im"),
                              (cf_re[:], "ssm_c_re"), (cf_im[:], "ssm_c_im")):
                pool.dma_start(dst, A[name]).then_inc(ssm_consts, 16)
            pool.dma_start(c_col[:], A["c_col"]).then_inc(c_loaded, 16)
            ssm_params_pool(pool, steps)
            pool.wait_ge(w_used, AT["w_u"][0])
            for dst, name in ((b_re[:], "ssm_b_re"), (b_im[:], "ssm_b_im")):
                pool.dma_start(dst, A[name]).then_inc(b_ready, 16)
            pool.dma_start(row_d[:], A["ssm_d"].partition_broadcast(P)).then_inc(row_ready, 16)
            ssm_tables_pool(pool, steps)
            ssm_steps_pool(pool, steps)
            pool.wait_ge(ssm_y_done, ST)
            pool.dma_start(log_mask[:], A["log_mask"]).then_inc(att_consts, 16)
            pool.dma_start(row_bglu[:], A["ssm_b_glu"].partition_broadcast(P)).then_inc(row_ready, 16)
            for dst, name in B2_LOADS:
                pool.dma_start(dst, A[name]).then_inc(b2_consts, 16)
            for dst, name in B2_ROWS:
                pool.dma_start(dst, A[name].partition_broadcast(P)).then_inc(b2_consts, 16)
            pool.wait_ge(w_used, AT["mod_gate"][0])
            pool.dma_start(fin_row[:], A["final_norm"].partition_broadcast(P)).then_inc(fin_loaded, 16)
            pool.dma_start(cen[:], A["ctx_2"].rearrange("(h p) d -> p h d", p=P)).then_inc(ctx_loaded, 16)
            pool.wait_ge(gt_prod, 2)
            pool.dma_start(neg_mask[:], A["neg_mask"]).then_inc(mask_loaded, 16)
            pool.wait_ge(nt_turned, turns["ha"][0] + 16)
            pool.dma_start(ln_w_row[:], A["ln_w_2"].partition_broadcast(P)).then_inc(ln_loaded, 16)
            pool.dma_start(ln_b_row[:], A["ln_b_2"].partition_broadcast(P)).then_inc(ln_loaded, 16)


def lay_out(inputs):
    def a(name):
        return np.ascontiguousarray(inputs[name])

    def by_feature(v):
        return np.ascontiguousarray(v.reshape(-1, P).T)

    o = {"x": a("x")[0]}
    for n in ("ffn1_w_gate", "ffn1_w_up", "ffn1_w_down"):
        o[n] = a(n)[0]
    o["gains"] = np.concatenate([by_feature(a("ffn1_norm")), by_feature(a("mix_norm")),
                                 np.concatenate([by_feature(a("ssm_out_norm")), by_feature(a("attn_out_norm"))], 1),
                                 by_feature(a("ffn2_norm"))], axis=1)
    for n in ("w_in", "ssm_w_glu", "w_out", "ffn2_w_gate", "ffn2_w_up", "ffn2_w_down"):
        o[n] = a(n)[0]
    for n in ("ssm_a_re", "ssm_a_im"):
        o[n] = np.ascontiguousarray(a(n)[0].reshape(ST, P).T)
    o["ssm_log_dt"] = np.ascontiguousarray(np.repeat(a("ssm_log_dt")[0], STATE).reshape(ST, P).T)
    for n in ("ssm_c_re", "ssm_c_im"):
        c = a(n)[0].reshape(ST, 2, GROUP, STATE)
        o[n] = np.zeros((P, ST, 2 * GROUP), np.float32)
        for g in range(2):
            o[n][STATE * g:STATE * (g + 1), :, GROUP * g:GROUP * (g + 1)] = c[:, g].transpose(2, 0, 1)
    for n in ("ssm_b_re", "ssm_b_im"):
        b = a(n)[0].reshape(8, 4, 2, STATE, GROUP)
        o[n] = np.zeros((P, 8, P), np.float32)
        for j in range(4):
            for g in range(2):
                q = 32 * j + GROUP * g
                o[n][q:q + GROUP, :, STATE * g:STATE * (g + 1)] = b[:, j, g].transpose(2, 0, 1)
    o["ssm_d"] = a("ssm_d").reshape(-1)
    o["ssm_b_glu"] = a("ssm_b_glu").reshape(-1)
    for n in ("w_mod_2", "w_in_2", "w_branch_a_2", "w_branch_b_2", "w_out_2"):
        o[n] = a(n)[0]
    o["ctx_2"] = a("ctx_2")[0]
    for n in ("final_norm", "b_if_2", "q_norm_w_2", "k_norm_w_2", "ln_w_2", "ln_b_2"):
        o[n] = a(n).reshape(-1)
    o["c_col"] = np.stack([by_feature(a("c_2").reshape(-1)), by_feature(a("c_ctx_2").reshape(-1))], axis=1)
    o["b_mod_col"] = by_feature(a("b_mod_2").reshape(-1))
    o["conv_w"] = np.ascontiguousarray(a("conv_w_2")[0].reshape(3, KT, P).transpose(2, 1, 0))
    o["conv_b"] = by_feature(a("conv_b_2").reshape(-1))
    o["mh_col"] = by_feature(a("mh_norm_w_2").reshape(-1))
    o["gate_w"] = np.ascontiguousarray(a("w_in_2")[0][:, GATE0:KB0].reshape(KT, P, KB0 - GATE0).transpose(1, 0, 2))
    half = HD_B // 4
    inv = 10000.0 ** (-np.arange(0, 2 * half, 2) / (2 * half))
    tok = np.arange(SEQ)
    angle = np.stack([(tok // GRID_W)[:, None] * inv, (tok % GRID_W)[:, None] * inv], axis=1)
    o["rope"] = np.ascontiguousarray(np.stack([np.cos(angle), np.sin(angle)]).reshape(2, 2, P, 2, half)
                                     .transpose(2, 0, 1, 3, 4).astype(np.float32))
    key, query = np.arange(SEQ)[:, None], np.arange(SEQ)[None, :]
    seen = np.stack([key <= query, key >= query])
    o["neg_mask"] = np.ascontiguousarray(np.where(seen, 0.0, BIG_NEG).astype(np.float32)
                                         .reshape(2, 2, P, SEQ).transpose(2, 0, 1, 3))
    t, s = np.arange(SEQ)[:, None], np.arange(SEQ)[None, :]
    n_branches = sum((t >= s) & (t - s <= w) & ((t - s) % d == 0) for w, d in ((128, 1), (512, 4), (2048, 16)))
    log_n = np.where(n_branches > 0, np.log(np.maximum(n_branches, 1)), BIG_NEG).astype(np.float32)
    o["log_mask"] = np.concatenate([log_n[:P, :P], log_n[P:, :]], axis=1)
    o["ident"] = np.eye(P, dtype=np.float32)
    return o


def kernel(**inputs):
    from concourse import bacc
    from concourse.bass_utils import run_bass_kernel_spmd

    nc = bacc.Bacc("TRN2", target_bir_lowering=False, num_devices=1)
    arrays, A = {}, {}
    for name, a in lay_out({k: np.asarray(v) for k, v in inputs.items()}).items():
        arrays[f"in_{name}"] = a
        A[name] = nc.dram_tensor(f"in_{name}", a.shape, mybir.dt.from_np(a.dtype), kind="ExternalInput").ap()
    out = nc.dram_tensor("out_x", (SEQ, D), F32, kind="ExternalOutput").ap()
    build(nc, A, out)
    r = run_bass_kernel_spmd(nc, [arrays], core_ids=[0])
    return r.results[0]["out_x"].reshape(1, SEQ, D)
```

```python
from contextlib import ExitStack

import numpy as np

import concourse.bass as bass
from concourse import mybir

F32 = mybir.dt.float32
F32R = mybir.dt.float32r
ALU = mybir.AluOpType
ACT = mybir.ActivationFunctionType
X_AXIS = mybir.AxisListType.X

P = 128
SEQ = 256
D = 2048
KT = D // P
D_FF = 5504
FT = D_FF // P
BLK = 512
HALF = D // 2
N_HEADS1, HD1 = 16, 64
GROUP, STATE = 16, 64
ST = 32
FRAME = 128
EPS = 1e-6
SLOTS = 4
LEAD = 4
BIG_NEG = -1e30
TWO_PI = 6.283185307179586
NH_A, DK_A, DV_A = 8, 128, 256
VA = DV_A + 1
NH_B, NKV_B, HD_B = 16, 4, 128
GRID_W = 64
ALPHA = 2.0 ** 0.25
GATE0 = 2 * NH_A * DK_A + NH_A * DV_A
KB0 = GATE0 + 4 * NH_A

JOBS = [("ffn1", None, None), ("w_u", 8, 2), ("w_qkv", 8, 6), ("glu", 4, 2), ("mod", 8, 8), ("w_out", 8, 4), ("ffn2", None, None),
        ("mod_gate", 8, 4), ("ctx_k", 8, 2), ("ctx_v", 8, 4), ("ctx_kv", 8, 2),
        ("x_qk", 8, 4), ("x_v", 8, 4), ("x_kv", 8, 2), ("x_o", 8, 4), ("x_q", 8, 4), ("x_z", 8, 4),
        ("x_ga", 8, 4), ("x_zb", 8, 4), ("x_gb", 8, 4), ("ba", 8, 4), ("bb", 8, 4), ("wo", 8, 4)]
DOWN_CHUNKS = 44
FFN_CHUNKS = 11 * 16 + 2 * DOWN_CHUNKS


def plan():
    chunk, pair, where = 0, 0, {}
    for name, nch, nb in JOBS:
        where[name] = (chunk, pair)
        chunk += FFN_CHUNKS if nch is None else nch * nb
        pair += 13 if nch is None else nb // 2
    where["end"] = (chunk, pair)
    return where


AT = plan()
TOTAL_CHUNKS = AT["end"][0]


class Steps:

    def __init__(self, eng, sem):
        self.eng, self.sem, self.n = eng, sem, 0

    def did(self, ins):
        self.n += 1
        ins.then_inc(self.sem, 1)
        return self.n

    def settle(self):
        self.eng.wait_ge(self.sem, self.n)


def build(nc, A, out):
    ctx = ExitStack()
    with ctx:
        def sem(name):
            return ctx.enter_context(nc.semaphore(name))

        top = [16512]

        def at(name, shape, dt=F32, offset=None):
            size = 4 * int(np.prod(shape[1:]))
            if offset is None:
                offset = top[0]
                top[0] += -(-size // 32) * 32
            assert offset + size <= 229344, (name, offset, size)
            return nc.alloc_sbuf_tensor_at(name, shape, dt, offset=offset)

        class Region:
            def __init__(self, offset):
                self.o = offset

            def __call__(self, name, shape, dt=F32):
                t = at(name, shape, dt, offset=self.o)
                self.o += -(-4 * int(np.prod(shape[1:])) // 32) * 32
                return t

        resid = at("resid", [P, 2, D])
        act_hi = at("act_hi", [P, KT, SEQ], F32R)
        act_lo = at("act_lo", [P, KT, SEQ], F32R)
        junk_full = at("junk_full", [P, 2, D], offset=16512 + 4 * 2 * D)
        junk_lo = at("junk_lo", [P, 2, D], offset=16512 + 4 * 2 * D + 4 * KT * SEQ)
        junk_lo_half = at("junk_lo_half", [P, 2, HALF], offset=16512 + 4 * 2 * D + 4 * 3 * KT // 2 * SEQ)
        w_raw = at("w_raw", [P, SLOTS, 2 * BLK])
        w_hi = at("w_hi", [P, SLOTS, 2 * BLK], F32R)
        w_lo = at("w_lo", [P, SLOTS, 2 * BLK], F32R)
        ident = at("ident_sb", [P, P])
        gains = at("gains_sb", [P, 4, KT])
        stat = at("stat", [P, 64])
        dscale = at("dscale", [P, 2, P])
        dscale_att = at("dscale_att", [P, 2, P])
        stage0 = top[0]

        r = Region(stage0)
        g_hi = r("g_hi", [P, FT, SEQ], F32R)
        g_lo = r("g_lo", [P, FT, SEQ], F32R)
        silu_gate = r("silu_gate", [P, 2, BLK])
        gated = r("gated", [P, 2, BLK])

        acc = ctx.enter_context(nc.psum_tensor("acc", [P, 2, 2, BLK], F32))
        pst = ctx.enter_context(nc.psum_tensor("pst", [P, 4, BLK], F32))

        w_raw_ready = [sem(f"w_raw_ready{s}") for s in range(SLOTS)]
        w_hi_done, w_lo_done, w_used = sem("w_hi_done"), sem("w_lo_done"), sem("w_used")
        fetched = [sem("fetched_a"), sem("fetched_b")]
        consts_ready, x_ready = sem("consts_ready"), sem("x_ready")
        dve_steps = sem("dve_steps")
        nt_square, nt_mean, nt_root, nt_diag = sem("nt_square"), sem("nt_mean"), sem("nt_root"), sem("nt_diag")
        nt_turned, nt_hi, nt_lo = sem("nt_turned"), sem("nt_hi"), sem("nt_lo")
        g_turned, g_hi_done, g_lo_done = sem("g_turned"), sem("g_hi_done"), sem("g_lo_done")
        steps = None
        out_done = sem("out_done")

        def cols(w, k0, col, n=BLK):
            return w.rearrange("(k p) n -> p k n", p=P)[:, k0:k0 + 2, bass.ds(col, n)]

        def load_chunk(sp, s, src, c=None):
            c = s if c is None else c
            if not isinstance(c, int) or c >= SLOTS:
                sp.wait_ge(w_lo_done, c - SLOTS + 1)
            view = w_raw[:, s % SLOTS, :]
            if len(src.shape) == 3:
                view = view.rearrange("p (k n) -> p k n", k=src.shape[1])
            sp.dma_start(view, src).then_inc(w_raw_ready[s % SLOTS], 16)

        def round_chunk(act, s, c=None, q=None):
            if s >= TOTAL_CHUNKS:
                return
            act.wait_ge(w_raw_ready[s % SLOTS], 16 * ((s // SLOTS if q is None else q) + 1))
            c = s if c is None else c
            if not isinstance(c, int) or c >= SLOTS:
                act.wait_ge(w_used, c - SLOTS + 1)
            act.activation(w_hi[:, s % SLOTS, :], w_raw[:, s % SLOTS, :], ACT.Copy).then_inc(w_hi_done, 1)

        def rest_chunk(dve, s, c=None):
            if s >= TOTAL_CHUNKS:
                return
            dve.wait_ge(w_hi_done, (s if c is None else c) + 1)
            dve.tensor_tensor(w_lo[:, s % SLOTS, :], w_raw[:, s % SLOTS, :],
                              w_hi[:, s % SLOTS, :].bitcast(F32), ALU.subtract).then_inc(w_lo_done, 1)

        def split_ahead(eng, s0, k, i, nch, first=LEAD, last=None):
            for j in range(first, nch + LEAD if last is None else last):
                s = s0 + j
                c = None if i is None else i * k + s
                if eng is nc_act:
                    round_chunk(eng, s, c, None if i is None else i * (k // SLOTS) + s // SLOTS)
                else:
                    rest_chunk(eng, s, c)

        nc_act, nc_dve = nc.scalar, nc.vector

        def block_product(pe, s0, c0, hi, lo, par, nch, pair, between=None, turning=None):
            pe.wait_ge(fetched[par], pair + 1)
            for j in range(nch):
                if turning is not None:
                    turning.before_chunk(j)
                pe.wait_ge(w_lo_done, c0 + j + 1)
                slot = (s0 + j) % SLOTS
                for kk in range(2):
                    k = 2 * j + kk
                    wh = w_hi[:, slot, kk * BLK:(kk + 1) * BLK]
                    wl = w_lo[:, slot, kk * BLK:(kk + 1) * BLK]
                    for h in range(2):
                        xh, xl = hi[:, k, h * P:(h + 1) * P], lo[:, k, h * P:(h + 1) * P]
                        o = acc[:, par, h, :]
                        pe.matmul(o, xh, wh, start=k == 0, stop=False)
                        pe.matmul(o, xh, wl, start=False, stop=False)
                        mm = pe.matmul(o, xl, wh, start=False, stop=k == 2 * nch - 1)
                mm.then_inc(w_used, 1)
                if between is not None:
                    between()

        turns = {}
        turn_count = [0, 0, 0]

        dscale_of = {name: dscale for name in ("ffn1", "mix", "ssm", "ffn2", "u_ctx", "u_x")}
        dscale_of["att"] = dscale_att

        def plan_turn(name, n, normed):
            turns[name] = (turn_count[0], turn_count[1], n, normed)
            turn_count[0] += n
            turn_count[1] += int(normed)

        for name, n, normed in (("ffn1", 16, True), ("mix", 16, True), ("y", 8, False), ("ssm", 8, True),
                                ("att", 8, True), ("ffn2", 16, True), ("u_ctx", 16, True), ("u_x", 16, True),
                                ("ha", 16, False), ("ob", 16, False), ("merge", 16, False)):
            plan_turn(name, n, normed)

        def norm_squares_act(act, src, junk):
            for h in range(2):
                act.activation(junk[:, h, :], src[:, h, :], ACT.Square,
                               accum_out=stat[:, h:h + 1]).then_inc(nt_square, 1)

        def norm_root_act(act, name):
            act.wait_ge(nt_mean, turns[name][1] + 1)
            act.activation(stat[:, 4:6], stat[:, 2:4], ACT.Sqrt).then_inc(nt_root, 1)

        def norm_act(act, name, src, junk):
            norm_squares_act(act, src, junk)
            norm_root_act(act, name)

        def norm_mean_dve(dve, name, width=D):
            dve.wait_ge(nt_square, 2 * (turns[name][1] + 1))
            dve.tensor_scalar(stat[:, 2:4], stat[:, 0:2], 1.0 / width, EPS, ALU.mult, ALU.add).then_inc(nt_mean, 1)

        def norm_diag_dve(dve, name):
            dve.wait_ge(nt_root, turns[name][1] + 1)
            steps.did(dve.reciprocal(stat[:, 6:8], stat[:, 4:6]))
            steps.settle()
            for h in range(2):
                dve.tensor_scalar(dscale_of[name][:, h, :], ident[:], stat[:, 6 + h:7 + h], None,
                                  ALU.mult).then_inc(nt_diag, 1)

        def norm_dve(dve, name, width=D):
            norm_mean_dve(dve, name, width)
            norm_diag_dve(dve, name)

        def turn_act(act, name, gain=None, dst=0, bias=None):
            t0, _, n, _ = turns[name]
            for k in range(n):
                act.wait_ge(nt_turned, t0 + k + 1)
                o, i = act_hi[:, dst + k, :], pst[:, (t0 + k) % 4, 0:SEQ]
                if bias is not None:
                    ins = act.activation(o, i, ACT.Identity, scale=gain[:, k:k + 1], bias=bias[:, k:k + 1])
                elif gain is not None:
                    ins = act.activation(o, i, ACT.Copy, scale=gain[:, k:k + 1])
                else:
                    ins = act.activation(o, i, ACT.Copy)
                ins.then_inc(nt_hi, 1)

        def turn_dve(dve, name, gain=None, dst=0, bias=None, tmp=None):
            t0, _, n, _ = turns[name]
            for k in range(n):
                dve.wait_ge(nt_hi, t0 + k + 1)
                o, i = act_lo[:, dst + k, :], pst[:, (t0 + k) % 4, 0:SEQ]
                hi = act_hi[:, dst + k, :].bitcast(F32)
                if bias is not None:
                    steps.did(dve.tensor_scalar(tmp[:, k % 2, :], i, gain[:, k:k + 1], bias[:, k:k + 1],
                                                ALU.mult, ALU.add))
                    steps.settle()
                    ins = dve.tensor_tensor(o, tmp[:, k % 2, :], hi, ALU.subtract)
                elif gain is not None:
                    ins = dve.scalar_tensor_tensor(out=o, in0=i, scalar=gain[:, k:k + 1], in1=hi,
                                                   op0=ALU.mult, op1=ALU.subtract)
                else:
                    ins = dve.tensor_tensor(o, i, hi, ALU.subtract)
                ins.then_inc(nt_lo, 1)

        class TurnedFirst:

            def __init__(self, pe, *parts):
                self.pe, self.tiles = pe, []
                for name, src in parts:
                    t0, c0, n, normed = turns[name]
                    self.tiles += [(name, src, t0 + k, k, c0 if normed else None) for k in range(n)]
                self.t0, self.issued = self.tiles[0][2], 0

            def issue(self, upto):
                while self.issued < min(upto, len(self.tiles)):
                    name, src, t, k, c0 = self.tiles[self.issued]
                    self.issued += 1
                    if c0 is not None and k == 0:
                        self.pe.wait_ge(nt_diag, 2 * (c0 + 1))
                    if t >= 4:
                        self.pe.wait_ge(nt_lo, t - 3)
                    for h in range(2):
                        o, lhs = pst[:, t % 4, h * P:(h + 1) * P], src[:, h, k * P:(k + 1) * P]
                        if c0 is not None:
                            mm = self.pe.matmul(o, lhs, dscale_of[name][:, h, :], start=True, stop=True)
                        else:
                            mm = self.pe.transpose(o, lhs, ident[:])
                    mm.then_inc(nt_turned, 1)

            def before_chunk(self, j):
                self.issue(4 * j + 6)
                self.pe.wait_ge(nt_lo, self.t0 + 2 * j + 2)

        NB = 11

        def ffn_iterations(eng, name, it):
            s0, p0 = AT[name]
            it(0, s0, s0, p0, None)
            with eng.Fori(1, NB - 1) as i:
                it(i, s0, i * 16 + s0, i + p0, i)
            it(NB - 1, s0 + 16 * (NB - 1), s0 + 16 * (NB - 1), p0 + NB - 1, None)

        def first(b):
            return isinstance(b, int) and b == 0

        def ffn_sp(sp, name, w_gate, w_up, w_down):
            def it(b, s, c, p, i):
                col = D_FF - BLK if isinstance(b, int) and b == NB - 1 else b * BLK
                for m, w in enumerate((w_gate, w_up)):
                    for j in range(8):
                        load_chunk(sp, s + 8 * m + j, cols(w, 2 * j, col), c + 8 * m + j)
            ffn_iterations(sp, name, it)
            s1 = AT[name][0] + 16 * NB
            wd = w_down.rearrange("(k p) n -> p k n", p=P)
            with sp.Fori(0, 2) as i:
                for j in range(DOWN_CHUNKS):
                    load_chunk(sp, s1 + j, wd[:, min(j, FT - 1), bass.ds(i * 1024, 1024)],
                               i * DOWN_CHUNKS + s1 + j)

        def tiles_of(b):
            return slice(FT - 4, FT) if isinstance(b, int) and b == NB - 1 else (
                slice(4 * b, 4 * b + 4) if isinstance(b, int) else bass.ds(b * 4, 4))

        turned_tiles = pst[:, 0:2, :].rearrange("p a (b t) -> p (a b) t", b=2)

        def ffn_act(act, name, n_use):
            b0 = NB * n_use

            def hi_tiles(b):
                act.wait_ge(g_turned, b + (b0 + 1))
                act.activation(g_hi[:, tiles_of(b), :], turned_tiles, ACT.Copy).then_inc(g_hi_done, 1)

            def it(b, s, c, p, i):
                split_ahead(act, s, 16, i, 16, LEAD, 8 + LEAD)
                act.wait_ge(w_used, c + 8)
                act.wait_ge(fetched[1], p + 1)
                act.activation(silu_gate[:], acc[:, 0, :, :], ACT.Silu).then_inc(fetched[0], 1)
                if not first(b):
                    hi_tiles(b - 1)
                split_ahead(act, s, 16, i, 16, 8 + LEAD, 16 + LEAD)
            ffn_iterations(act, name, it)
            hi_tiles(NB - 1)
            s1 = AT[name][0] + 16 * NB
            with act.Fori(0, 2) as i:
                split_ahead(act, s1, DOWN_CHUNKS, i, DOWN_CHUNKS)

        def ffn_dve(dve, name, n_use):
            b0 = NB * n_use

            def lo_tiles(b):
                dve.wait_ge(g_hi_done, b + (b0 + 1))
                dve.tensor_tensor(g_lo[:, tiles_of(b), :], turned_tiles,
                                  g_hi[:, tiles_of(b), :].bitcast(F32), ALU.subtract).then_inc(g_lo_done, 1)

            def it(b, s, c, p, i):
                split_ahead(dve, s, 16, i, 16, LEAD, 8 + LEAD)
                if not first(b):
                    lo_tiles(b - 1)
                split_ahead(dve, s, 16, i, 16, 8 + LEAD, 16 + LEAD)
                dve.wait_ge(w_used, c + 16)
                dve.wait_ge(fetched[0], p + 2)
                if not first(b):
                    dve.wait_ge(g_turned, b + b0)
                dve.tensor_tensor(gated[:], silu_gate[:], acc[:, 1, :, :], ALU.mult).then_inc(fetched[1], 1)
            ffn_iterations(dve, name, it)
            lo_tiles(NB - 1)
            s1 = AT[name][0] + 16 * NB
            with dve.Fori(0, 2) as i:
                split_ahead(dve, s1, DOWN_CHUNKS, i, DOWN_CHUNKS)
                dve.wait_ge(w_used, i * DOWN_CHUNKS + (s1 + DOWN_CHUNKS))
                for par in range(2):
                    o = resid[:, :, bass.ds(i * 1024 + par * BLK, BLK)]
                    dve.scalar_tensor_tensor(out=o, in0=acc[:, par, :, :], scalar=0.5, in1=o,
                                             op0=ALU.mult, op1=ALU.add).then_inc(fetched[par], 1)

        def ffn_pe(pe, name, n_use, turning):
            b0 = NB * n_use

            def turn_gated(b, p):
                pe.wait_ge(fetched[1], p + 2)
                pe.wait_ge(g_lo_done, b + (b0 + 1))
                for t in range(4):
                    for h in range(2):
                        mm = pe.transpose(turned_tiles[:, t, h * P:(h + 1) * P],
                                          gated[:, h, t * P:(t + 1) * P], ident[:])
                mm.then_inc(g_turned, 1)

            def it(b, s, c, p, i):
                block_product(pe, s, c, act_hi, act_lo, 0, 8, p, turning=turning if first(b) else None)
                if not first(b):
                    turn_gated(b - 1, p - 1)
                block_product(pe, s + 8, c + 8, act_hi, act_lo, 1, 8, p)
            ffn_iterations(pe, name, it)
            s0, p0 = AT[name]
            turn_gated(NB - 1, p0 + NB - 1)
            s1 = s0 + 16 * NB
            pe.wait_ge(g_lo_done, NB + b0 + 1)
            with pe.Fori(0, 2) as i:
                for par in range(2):
                    pe.wait_ge(fetched[par], i + (p0 + NB + 1))
                for j in range(FT):
                    pe.wait_ge(w_lo_done, i * DOWN_CHUNKS + (s1 + j + (1 if j < FT - 1 else 2)))
                    slot = (s1 + j) % SLOTS
                    for par in range(2):
                        wh = w_hi[:, slot, par * BLK:(par + 1) * BLK]
                        wl = w_lo[:, slot, par * BLK:(par + 1) * BLK]
                        for h in range(2):
                            gh, gl = g_hi[:, j, h * P:(h + 1) * P], g_lo[:, j, h * P:(h + 1) * P]
                            o = acc[:, par, h, :]
                            pe.matmul(o, gh, wh, start=j == 0, stop=False)
                            pe.matmul(o, gh, wl, start=False, stop=False)
                            mm = pe.matmul(o, gl, wh, start=False, stop=j == FT - 1)
                    mm.then_inc(w_used, 1 if j < FT - 1 else 2)

        def job(name):
            nch, nb = next((n, b) for j, n, b in JOBS if j == name)
            return AT[name] + (nch, nb)

        def pairs(eng, name, body, unrolled=False, peeled=0):
            s0, p0, nch, nb = job(name)
            if nb == 2 or unrolled or name == JOBS[-1][0]:
                for i in range(nb // 2):
                    s = s0 + 2 * nch * i
                    body(i, s, s, p0 + i)
            else:
                for i in range(peeled):
                    body(i, s0 + 2 * nch * i, s0 + 2 * nch * i, p0 + i)
                with eng.Fori(peeled, nb // 2) as i:
                    body(i, s0, i * (2 * nch) + s0, i + p0)

        def stream_sp(sp, name, w, col0):
            nch = job(name)[2]

            def body(i, s, c, p):
                for m in range(2):
                    for j in range(nch):
                        load_chunk(sp, s + nch * m + j, cols(w, 2 * j, (i * 2 + m) * BLK + col0), c + nch * m + j)
            pairs(sp, name, body)

        def stream_pe(pe, name, between=None, turning=None):
            nch = job(name)[2]

            def body(i, s, c, p):
                for m in range(2):
                    block_product(pe, s + nch * m, c + nch * m, act_hi, act_lo, m, nch, p, between,
                                  turning if isinstance(i, int) and i == 0 and m == 0 else None)
            pairs(pe, name, body, between is not None, 0 if turning is None else 1)

        def stream_split(eng, name, fetch=None, between=None, unrolled=False):
            nch = job(name)[2]

            def body(i, s, c, p):
                for m in range(2):
                    if between is None:
                        split_ahead(eng, s + nch * m, 2 * nch, None if isinstance(i, int) else i, nch)
                    else:
                        for j in range(nch):
                            between()
                            split_ahead(eng, s + nch * m, 2 * nch, None, nch, j + LEAD, j + LEAD + 1)
                    if fetch is not None:
                        eng.wait_ge(w_used, c + nch * (m + 1))
                        fetch(m, i * 2 + m, p)
            pairs(eng, name, body, between is not None or unrolled)

        def spread(step, eng, steps, *names, skip=0):
            chunks = sum(job(name)[2] * job(name)[3] for name in names) - skip
            state = [-skip, 0]

            def between():
                state[0] += 1
                while state[1] < state[0] * steps // chunks:
                    step(eng, state[1])
                    state[1] += 1
            return between

        r = Region(stage0)
        prj = r("prj", [P, 2, 4 * HALF])
        q_nat, k_nat, v_nat, u_nat = (prj[:, :, n * HALF:(n + 1) * HALF] for n in range(4))
        att, ssm_y = q_nat, u_nat
        u_t = r("u_t", [P, 8, SEQ])
        glu_in = at("glu_in", [P, 2, HALF], offset=r.o - 4 * 2 * HALF)
        mix_x = r.o
        rot_cos, rot_sin = r("rot_cos", [P, ST, FRAME]), r("rot_sin", [P, ST, FRAME])
        b_re, b_im = (r(n, [P, 8, P]) for n in ("b_re", "b_im"))
        ssm_temps = r.o
        turn_tmp = Region(ssm_temps)("turn_tmp", [P, ST, FRAME // 2])
        prod = r("prod", [P, 2, SEQ])
        st_z = r("st_z", [P, 2, 2, SEQ])
        r = Region(stage0 + 4 * (2 * FT * SEQ + 4 * BLK))
        par_ = r("ssm_par", [P, 22, ST])
        cf_re, cf_im = (r(n, [P, ST, 2 * GROUP]) for n in ("cf_re", "cf_im"))
        cf_tmp = r("cf_tmp", [P, 3, ST // 8, 2 * GROUP])
        frame_init = r("frame_init", [P, 2, 2])
        c_col = r("c_col", [P, 2, KT])
        pick = r("pick", [P, 2])
        assert r.o <= 229344
        r = Region(ssm_temps + 4 * 6 * SEQ)
        z_prod = r("z_prod", [P, 2, SEQ])
        st_s = r("st_s", [P, 3, 2, SEQ])
        assert r.o <= stage0 + 4 * (2 * FT * SEQ + 4 * BLK), (r.o, stage0 + 4 * (2 * FT * SEQ + 4 * BLK))
        r = Region(mix_x)
        q_t, k_t = r("q_t", [P, 8, SEQ]), r("k_t", [P, 8, SEQ])
        log_mask = r("log_mask", [P, 3 * P])
        scores, probs, probs_t = (r(n, [P, 2, 3 * P]) for n in ("scores", "probs", "probs_t"))
        row_max, row_sum, row_inv = (r(n, [P, 2 * N_HEADS1]) for n in ("row_max", "row_sum", "row_inv"))
        row_bglu = r("row_bglu", [P, HALF])
        mod_nat = r("mod_nat", [P, 2 * D])
        assert r.o <= stage0 + 4 * (2 * FT * SEQ + 4 * BLK)
        row_d = at("row_d", [P, HALF], offset=ssm_temps + 4 * 8 * SEQ)

        att_consts, ssm_consts, row_ready = sem("att_consts"), sem("ssm_consts"), sem("row_ready")
        b_ready = sem("b_ready")
        tq_turned, tq_fetched = sem("tq_turned"), [sem("tq_fetched_act"), sem("tq_fetched_dve")]
        at_scores, at_max, at_probs, at_turned, at_copied, at_out, at_fetched = (
            sem("at_" + n) for n in ("scores", "max", "probs", "turned", "copied", "out", "fetched"))
        sp_act, sp_ready, sp_recip, tables_ready = (sem("sp_" + n) for n in ("act", "ready", "recip", "tables"))
        pool_steps, ssm_z = sem("pool_steps"), sem("ssm_z")
        ssm_b, ssm_b_read, ssm_s, ssm_y_done, ssm_y_read, ssm_gelu = (
            sem(n) for n in ("ssm_b", "ssm_b_read", "ssm_s", "ssm_y_done", "ssm_y_read", "ssm_gelu"))
        glu_sig, glu_out = sem("glu_sig"), sem("glu_out")

        def fetch_prj(act, first):
            def fetch(m, blk, p):
                act.activation(prj[:, :, bass.ds((first + blk) * BLK, BLK)], acc[:, m, :, :],
                               ACT.Copy).then_inc(fetched[m], 1)
            return fetch

        TQ = [(u_t, 3 * HALF, n) for n in range(4)] + [(q_t, 0, n) for n in range(4)] + [(k_t, HALF, n) for n in range(4)]

        def turn_qku_pe(pe, first, last, after):
            for m in range(2):
                pe.wait_ge(fetched[m], AT[after][1] + 1)
            for n, (dst, col, t) in list(enumerate(TQ))[first:last]:
                if n >= 4:
                    pe.wait_ge(tq_fetched[n % 2], (n - 4) // 2 + 1)
                for tt in range(2):
                    for h in range(2):
                        c = col + (2 * t + tt) * P
                        mm = pe.transpose(pst[:, n % 4, tt * SEQ + h * P:tt * SEQ + (h + 1) * P],
                                          prj[:, h, c:c + P], ident[:])
                mm.then_inc(tq_turned, 1)

        def turn_qku_fetch(eng, par, first, last, copy):
            for n, (dst, col, t) in enumerate(TQ):
                if n % 2 == par and first <= n < last:
                    eng.wait_ge(tq_turned, n + 1)
                    copy(dst[:, 2 * t:2 * t + 2, :], pst[:, n % 4, :].rearrange("p (a t) -> p a t", a=2)).then_inc(
                        tq_fetched[par], 1)

        def head_rows(n):
            return slice(64 * (n % 2), 64 * (n % 2) + 64), n // 2

        ATT1_STEPS = N_HEADS1 + 4

        def attention1_step_pe(pe, s):
            if s < N_HEADS1:
                if s >= 2:
                    pe.wait_ge(at_max, s - 1)
                rows, t = head_rows(s)
                pe.matmul(pst[:, s % 2, 0:P], q_t[rows, t, 0:P], k_t[rows, t, 0:P], start=True, stop=True)
                pe.matmul(pst[:, s % 2, P:3 * P], q_t[rows, t, P:SEQ], k_t[rows, t, :],
                          start=True, stop=True).then_inc(at_scores, 1)
            n = s - 2
            if 0 <= n < N_HEADS1:
                pe.wait_ge(at_probs, n + 1)
                if n >= 2:
                    pe.wait_ge(at_copied, n - 1)
                for b in range(3):
                    mm = pe.transpose(pst[:, 2 + n % 2, b * P:(b + 1) * P],
                                      probs[:, n % 2, b * P:(b + 1) * P], ident[:])
                mm.then_inc(at_turned, 1)
            n = s - 3
            if 0 <= n < N_HEADS1:
                pe.wait_ge(at_copied, n + 1)
                if n >= 2:
                    pe.wait_ge(at_fetched, n - 1)
                o = acc[:, n % 2, 1, :]
                v = v_nat[:, :, n * HD1:(n + 1) * HD1]
                pe.matmul(o[:, 0:HD1], probs_t[:, n % 2, 0:P], v[:, 0, :], start=True, stop=True)
                pe.matmul(o[:, HD1:2 * HD1], probs_t[:, n % 2, P:2 * P], v[:, 0, :], start=True, stop=False)
                pe.matmul(o[:, HD1:2 * HD1], probs_t[:, n % 2, 2 * P:3 * P], v[:, 1, :],
                          start=False, stop=True).then_inc(at_out, 1)

        def attention1_step_act(act, s):
            n = s - 1
            if 0 <= n < N_HEADS1:
                act.wait_ge(at_max, n + 1)
                if n >= 2:
                    act.wait_ge(at_turned, n - 1)
                for h, (a, b) in enumerate(((0, P), (P, 3 * P))):
                    ins = act.activation(probs[:, n % 2, a:b], scores[:, n % 2, a:b], ACT.Exp,
                                         bias=row_max[:, 2 * n + h:2 * n + h + 1],
                                         accum_out=row_sum[:, 2 * n + h:2 * n + h + 1])
                ins.then_inc(at_probs, 1)
            n = s - 2
            if 0 <= n < N_HEADS1:
                act.wait_ge(at_turned, n + 1)
                if n >= 2:
                    act.wait_ge(at_out, n - 1)
                act.activation(probs_t[:, n % 2, :], pst[:, 2 + n % 2, 0:3 * P], ACT.Copy).then_inc(at_copied, 1)

        def attention1_step_dve(dve, s):
            n = s - 4
            if 0 <= n < N_HEADS1:
                dve.wait_ge(at_out, n + 1)
                steps.did(dve.reciprocal(row_inv[:, 2 * n:2 * n + 2], row_sum[:, 2 * n:2 * n + 2]))
                steps.settle()
                dve.tensor_tensor(att[:, :, n * HD1:(n + 1) * HD1],
                                  acc[:, n % 2, 1, 0:2 * HD1].rearrange("p (h e) -> p h e", h=2),
                                  row_inv[:, 2 * n:2 * n + 2].unsqueeze(2).broadcast_to([P, 2, HD1]),
                                  ALU.mult).then_inc(at_fetched, 1)
            if s < N_HEADS1:
                dve.wait_ge(at_scores, s + 1)
                if s >= 2:
                    dve.wait_ge(at_probs, s - 1)
                steps.did(dve.scalar_tensor_tensor(out=scores[:, s % 2, :], in0=pst[:, s % 2, 0:3 * P],
                                                   scalar=HD1 ** -0.5, in1=log_mask[:], op0=ALU.mult, op1=ALU.add))
                steps.settle()
                for h, (a, b) in enumerate(((0, P), (P, 3 * P))):
                    ins = dve.tensor_reduce(row_inv[:, 2 * s + h:2 * s + h + 1], scores[:, s % 2, a:b],
                                            X_AXIS, ALU.max)
                steps.did(ins)
                steps.settle()
                dve.tensor_scalar(row_max[:, 2 * s:2 * s + 2], row_inv[:, 2 * s:2 * s + 2], -1.0, None,
                                  ALU.mult).then_inc(at_max, 1)

        LDT, LR, LI, DT, LRDT, TH, MAG, N_, RED, SINH, SIN, COS, LRE, LIM, NR, DEN, FRE, FIM, T0, T1 = range(20)

        def pr(n):
            return par_[:, n, :]

        def ssm_params_act(act, part):
            if part == 0:
                act.wait_ge(ssm_consts, 16 * 5)
                act.activation(pr(DT), pr(LDT), ACT.Exp).then_inc(sp_act, 1)
            else:
                act.wait_ge(sp_ready, 1)
                act.activation(pr(MAG), pr(LRDT), ACT.Exp).then_inc(sp_act, 1)
                act.activation(pr(SINH), pr(RED), ACT.Sin, scale=0.5).then_inc(sp_act, 1)
                act.activation(pr(SIN), pr(RED), ACT.Sin).then_inc(sp_act, 1)

        def ssm_params_pool(pool, steps):
            M, A_, S = ALU.mult, ALU.add, ALU.subtract

            def tt(o, a, b, op):
                steps.did(pool.tensor_tensor(o, a, b, op))

            def ts(o, a, s1, op0, s2=None, op1=None):
                if s2 is None:
                    steps.did(pool.tensor_scalar(o, a, s1, None, op0))
                else:
                    steps.did(pool.tensor_scalar(o, a, s1, s2, op0, op1))
            pool.wait_ge(sp_act, 1)
            tt(pr(TH), pr(LI), pr(DT), M)
            tt(pr(LRDT), pr(LR), pr(DT), M)
            steps.settle()
            magic = 1.5 * 2.0 ** 23
            ts(pr(N_), pr(TH), 1.0 / TWO_PI, M, magic, A_)
            steps.settle()
            ts(pr(T0), pr(N_), magic, S)
            steps.settle()
            c1 = 6.28125
            c2 = 0.0019350051879882812
            c3 = TWO_PI - c1 - c2
            src = TH
            for c, dst in ((c1, T1), (c2, RED), (c3, T1)):
                ts(pr(N_), pr(T0), c, M)
                steps.settle()
                tt(pr(dst), pr(src), pr(N_), S)
                steps.settle()
                src = dst
            pool.tensor_scalar(pr(RED), pr(T1), 3.1415925, -3.1415925, ALU.min, ALU.max).then_inc(sp_ready, 1)
            pool.wait_ge(sp_act, 4)
            tt(pr(T0), pr(SINH), pr(SINH), M)
            tt(pr(LIM), pr(MAG), pr(SIN), M)
            tt(pr(DEN), pr(LR), pr(LR), M)
            tt(pr(T1), pr(LI), pr(LI), M)
            steps.settle()
            ts(pr(COS), pr(T0), -2.0, M, 1.0, A_)
            pool.tensor_tensor(pr(DEN), pr(DEN), pr(T1), A_).then_inc(sp_ready, 1)
            steps.settle()
            tt(pr(LRE), pr(MAG), pr(COS), M)
            steps.settle()
            ts(pr(NR), pr(LRE), 1.0, S)
            steps.settle()
            tt(pr(FRE), pr(NR), pr(LR), M)
            tt(pr(T0), pr(LIM), pr(LI), M)
            tt(pr(FIM), pr(LIM), pr(LR), M)
            tt(pr(N_), pr(NR), pr(LI), M)
            steps.settle()
            tt(pr(FRE), pr(FRE), pr(T0), A_)
            tt(pr(FIM), pr(FIM), pr(N_), S)
            steps.settle()
            pool.wait_ge(sp_recip, 1)
            tt(pr(FRE), pr(FRE), pr(T1), M)
            tt(pr(FIM), pr(FIM), pr(T1), M)
            steps.settle()
            pool.wait_ge(ssm_consts, 16 * 5)
            n = ST // 8
            wide = [P, n, 2 * GROUP]
            for g in range(8):
                t = slice(g * n, (g + 1) * n)
                fr, fi = (par_[:, v, t].unsqueeze(2).broadcast_to(wide) for v in (FRE, FIM))
                re, im = cf_re[:, t, :], cf_im[:, t, :]
                tt(cf_tmp[:, 0], im, fi, M)
                tt(cf_tmp[:, 1], re, fi, M)
                tt(cf_tmp[:, 2], im, fr, M)
                tt(re, re, fr, M)
                steps.settle()
                tt(re, re, cf_tmp[:, 0], S)
                tt(cf_tmp[:, 1], cf_tmp[:, 1], cf_tmp[:, 2], A_)
                steps.settle()
                ts(im, cf_tmp[:, 1], -1.0, M)
                steps.settle()

        def ssm_tables_pool(pool, steps):
            M, A_, S = ALU.mult, ALU.add, ALU.subtract

            def tt(o, a, b, op):
                steps.did(pool.tensor_tensor(o, a, b, op))
            steps.did(pool.tensor_copy(rot_cos[:, :, 0:1], pr(COS).unsqueeze(2)))
            steps.did(pool.tensor_copy(rot_sin[:, :, 0:1], pr(SIN).unsqueeze(2)))
            steps.settle()
            w = 1
            while w < FRAME:
                shape = [P, ST, w]
                ec = rot_cos[:, :, w - 1:w].broadcast_to(shape)
                es = rot_sin[:, :, w - 1:w].broadcast_to(shape)
                co, si = rot_cos[:, :, 0:w], rot_sin[:, :, 0:w]
                nc_, ns_ = rot_cos[:, :, w:2 * w], rot_sin[:, :, w:2 * w]
                tmp = turn_tmp[:, :, 0:w]
                tt(nc_, co, ec, M)
                tt(ns_, co, es, M)
                tt(tmp, si, es, M)
                steps.settle()
                tt(nc_, nc_, tmp, S)
                steps.settle()
                tt(tmp, si, ec, M)
                steps.settle()
                tt(ns_, ns_, tmp, A_)
                steps.settle()
                w *= 2
            pool.sem_inc(tables_ready, 1)

        SSM_STEPS = ST + 5
        OUT_LAG = 3

        def ssm_input_pe(pe, i):
            if i >= 2:
                pe.wait_ge(ssm_b_read, i - 1)
            c, j = i // 4, 32 * (i % 4)
            for part, b in enumerate((b_re, b_im)):
                mm = pe.matmul(pst[:, i % 2, part * SEQ:(part + 1) * SEQ], b[j:j + 32, c, :],
                               u_t[j:j + 32, c, :], start=True, stop=True)
            mm.then_inc(ssm_b, 1)

        def ssm_step_pe(pe, i):
            if i + 1 < ST:
                ssm_input_pe(pe, i + 1)
            o = i - OUT_LAG
            if 0 <= o < ST:
                pe.wait_ge(ssm_s, o + 1)
                if o == ST // 2:
                    pe.wait_ge(ssm_y_read, 1)
                c = 2 * GROUP * (o % (ST // 2))
                for h in range(2):
                    dst = pst[:, 2 + h, c:c + 2 * GROUP]
                    pe.matmul(dst, st_s[:, o % 3, 0, h * P:(h + 1) * P], cf_re[:, o, :], start=True, stop=False)
                    mm = pe.matmul(dst, st_s[:, o % 3, 1, h * P:(h + 1) * P], cf_im[:, o, :], start=False, stop=True)
                mm.then_inc(ssm_y_done, 1)

        def ssm_step_dve(dve, i):
            M, A_, S = ALU.mult, ALU.add, ALU.subtract
            done = i - OUT_LAG - 1
            if done in (ST // 2 - 1, ST - 1):
                g = done // (ST // 2)
                dve.wait_ge(ssm_y_done, done + 1)
                o = ssm_y[:, :, g * BLK:(g + 1) * BLK]
                dve.tensor_tensor(o, pst[:, 2:4, :], o, A_).then_inc(ssm_y_read, 1)
            if i >= ST:
                return
            dve.wait_ge(ssm_b, i + 1)
            if i >= 2:
                dve.wait_ge(ssm_s, i - 1)

            def framed(x):
                return x.rearrange("p (f j) -> p f j", f=2)
            bu_re, bu_im = framed(pst[:, i % 2, 0:SEQ]), framed(pst[:, i % 2, SEQ:2 * SEQ])
            co = rot_cos[:, i, :].unsqueeze(1).broadcast_to([P, 2, FRAME])
            si = rot_sin[:, i, :].unsqueeze(1).broadcast_to([P, 2, FRAME])
            z = st_z[:, i % 2, :, :]
            dve.tensor_tensor(framed(z[:, 0, :]), bu_re, co, M)
            dve.tensor_tensor(framed(z[:, 1, :]), bu_im, co, M)
            dve.tensor_tensor(framed(prod[:, 0, :]), bu_im, si, M)
            dve.tensor_tensor(framed(prod[:, 1, :]), bu_re, si, M).then_inc(ssm_b_read, 1)
            dve.wait_ge(ssm_b_read, i + 1)
            dve.tensor_tensor(z[:, 0, :], z[:, 0, :], prod[:, 0, :], A_)
            steps.did(dve.tensor_tensor(z[:, 1, :], z[:, 1, :], prod[:, 1, :], S))
            steps.settle()
            mag = par_[:, MAG, i:i + 1].broadcast_to([P, FRAME])
            for part in range(2):
                ins = dve.tensor_tensor_scan(z[:, part, 0:FRAME], mag, z[:, part, 0:FRAME], 0.0, M, A_)
            steps.did(ins)
            steps.settle()
            zr, zi = z[:, 0, FRAME - 1:FRAME], z[:, 1, FRAME - 1:FRAME]
            ce, se = rot_cos[:, i, FRAME - 1:FRAME], rot_sin[:, i, FRAME - 1:FRAME]
            dve.tensor_tensor(frame_init[:, 1, 0:1], zi, se, M)
            steps.did(dve.tensor_tensor(frame_init[:, 1, 1:2], zr, se, M))
            steps.settle()
            dve.scalar_tensor_tensor(out=frame_init[:, 0, 0:1], in0=zr, scalar=ce, in1=frame_init[:, 1, 0:1], op0=M, op1=S)
            steps.did(dve.scalar_tensor_tensor(out=frame_init[:, 0, 1:2], in0=zi, scalar=ce, in1=frame_init[:, 1, 1:2],
                                               op0=M, op1=A_))
            steps.settle()
            for part in range(2):
                ins = dve.tensor_tensor_scan(z[:, part, FRAME:SEQ], mag, z[:, part, FRAME:SEQ],
                                             frame_init[:, 0, part:part + 1], M, A_)
            ins.then_inc(ssm_z, 1)

        def ssm_steps_pool(pool, steps):
            M, A_, S = ALU.mult, ALU.add, ALU.subtract

            def framed(x):
                return x.rearrange("p (f j) -> p f j", f=2)
            for i in range(ST):
                pool.wait_ge(ssm_z, i + 1)
                if i >= 3:
                    pool.wait_ge(ssm_y_done, i - 2)
                z, o = st_z[:, i % 2, :, :], st_s[:, i % 3, :, :]
                co = rot_cos[:, i, :].unsqueeze(1).broadcast_to([P, 2, FRAME])
                si = rot_sin[:, i, :].unsqueeze(1).broadcast_to([P, 2, FRAME])
                pool.tensor_tensor(framed(o[:, 0, :]), framed(z[:, 0, :]), co, M)
                pool.tensor_tensor(framed(o[:, 1, :]), framed(z[:, 1, :]), co, M)
                pool.tensor_tensor(framed(z_prod[:, 0, :]), framed(z[:, 1, :]), si, M)
                steps.did(pool.tensor_tensor(framed(z_prod[:, 1, :]), framed(z[:, 0, :]), si, M))
                steps.settle()
                pool.tensor_tensor(o[:, 0, :], o[:, 0, :], z_prod[:, 0, :], S)
                steps.did(pool.tensor_tensor(o[:, 1, :], o[:, 1, :], z_prod[:, 1, :], A_))
                steps.settle()
                pool.sem_inc(ssm_s, 1)

        def ssm_act(act):
            for g in range(2):
                act.wait_ge(ssm_y_read, g + 1)
                y = ssm_y[:, :, g * BLK:(g + 1) * BLK]
                act.activation(y, y, ACT.Gelu_apprx_tanh).then_inc(ssm_gelu, 1)

        def glu_fetch_dve(dve):
            dve.wait_ge(row_ready, 32)

            def fetch(m, blk, p):
                cs = slice(m * BLK, (m + 1) * BLK)
                dve.tensor_tensor(glu_in[:, :, cs], acc[:, m, :, :],
                                  row_bglu[:, cs].unsqueeze(1).broadcast_to([P, 2, BLK]), ALU.add).then_inc(fetched[m], 1)
            return fetch

        def fetch_residual(dve):
            def fetch(m, blk, p):
                o = resid[:, :, bass.ds(blk * BLK, BLK)]
                dve.tensor_tensor(o, acc[:, m, :, :], o, ALU.add).then_inc(fetched[m], 1)
            return fetch

        def glu_act(act):
            for m in range(2):
                act.wait_ge(fetched[m], AT["mod"][1] + 1)
                o = glu_in[:, :, m * BLK:(m + 1) * BLK]
                act.activation(o, o, ACT.Sigmoid).then_inc(glu_sig, 1)

        def glu_dve(dve):
            for m in range(2):
                dve.wait_ge(glu_sig, m + 1)
                o = ssm_y[:, :, m * BLK:(m + 1) * BLK]
                dve.tensor_tensor(o, o, glu_in[:, :, m * BLK:(m + 1) * BLK], ALU.mult).then_inc(glu_out, 1)

        top2 = stage0 + 4 * (2 * FT * SEQ + 4 * BLK)
        r = Region(top2)
        gate_w_parts = r("gate_w_parts", [P, KT, 2, 4 * NH_A], F32R)
        gate_w_hi, gate_w_lo = gate_w_parts[:, :, 0, :], gate_w_parts[:, :, 1, :]
        neg_mask = at("neg_mask_sb", [P, 2, 2, SEQ], offset=top2)
        gate_w = r("gate_w", [P, KT, 4 * NH_A])
        b_mod_col = r("b_mod_col", [P, 3 * KT])
        mod_col = r("mod_col", [P, 3 * KT, 2])
        conv_w, conv_b = r("conv_w_sb", [P, KT, 3]), r("conv_b_sb", [P, KT])
        b_if_row = r("b_if_row", [P, 4 * NH_A])
        mh_col = r("mh_col", [P, KT])
        q_gain, k_gain = r("q_gain", [P, HD_B]), r("k_gain", [P, HD_B])
        rope = r("rope_sb", [P, 2, 2, 2, 32])
        m_rows = [r(f"m_rows{d}", [NH_A, SEQ + 1]) for d in range(2)]
        ones_row = r("ones_row", [NH_A, SEQ])
        gate_pre, gate_log, gate_tmp = (r(n, [P, 2, 4 * NH_A]) for n in ("gate_pre", "gate_log", "gate_tmp"))
        w_col = r("w_col", [P, 2, 2, NH_A])
        g_col, e_col = r("g_col", [P, 2, 2, NH_A]), r("e_col", [P, 2, 2, NH_A])
        row_s = [r(f"row_s{d}", [NH_A, 4]) for d in range(2)]
        r = Region(stage0)
        keys_t, vals = r("keys_t", [P, NKV_B, 2 * SEQ]), r("vals", [P, 4, NKV_B * HD_B])
        area1 = r.o
        q_c, k_c = r("q_c", [P, NH_A, SEQ]), r("k_c", [P, NH_A, SEQ])
        area2 = r.o
        c0 = r("c0", [P, 2 * NH_A, VA])
        area3 = r.o
        ha = r("ha", [P, 2, D])
        area4 = r.o
        va = r("va", [P, 2, NH_A, VA])
        area5 = r.o
        r = Region(area1)
        ck_nat, ckb_nat, conv_acc_c = r("ck_nat", [P, 2, HALF]), r("ckb_nat", [P, 2, BLK]), r("conv_acc_c", [P, 4, SEQ])
        assert r.o <= area2
        mod_nat_gate = at("mod_nat_gate", [P, D], offset=area2)
        cen, qk_nat = at("cen", [P, 2, D], offset=area3), at("qk_nat", [P, 2, D], offset=area3)
        fin_row = at("fin_row", [P, D], offset=area5)
        ha_squares = at("ha_squares", [P, 2, D], offset=area4)
        r = Region(area5)
        ck_t = r("ck_t", [P, NH_A, SEQ])
        rows_c = at("rows_c", [NH_A, 2, 4, SEQ], offset=area5)
        turn_tmp2 = at("turn_tmp2", [P, 2, SEQ], offset=r.o)
        kw = r("kw", [P, 2, 2, P])
        hn0 = r("hn0", [P, 3, 2 * NKV_B])
        assert r.o <= top2
        r = Region(area5)
        kb_nat = r("kb_nat", [P, 2, NKV_B * HD_B])
        conv_acc_x = at("conv_acc_x", [P, 4, SEQ], offset=r.o)
        rows_of = (rows_c, at("rows_x", [NH_A, 2, 4, SEQ], offset=r.o))
        m_bc, q_in, decay = r("m_bc", [P, 2, SEQ + 1]), r("q_in", [P, 2, SEQ]), r("decay", [P, 2, 2, SEQ])
        squares = r("squares", [P, DV_A])
        q_squares = at("q_squares", [P, 2, HD_B], offset=r.o - 4 * DV_A)
        assert r.o <= top2, (r.o, top2)
        den = stat[:, 60:64].rearrange("p (a b) -> p a b", a=2)
        qb_nat, sg_a = at("qb_nat", [P, 2, D], offset=area1), at("sg_a", [P, 2, D], offset=area1)
        qb_t, sg_b = at("qb_t", [P, NH_B, SEQ], offset=area2), at("sg_b", [P, 2, D], offset=area2)
        ob = at("ob", [P, 2, D], offset=area4)
        r = Region(area5 + 4 * 2 * NKV_B * HD_B)
        rope_tmp = r("rope_tmp", [P, NH_B, 2, 32])
        hn = r("hn", [P, 3, 2 * NH_B])
        row2 = r("row2", [P, 3, 2 * NH_B])
        hn_keys = r("hn_keys", [P, 3, 2 * NKV_B])
        assert r.o <= top2
        probs2 = at("probs2", [P, 2, BLK], offset=area5)
        probs2_t = at("probs2_t", [P, 2, BLK], offset=area5 + 4 * 2 * NKV_B * HD_B)
        gate_row, ln_w_row = at("gate_row", [P, D], offset=stage0), at("ln_w_row", [P, D], offset=stage0 + 4 * D)
        r = Region(area3)
        ln_b_row, diag_g, ones_full = r("ln_b_row", [P, D]), r("diag_g", [P, 4, P]), r("ones_full", [P, P])

        b2_consts, ctx_loaded, fin_loaded, mask_loaded, ln_loaded = (
            sem(n) for n in ("b2_consts", "ctx_loaded", "fin_loaded", "mask_loaded", "ln_loaded"))
        c_loaded, mod_turned, mod_done = sem("c_loaded"), sem("mod_turned"), sem("mod_done")
        c_silu, c_hi, c_lo = sem("c_silu"), sem("c_hi"), sem("c_lo")
        cen_sum, x1_half = sem("cen_sum"), sem("x1_half")
        cen_done, fin_sq, fin_ms, fin_root, x1_done = (sem(n) for n in ("cen_done", "fin_sq", "fin_ms", "fin_root", "x1_done"))
        gw_hi, gw_lo = sem("gw_hi"), sem("gw_lo")
        gt_prod, gt_pre, gt_ln, gt_log, gt_rows, gt_exp_in, gt_exp, gt_w, gt_cols, gt_done = (
            sem("gt_" + n) for n in ("prod", "pre", "ln", "log", "rows", "exp_in", "exp", "w", "cols", "done"))
        cv_turned, cv_acc, cv_silu = sem("cv_turned"), sem("cv_acc"), sem("cv_silu")
        ones_set = sem("ones_set")
        ks_turned, ks_scaled, ks_prod, ks_done = (sem("ks_" + n) for n in ("turned", "scaled", "prod", "done"))
        ml_s, ml_m, ml_copy, ml_a, ml_mask, ml_exp, ml_ws, ml_num, ml_out = (
            sem("ml_" + n) for n in ("s", "m", "copy", "a", "mask", "exp", "ws", "num", "out"))
        hn_sq, hn_ms, hn_root, hn_turnable, hn_turned, hn_stored = (
            sem("hn_" + n) for n in ("sq", "ms", "root", "turnable", "turned", "stored"))
        gate_ready = sem("gate_ready")
        q_scaled, q_gained = sem("q_scaled"), sem("q_gained")
        a2_scores, a2_max, a2_probs, a2_turned, a2_out, a2_fetched = (
            sem("a2_" + n) for n in ("scores", "max", "probs", "turned", "out", "fetched"))
        a2_copied = sem("a2_copied")
        gr_diag, gr_row, gr_done = sem("gr_diag"), sem("gr_row"), sem("gr_done")
        end_sq, end_ms, end_root, end_done = (sem("end_" + n) for n in ("sq", "ms", "root", "done"))
        hr_sq, hr_ms, hr_root = (sem("hr_" + n) for n in ("sq", "ms", "root"))
        M_, A_, S_ = ALU.mult, ALU.add, ALU.subtract

        c_rep = act_hi[:, KT // 2:KT, :].rearrange("p k (a m) -> p (k a) m", a=2)
        MOD_TILES = (2 * KT, KT)

        def mod_act(act, use):
            act.wait_ge(b2_consts if use else c_loaded, 16 * N_B2 if use else 16)
            if use == 0:
                act.activation(c_col[:], c_col[:], ACT.Silu).then_inc(c_silu, 1)
                act.wait_ge(c_silu, 1)
            act.wait_ge(w_used, AT["ffn2"][0] + 16 * NB if use else AT["glu"][0])
            for v in range(4):
                ins = act.activation(c_rep[:, :, 32 * v:32 * v + 32],
                                     c_col[:, v % 2, :].unsqueeze(2).broadcast_to([P, KT, 32]), ACT.Copy)
            ins.then_inc(c_hi, 1)

        def mod_dve(dve, use):
            if use == 0:
                for v in range(2):
                    steps.did(dve.tensor_tensor(pick[:, v:v + 1], ident[:, 32 * v:32 * v + 1],
                                                ident[:, 64 + 32 * v:65 + 32 * v], ALU.add))
            dve.wait_ge(c_hi, use + 1)
            for v in range(2):
                ins = dve.tensor_tensor(c_rep[:, :, 64 + 32 * v:96 + 32 * v],
                                        c_col[:, v, :].unsqueeze(2).broadcast_to([P, KT, 32]),
                                        c_rep[:, :, 32 * v:32 * v + 32].bitcast(F32), ALU.subtract)
            ins.then_inc(c_lo, 1)

        def mod_fetch(act, use):
            def fetch(m, blk, p):
                act.activation((mod_nat, mod_nat_gate)[use][:, bass.ds(blk * BLK, BLK)], acc[:, m, 0, :],
                               ACT.Copy).then_inc(fetched[m], 1)
            return fetch

        def mod_pe(pe, name, use, between=None):
            pe.wait_ge(c_lo, use + 1)
            nch = job(name)[2]

            def body(i, s, c, p):
                for m in range(2):
                    pe.wait_ge(fetched[m], p + 1)
                    for j in range(nch):
                        pe.wait_ge(w_lo_done, c + nch * m + j + 1)
                        slot = (s + nch * m + j) % SLOTS
                        for kk in range(2):
                            k = 2 * j + kk
                            x, o = c_rep[:, k, :], acc[:, m, 0, :]
                            pe.matmul(o, x, w_hi[:, slot, kk * BLK:(kk + 1) * BLK], start=k == 0, stop=False)
                            mm = pe.matmul(o, x, w_lo[:, slot, kk * BLK:(kk + 1) * BLK], start=False, stop=k == KT - 1)
                        mm.then_inc(w_used, 1)
                        if between is not None:
                            between()
            pairs(pe, name, body, between is not None)

        def mod_turn_pe(pe, after, use):
            for m in range(2):
                pe.wait_ge(fetched[m], AT[after][1] + 1)
            src = (mod_nat, mod_nat_gate)[use]
            for t in range(MOD_TILES[use]):
                mm = pe.matmul(pst[:, 0, 2 * t:2 * t + 2], src[:, t * P:(t + 1) * P], pick[:], start=True, stop=True)
            mm.then_inc(mod_turned, 1)

        def wo1_step_pe(pe, s):
            if s == 0:
                mod_turn_pe(pe, "w_out", 0)

        def wo1_step_dve(dve, s):
            if s == 1:
                mod_col_dve(dve, 0)

        def mod_col_dve(dve, use):
            dve.wait_ge(mod_turned, use + 1)
            a, n = 2 * KT * use, MOD_TILES[use]
            dve.wait_ge(b2_consts, 16 * N_B2)
            steps.did(dve.tensor_tensor(mod_col[:, a:a + n, :], pst[:, 0, 0:2 * n].rearrange("p (t v) -> p t v", v=2),
                                        b_mod_col[:, a:a + n].unsqueeze(2).broadcast_to([P, n, 2]), ALU.add))
            steps.settle()
            if use == 0:
                steps.did(dve.tensor_scalar(mod_col[:, KT:2 * KT, :], mod_col[:, KT:2 * KT, :], 1.0, None, ALU.add))
                steps.settle()
            dve.sem_inc(mod_done, 1)

        def row_sums_act(act, src, junk):
            for h in range(2):
                act.activation(junk[:, h, :], src[:, h, :], ACT.Copy, accum_out=stat[:, 8 + h:9 + h]).then_inc(cen_sum, 1)

        def centre_dve(dve, use, dst, src):
            dve.wait_ge(cen_sum, 2 * use + 2)
            steps.did(dve.tensor_scalar(stat[:, 10:12], stat[:, 8:10], 1.0 / D, None, M_))
            steps.settle()
            for h in range(2):
                dve.tensor_scalar(dst[:, h, :], src[:, h, :], stat[:, 10 + h:11 + h], None, S_).then_inc(cen_done, 1)

        MG_STEPS = 6

        def mg_step_act(act, s):
            if s == 0:
                act.wait_ge(ctx_loaded, 16)
                row_sums_act(act, cen, junk_lo)
            elif s == 2:
                act.wait_ge(cen_done, 2)
                act.wait_ge(cen_sum, 2)
                norm_squares_act(act, cen, junk_lo)
            elif s == 4:
                norm_root_act(act, "u_ctx")

        def mg_step_dve(dve, s):
            if s == 1:
                centre_dve(dve, 0, cen, cen)
            elif s == 3:
                norm_mean_dve(dve, "u_ctx")
            elif s == 5:
                norm_diag_dve(dve, "u_ctx")

        CK_STEPS = 11

        def ck_step_act(act, s):
            if s == 0:
                act.wait_ge(fetched[1], AT["mod_gate"][1] + 1)
                for h in range(2):
                    ins = act.activation(cen[:, h, :], resid[:, h, :], ACT.Square, accum_out=stat[:, 12 + h:13 + h])
                ins.then_inc(fin_sq, 1)
            elif s == 2:
                act.wait_ge(fin_ms, 1)
                act.activation(stat[:, 16:18], stat[:, 14:16], ACT.Sqrt).then_inc(fin_root, 1)
            elif s == 5:
                act.wait_ge(x1_done, 1)
                row_sums_act(act, resid, cen)
            elif s == 7:
                act.wait_ge(cen_done, 4)
                norm_squares_act(act, cen, ha_squares)
            elif s == 9:
                norm_root_act(act, "u_x")

        def ck_step_pe(pe, s):
            if s == 7:
                mod_turn_pe(pe, "ctx_k", 1)

        def ck_step_dve(dve, s):
            if s == 1:
                dve.wait_ge(fin_sq, 1)
                dve.tensor_scalar(stat[:, 14:16], stat[:, 12:14], 1.0 / D, EPS, M_, A_).then_inc(fin_ms, 1)
            elif s == 3:
                dve.wait_ge(fin_root, 1)
                steps.did(dve.reciprocal(stat[:, 18:20], stat[:, 16:18]))
                steps.settle()
                dve.wait_ge(fin_loaded, 16)
            if s in (3, 4):
                h = s - 3
                dve.scalar_tensor_tensor(out=resid[:, h, :], in0=resid[:, h, :], scalar=stat[:, 18 + h:19 + h],
                                         in1=fin_row[:], op0=M_, op1=M_).then_inc(x1_half, 1)
            if s == 4:
                dve.wait_ge(x1_half, 2)
                dve.sem_inc(x1_done, 1)
            elif s == 6:
                centre_dve(dve, 1, cen, resid)
            elif s == 8:
                norm_mean_dve(dve, "u_x")
            elif s == 9:
                mod_col_dve(dve, 1)
            elif s == 10:
                norm_diag_dve(dve, "u_x")

        def gates_pe_product(pe, n_use):
            pe.wait_ge(gw_lo, 1)
            for h in range(2):
                for k in range(KT):
                    xh, xl = act_hi[:, k, h * P:(h + 1) * P], act_lo[:, k, h * P:(h + 1) * P]
                    o, w = pst[:, 0, h * 64:(h + 1) * 64], gate_w_parts[:, k, :, :].rearrange("p a c -> p (a c)")
                    pe.matmul(o, xh, w, start=k == 0, stop=False)
                    mm = pe.matmul(o, xl, w, start=False, stop=k == KT - 1)
            mm.then_inc(gt_prod, 1)

        def gates_pe_rows(pe, n_use):
            pe.wait_ge(gt_log, n_use + 1)
            for d in range(2):
                for f, src in ((0, gate_pre), (1, gate_log)):
                    for h in range(2):
                        c = 16 * d + 8 * f
                        mm = pe.matmul(pst[0:NH_A, 1 + d, f * SEQ + h * P:f * SEQ + (h + 1) * P],
                                       src[:, h, c:c + NH_A], ident[:], start=True, stop=True)
            mm.then_inc(gt_rows, 1)

        def gates_pe_cols(pe, n_use):
            pe.wait_ge(gt_w, n_use + 1)
            for d in range(2):
                for q, slot in ((0, 3), (1, 1)) if n_use else ((0, 3),):
                    for h in range(2):
                        mm = pe.matmul(pst[:, 3, 32 * q + 16 * h + 8 * d:32 * q + 16 * h + 8 * d + 8],
                                       rows_of[n_use][:, d, slot, h * P:(h + 1) * P], ident[0:NH_A, 0:NH_A],
                                       start=True, stop=True)
            mm.then_inc(gt_cols, 1)

        def gates_act_log(act, n_use):
            act.wait_ge(gt_pre, n_use + 1)
            act.activation(gate_tmp[:], gate_pre[:], ACT.Abs).then_inc(gt_ln, 1)
            act.wait_ge(gt_ln, 3 * n_use + 1)
            act.activation(gate_tmp[:], gate_tmp[:], ACT.Exp, scale=-1.0).then_inc(gt_ln, 1)
            act.wait_ge(gt_ln, 3 * n_use + 2)
            act.activation(gate_tmp[:], gate_tmp[:], ACT.Ln, bias=1.0).then_inc(gt_ln, 1)

        def gates_act_exp(act, n_use):
            act.wait_ge(gt_exp_in, n_use + 1)
            for d in range(2):
                if n_use == 0:
                    ins = act.activation(rows_of[0][:, d, 3, :], rows_of[0][:, d, 1, :], ACT.Exp, bias=row_s[d][:, 1:2])
                else:
                    ins = act.activation(rows_of[1][:, d, 3, :], rows_of[1][:, d, 2, :], ACT.Exp, scale=-1.0)
            ins.then_inc(gt_exp, 1)

        def gates_dve_pre(dve, n_use):
            dve.wait_ge(gt_prod, n_use + 1)
            by_part = pst[:, 0, 0:128].rearrange("p (h a c) -> p a h c", h=2, a=2)
            steps.did(dve.tensor_tensor(gate_pre[:], by_part[:, 0], b_if_row[:].unsqueeze(1).broadcast_to([P, 2, 32]), A_))
            steps.settle()
            dve.tensor_tensor(gate_pre[:], gate_pre[:], by_part[:, 1], A_).then_inc(gt_pre, 1)

        def gates_dve_log(dve, n_use):
            dve.wait_ge(gt_ln, 3 * n_use + 3)
            dve.wait_ge(gt_pre, n_use + 1)
            dve.scalar_tensor_tensor(out=gate_log[:], in0=gate_pre[:], scalar=0.0, in1=gate_tmp[:],
                                     op0=ALU.min, op1=S_).then_inc(gt_log, 1)

        def run(x, d):
            return x if d == 0 else x[:, ::-1]

        def gates_dve_scan(dve, n_use):
            rw = rows_of[n_use]
            dve.wait_ge(gt_rows, n_use + 1)
            for d in range(2):
                f_row = pst[0:NH_A, 1 + d, SEQ:2 * SEQ]
                steps.did(dve.tensor_tensor_scan(run(rw[:, d, 0, :], d), run(ones_row[:], d), run(f_row, d), 0.0, M_, A_))
            steps.settle()
            for d in range(2):
                steps.did(dve.tensor_tensor(rw[:, d, 1, :], pst[0:NH_A, 1 + d, 0:SEQ], rw[:, d, 0, :], S_))
            steps.settle()
            if n_use == 0:
                for d in range(2):
                    steps.did(dve.tensor_reduce(row_s[d][:, 0:1], rw[:, d, 1, :], X_AXIS, ALU.max))
                steps.settle()
                for d in range(2):
                    last = 0 if d else SEQ - 1
                    steps.did(dve.tensor_tensor(row_s[d][:, 2:3], row_s[d][:, 0:1], rw[:, d, 0, last:last + 1], A_))
                    ins = dve.tensor_scalar(row_s[d][:, 1:2], row_s[d][:, 0:1], -1.0, None, M_)
                ins.then_inc(gt_exp_in, 1)
            else:
                for d in range(2):
                    steps.did(dve.tensor_copy(m_rows[d][:, SEQ:SEQ + 1], row_s[d][:, 2:3]))
                    steps.did(dve.tensor_tensor_scan(run(m_rows[d][:, 0:SEQ], d), run(ones_row[:], d),
                                                     run(rw[:, d, 1, :], d), row_s[d][:, 2:3], M_, ALU.max))
                steps.settle()
                for d in range(2):
                    ins = dve.tensor_tensor(rw[:, d, 2, :], rw[:, d, 0, :], m_rows[d][:, 0:SEQ], A_)
                ins.then_inc(gt_exp_in, 1)

        def gates_dve_weights(dve, n_use):
            dve.wait_ge(gt_exp, n_use + 1)
            if n_use == 0:
                for d in range(2):
                    ins = dve.tensor_scalar(rows_c[:, d, 3, :], rows_c[:, d, 3, :], DK_A ** -0.5, None, M_)
                ins.then_inc(gt_w, 1)
            else:
                dve.sem_inc(gt_w, 1)

        def gates_dve_cols(dve, n_use):
            dve.wait_ge(gt_cols, n_use + 1)
            if n_use == 0:
                dve.tensor_copy(w_col[:].rearrange("p h d n -> p (h d n)"), pst[:, 3, 0:32]).then_inc(gt_done, 1)
            else:
                dve.tensor_copy(e_col[:].rearrange("p h d n -> p (h d n)"), pst[:, 3, 0:32])
                dve.tensor_copy(g_col[:].rearrange("p h d n -> p (h d n)"), pst[:, 3, 32:64]).then_inc(gt_done, 1)

        CONVS = ((NH_A, conv_acc_c, 2), (0, conv_acc_x, 4))

        def conv_step_pe(pe, use, g):
            n = 2 * use + g
            if n:
                pe.wait_ge(cv_acc, n)
            src = (ck_nat, qk_nat)[use]
            for t in range(4):
                for h in range(2):
                    c = (4 * g + t) * P
                    mm = pe.transpose(pst[:, t, h * P:(h + 1) * P], src[:, h, c:c + P], ident[:])
            mm.then_inc(cv_turned, 1)

        def conv_step_dve(dve, use, g):
            w0, conv_acc, _ = CONVS[use]
            n = 2 * use + g
            dve.wait_ge(cv_turned, n + 1)
            if n:
                dve.wait_ge(cv_silu, n)
            for tap in range(3):
                for t in range(4):
                    k = w0 + 4 * g + t
                    ps, w = pst[:, t, 0:SEQ], conv_w[:, k, :]
                    if tap == 0:
                        ins = dve.tensor_scalar(conv_acc[:, t, :], ps, w[:, 1:2], conv_b[:, k:k + 1], M_, A_)
                    elif tap == 1:
                        o = conv_acc[:, t, 1:SEQ]
                        ins = dve.scalar_tensor_tensor(out=o, in0=ps[:, 0:SEQ - 1], scalar=w[:, 0:1], in1=o, op0=M_, op1=A_)
                    else:
                        o = conv_acc[:, t, 0:SEQ - 1]
                        ins = dve.scalar_tensor_tensor(out=o, in0=ps[:, 1:SEQ], scalar=w[:, 2:3], in1=o, op0=M_, op1=A_)
                if tap < 2:
                    steps.did(ins)
                    steps.settle()
            ins.then_inc(cv_acc, 1)

        def conv_step_act(act, use, g):
            act.wait_ge(cv_acc, 2 * use + g + 1)
            dst = (ck_t, ck_t, q_c, k_c)[2 * use + g // 2][:, 4 * (g % 2):4 * (g % 2) + 4, :]
            act.activation(dst, CONVS[use][1][:], ACT.Silu).then_inc(cv_silu, 1)

        def state_step_pe(pe, s):
            if s == 0:
                pe.wait_ge(cv_silu, 2)
            if s < NH_A:
                if s >= 2:
                    pe.wait_ge(ks_scaled, s - 1)
                for h in range(2):
                    mm = pe.transpose(pst[:, s % 2, h * P:(h + 1) * P], ck_t[:, s, h * P:(h + 1) * P], ident[:])
                mm.then_inc(ks_turned, 1)
            if s >= 1:
                n = s - 1
                pe.wait_ge(ks_scaled, n + 1)
                if n >= 1:
                    pe.wait_ge(ks_done, n)
                for d in range(2):
                    for h in range(2):
                        mm = pe.matmul(pst[:, 2 + d, 0:VA], kw[:, d, h, :], va[:, h, n, :], start=h == 0, stop=h == 1)
                mm.then_inc(ks_prod, 1)

        def state_step_act(act, s):
            if s < NH_A:
                act.wait_ge(ks_turned, s + 1)
                if s >= 1:
                    act.wait_ge(ks_prod, s)
                for d in range(2):
                    for h in range(2):
                        ins = act.activation(kw[:, d, h, :], pst[:, s % 2, h * P:(h + 1) * P], ACT.Copy,
                                             scale=w_col[:, h, d, s:s + 1])
                ins.then_inc(ks_scaled, 1)

        def state_step_dve(dve, s):
            if s >= 1:
                dve.wait_ge(ks_prod, s)
                dve.tensor_copy(c0[:, 2 * s - 2:2 * s, :], pst[:, 2:4, 0:VA]).then_inc(ks_done, 1)

        CTX_STEPS = 2 + NH_A + 1 + 3
        CTX_TURN = 2 + NH_A + 1

        def ctx_step_pe(pe, s):
            if s < 2:
                conv_step_pe(pe, 0, s)
            elif s < CTX_TURN:
                if s == 2:
                    pe.wait_ge(cv_acc, 2)
                state_step_pe(pe, s - 2)
            elif s == CTX_TURN:
                for b in range(NKV_B // 2):
                    qk_turn_pe(pe, 0, b)
            elif s == CTX_TURN + 1:
                pe.wait_ge(hn_stored, TURN_BANKS[1])
                gates_pe_product(pe, 1)

        def ctx_step_act(act, s):
            if s < 2:
                conv_step_act(act, 0, s)
            elif s < CTX_TURN:
                state_step_act(act, s - 2)
                if s == 5:
                    for h in range(2):
                        qk_root_act(act, 0, h)
            elif s == CTX_TURN:
                for b in range(NKV_B // 2):
                    qk_store_act(act, 0, b)

        def ctx_step_dve(dve, s):
            if s < 2:
                conv_step_dve(dve, 0, s)
            elif s < CTX_TURN:
                state_step_dve(dve, s - 2)
                if s in (4, 6):
                    for h in range(2):
                        for part in (0, 1) if s == 4 else range(2, QK_PARTS):
                            qk_part_dve(dve, 0, h, part)
            elif s == CTX_TURN + 2:
                gates_dve_pre(dve, 1)

        XV_STEPS = 10

        def xv_step_pe(pe, s):
            if s < 4:
                conv_step_pe(pe, 1, s)
            gates_step_pe(pe, 1, s)

        def xv_step_act(act, s):
            if s < 4:
                conv_step_act(act, 1, s)
            gates_step_act(act, 1, s)

        def xv_step_dve(dve, s):
            if s < 4:
                conv_step_dve(dve, 1, s)
            gates_step_dve(dve, 1, s)

        def gates_step_pe(pe, n_use, s):
            if s == 4:
                if n_use:
                    pe.wait_ge(cv_acc, 6)
                gates_pe_rows(pe, n_use)
            elif s == 8:
                gates_pe_cols(pe, n_use)

        def gates_step_act(act, n_use, s):
            if s == 2:
                gates_act_log(act, n_use)
            elif s == 6:
                gates_act_exp(act, n_use)

        def gates_step_dve(dve, n_use, s):
            if s == 1 and n_use == 0:
                gates_dve_pre(dve, 0)
            elif s == 3:
                gates_dve_log(dve, n_use)
            elif s == 5:
                if n_use:
                    dve.wait_ge(cv_silu, 6)
                gates_dve_scan(dve, n_use)
            elif s == 7:
                gates_dve_weights(dve, n_use)
            elif s == 9:
                gates_dve_cols(dve, n_use)

        def cv_step_pe(pe, s):
            gates_step_pe(pe, 0, s)

        def cv_step_act(act, s):
            gates_step_act(act, 0, s)

        def cv_step_dve(dve, s):
            gates_step_dve(dve, 0, s)

        NU = 2 * NH_A

        MLSTM_STEPS = NU + 4

        def mlstm_step_pe(pe, s):
            if s == 0:
                pe.wait_ge(gt_done, 2)
                pe.wait_ge(cv_silu, 6)
            if s < NU and s % 2 == 1:
                head = s // 2
                if s >= 2:
                    pe.wait_ge(ml_ws, s - 1)
                for st in range(2):
                    mm = pe.matmul(pst[:, 0, st * SEQ:(st + 1) * SEQ],
                                   k_c[:, head, st * P:(st + 1) * P], q_c[:, head, :], start=True, stop=True)
                mm.then_inc(ml_s, 1)
            if s < NU:
                if s >= 1:
                    pe.wait_ge(ml_copy, s)
                pe.matmul(pst[:, 1, 0:SEQ + 1], ident[0:NH_A, s // 2:s // 2 + 1].broadcast_to([NH_A, P]),
                          m_rows[s % 2][:], start=True, stop=True).then_inc(ml_m, 1)
            n = s - 2
            if 0 <= n < NU:
                head, d = n // 2, n % 2
                pe.wait_ge(ml_ws, n + 1)
                if n >= 1:
                    pe.wait_ge(ml_out, n)
                for th in range(2):
                    o = pst[:, 2 + th, 0:VA]
                    for j, st in enumerate([0, 1] if th != d else [th]):
                        pe.matmul(o, decay[:, n % 2, st, th * P:(th + 1) * P], va[:, st, head, :],
                                  start=j == 0, stop=False)
                    mm = pe.matmul(o, q_in[:, n % 2, th * P:(th + 1) * P], c0[:, n, :], start=False, stop=True)
                mm.then_inc(ml_num, 1)

        def mlstm_step_act(act, s):
            if s < NU:
                act.wait_ge(ml_m, s + 1)
                if s >= 2:
                    act.wait_ge(ml_mask, s - 1)
                    act.wait_ge(ml_a, s - 1)
                act.activation(m_bc[:, s % 2, :], pst[:, 1, 0:SEQ + 1], ACT.Copy).then_inc(ml_copy, 1)
                act.wait_ge(ml_copy, s + 1)
                if s >= 2:
                    act.wait_ge(ml_num, s - 1)
                act.activation(q_in[:, s % 2, :], m_bc[:, s % 2, 0:SEQ], ACT.Exp, scale=-1.0,
                               bias=m_bc[:, s % 2, SEQ:SEQ + 1]).then_inc(ml_a, 1)
            if 1 <= s <= NU:
                n = s - 1
                act.wait_ge(ml_mask, n + 1)
                for st in range(2):
                    o = decay[:, n % 2, st, :]
                    ins = act.activation(o, o, ACT.Exp, bias=g_col[:, st, n % 2, n // 2:n // 2 + 1])
                ins.then_inc(ml_exp, 1)
            if s >= 5 and s % 2 == 1:
                head = (s - 5) // 2
                act.wait_ge(ml_out, 2 * head + 2)
                for h in range(2):
                    act.activation(squares[:], ha[:, h, head * DV_A:(head + 1) * DV_A], ACT.Square,
                                   accum_out=stat[:, 20 + 8 * h + head:21 + 8 * h + head]).then_inc(hr_sq, 1)
                    act.wait_ge(hr_sq, 2 * head + h + 1)

        def mlstm_step_dve(dve, s):
            if s == 0:
                dve.wait_ge(mask_loaded, 16)
            n = s - 3
            if 0 <= n < NU:
                head, d = n // 2, n % 2
                dve.wait_ge(ml_num, n + 1)
                if n >= 1:
                    dve.wait_ge(ml_out, n)
                total = pst[:, 2:4, VA - 1]
                steps.did(dve.scalar_tensor_tensor(out=den[:, 0, :], in0=total, scalar=-1.0,
                                                   in1=e_col[:, :, d, head], op0=M_, op1=ALU.max))
                steps.settle()
                steps.did(dve.tensor_tensor(den[:, 0, :], total, den[:, 0, :], ALU.max))
                steps.settle()
                steps.did(dve.reciprocal(den[:, 1, :], den[:, 0, :]))
                steps.settle()
                for th in range(2):
                    o = ha[:, th, head * DV_A:(head + 1) * DV_A]
                    x = pst[:, 2 + th, 0:DV_A]
                    if d == 0:
                        ins = dve.tensor_scalar(o, x, den[:, 1, th:th + 1], None, M_)
                    else:
                        ins = dve.scalar_tensor_tensor(out=o, in0=x, scalar=den[:, 1, th:th + 1], in1=o, op0=M_, op1=A_)
                ins.then_inc(ml_out, 1)
            if s < NU:
                dve.wait_ge(ml_copy, s + 1)
                if s >= 2:
                    dve.wait_ge(ml_num, s - 1)
                dve.tensor_tensor(decay[:, s % 2, :, :], neg_mask[:, s % 2, :, :],
                                  m_bc[:, s % 2, 0:SEQ].unsqueeze(1).broadcast_to([P, 2, SEQ]), S_).then_inc(ml_mask, 1)
            if 1 <= s <= NU:
                n = s - 1
                dve.wait_ge(ml_a, n + 1)
                dve.wait_ge(ml_s, n // 2 + 1)
                dve.tensor_tensor(q_in[:, n % 2, :], q_in[:, n % 2, :], q_c[:, n // 2, :], M_)
                dve.wait_ge(ml_exp, n + 1)
                o = decay[:, n % 2, :, :]
                dve.scalar_tensor_tensor(out=o, in0=pst[:, 0, :].rearrange("p (a t) -> p a t", a=2),
                                         scalar=DK_A ** -0.5, in1=o, op0=M_, op1=M_).then_inc(ml_ws, 1)

        def head_norm_act(act):
            act.wait_ge(hr_ms, 1)
            act.activation(stat[:, 36:52], stat[:, 36:52], ACT.Sqrt).then_inc(hr_root, 1)

        def head_norm_dve(dve):
            dve.wait_ge(hr_sq, 2 * NH_A)
            dve.tensor_scalar(stat[:, 36:52], stat[:, 20:36], 1.0 / DV_A, EPS, M_, A_).then_inc(hr_ms, 1)
            dve.wait_ge(hr_root, 1)
            steps.did(dve.reciprocal(stat[:, 36:52], stat[:, 36:52]))
            steps.settle()

        def gated_act(act, func, base):
            def fetch(m, blk, p):
                act.activation(acc[:, m, :, :], acc[:, m, :, :], func).then_inc(gate_ready, 1)
            return fetch

        def gated_dve(dve, dst, base, kind=None):
            def fetch(m, blk, p):
                dve.wait_ge(gate_ready, blk + (base + 1))
                o = dst[:, :, bass.ds(blk * BLK, BLK)]
                if kind == "o":
                    dve.wait_ge(hr_sq, 4 * (blk + 1))
                if kind == "z":
                    for n in range(2 * blk, 2 * blk + 2):
                        for h in range(2):
                            o = dst[:, h, n * DV_A:(n + 1) * DV_A]
                            c = (n % 2) * DV_A
                            ins = dve.scalar_tensor_tensor(out=o, in0=o, scalar=stat[:, 36 + 8 * h + n:37 + 8 * h + n],
                                                           in1=acc[:, m, h, c:c + DV_A], op0=M_, op1=M_)
                else:
                    ins = dve.tensor_tensor(o, o, acc[:, m, :, :], M_)
                ins.then_inc(fetched[m], 1)
            return fetch

        QK_PARTS = 6

        def qk_norm(use):
            src, gain, n = ((ckb_nat, k_gain, NKV_B), (kb_nat, k_gain, NKV_B), (qb_nat, q_gain, NH_B))[use]
            return src, gain, n, ob if use else ckb_nat, (hn0, hn_keys, hn)[use]

        def qk_root_act(act, use, h):
            n, hs = qk_norm(use)[2], qk_norm(use)[4]
            act.wait_ge(hn_ms, 2 * use + h + 1)
            act.activation(hs[:, 1, h * n:(h + 1) * n], hs[:, 0, h * n:(h + 1) * n], ACT.Sqrt).then_inc(hn_root, 1)

        def q_squares_act(act, h, n0):
            act.wait_ge(fetched[0], AT["x_z"][1] + 1)
            act.wait_ge(fetched[1], AT["x_z"][1] + 1)
            for n in range(n0, n0 + 8):
                c = h * NH_B + n
                if c >= 2:
                    act.wait_ge(hn_sq, c - 1)
                act.activation(q_squares[:, n % 2, :], qb_nat[:, h, n * HD_B:(n + 1) * HD_B], ACT.Square,
                               accum_out=hn[:, 0, c:c + 1]).then_inc(hn_sq, 1)

        def qk_part_dve(dve, use, h, part):
            src, gain, n, dst, hs = qk_norm(use)
            x = src[:, h, :].rearrange("p (n e) -> p n e", e=HD_B)
            y = (ob if use else ck_nat)[:, h, 0:n * HD_B]
            sums, roots, scales = (hs[:, v, h * n:(h + 1) * n] for v in range(3))
            if part == 0:
                if use == 2:
                    return
                for m in range(2):
                    dve.wait_ge(fetched[m], AT[("x_qk", "x_o")[use]][1] + 1)
                steps.did(dve.tensor_tensor(y, src[:, h, :], src[:, h, :], M_))
                steps.settle()
            elif part == 1:
                if use == 2:
                    dve.wait_ge(hn_sq, NH_B * (h + 1))
                    for m in range(2):
                        dve.wait_ge(fetched[m], AT["x_z"][1] + 1)
                else:
                    steps.did(dve.tensor_reduce(sums, y.rearrange("p (n e) -> p n e", e=HD_B), X_AXIS, A_))
                    steps.settle()
                dve.tensor_scalar(sums, sums, 1.0 / HD_B, EPS, M_, A_).then_inc(hn_ms, 1)
            elif part == 2:
                dve.wait_ge(hn_root, 2 * use + h + 1)
                steps.did(dve.reciprocal(scales, roots))
                steps.settle()
                steps.did(dve.tensor_tensor(x, x, scales.unsqueeze(2).broadcast_to([P, n, HD_B]), M_))
                steps.settle()
                if use == 2:
                    dve.sem_inc(q_scaled, 1)
            elif part == 3 and use < 2:
                steps.did(dve.tensor_tensor(x, x, gain[:].unsqueeze(1).broadcast_to([P, n, HD_B]), M_))
                steps.settle()
            elif use:
                if use == 2 and part == 4:
                    dve.wait_ge(q_gained, h + 1)
                    dve.wait_ge(hn_turned, TURN_BANKS[2])
                xv = src[:, h, :].rearrange("p (n r s e) -> p n r s e", r=2, s=2, e=32)
                yv = ob[:, h, 0:n * HD_B].rearrange("p (n r s e) -> p n r s e", r=2, s=2, e=32)
                x1, x2, y1, y2 = xv[:, :, :, 0, :], xv[:, :, :, 1, :], yv[:, :, :, 0, :], yv[:, :, :, 1, :]
                shape = [P, n, 2, 32]
                co = rope[:, 0, h, :, :].unsqueeze(1).broadcast_to(shape)
                si = rope[:, 1, h, :, :].unsqueeze(1).broadcast_to(shape)
                t = rope_tmp[:, 0:n, :, :]
                a, b, o, op = (co, si, y1, S_) if part == 4 else (si, co, y2, A_)
                steps.did(dve.tensor_tensor(o, x1, a, M_))
                steps.did(dve.tensor_tensor(t, x2, b, M_))
                steps.settle()
                steps.did(dve.tensor_tensor(o, o, t, op))
                steps.settle()
            if part == 5:
                dve.sem_inc(hn_turnable, 1)

        TURN_BANKS = (0, 2, 4, 12)

        def qk_turn_pe(pe, use, b):
            dst = qk_norm(use)[3]
            pe.wait_ge(hn_turnable, 2 * use + 2)
            done = TURN_BANKS[use] + b
            if done >= 2:
                pe.wait_ge(hn_stored, done - 1)
            for t in range(2):
                for h in range(2):
                    mm = pe.transpose(pst[:, done % 2, t * SEQ + h * P:t * SEQ + (h + 1) * P],
                                      dst[:, h, (2 * b + t) * HD_B:(2 * b + t + 1) * HD_B], ident[:])
            mm.then_inc(hn_turned, 1)

        def qk_store_act(act, use, b):
            done = TURN_BANKS[use] + b
            act.wait_ge(hn_turned, done + 1)
            x = pst[:, done % 2, :].rearrange("p (t s) -> p t s", t=2)
            o = qb_t[:, 2 * b:2 * b + 2, :] if use == 2 else keys_t[:, 2 * b:2 * b + 2, use * SEQ:(use + 1) * SEQ]
            act.activation(o, x, ACT.Copy).then_inc(hn_stored, 1)

        Q_PARTS = ((2, 0, 1), (4, 0, 2), (4, 1, 1), (6, 1, 2), (7, 0, 4), (8, 0, 5), (9, 1, 4), (10, 1, 5))
        Q_TURN = 11
        XZ_STEPS = Q_TURN + NH_B // 2

        def xz_step_pe(pe, s):
            if s == 2:
                for b in range(NKV_B // 2):
                    qk_turn_pe(pe, 1, b)
            elif s >= Q_TURN:
                qk_turn_pe(pe, 2, s - Q_TURN)

        def xz_step_act(act, s):
            if s < 2:
                qk_root_act(act, 1, s)
            if s == 2:
                for b in range(NKV_B // 2):
                    qk_store_act(act, 1, b)
            if s < 4:
                q_squares_act(act, s // 2, 8 * (s % 2))
            if s in (3, 5):
                qk_root_act(act, 2, s // 4)
            if s >= Q_TURN:
                qk_store_act(act, 2, s - Q_TURN)

        def xz_step_dve(dve, s):
            if s < 2:
                for part in range(QK_PARTS):
                    qk_part_dve(dve, 1, s, part)
            for step, h, part in Q_PARTS:
                if s == step:
                    qk_part_dve(dve, 2, h, part)

        def q_gain_pool(pool, h):
            pool.wait_ge(q_scaled, h + 1)
            x = qb_nat[:, h, :].rearrange("p (n e) -> p n e", e=HD_B)
            pool.tensor_tensor(x, x, q_gain[:].unsqueeze(1).broadcast_to([P, NH_B, HD_B]), M_).then_inc(q_gained, 1)

        NQ = 2 * NH_B
        SCALE_B = HD_B ** -0.5
        ATT2_STEPS = NQ + 4

        def attention2_step_pe(pe, s):
            if s == 0:
                pe.wait_ge(hn_stored, TURN_BANKS[3])
            if s < NQ:
                if s >= 2:
                    pe.wait_ge(a2_probs, s - 1)
                head, h = s // 2, s % 2
                pe.matmul(pst[:, s % 2, :], qb_t[:, head, h * P:(h + 1) * P], keys_t[:, head // 4, :],
                          start=True, stop=True).then_inc(a2_scores, 1)
            u = s - 2
            if 0 <= u < NQ:
                pe.wait_ge(a2_probs, u + 1)
                if u >= 1:
                    pe.wait_ge(a2_copied, u)
                for b in range(4):
                    mm = pe.transpose(pst[:, 2, b * P:(b + 1) * P], probs2[:, u % 2, b * P:(b + 1) * P], ident[:])
                mm.then_inc(a2_turned, 1)
            u = s - 3
            if 0 <= u < NQ:
                head = u // 2
                pe.wait_ge(a2_copied, u + 1)
                if u >= 1:
                    pe.wait_ge(a2_fetched, u)
                kv = head // 4
                for b in range(4):
                    mm = pe.matmul(pst[:, 3, 0:HD_B], probs2_t[:, u % 2, b * P:(b + 1) * P],
                                   vals[:, b, kv * HD_B:(kv + 1) * HD_B], start=b == 0, stop=b == 3)
                mm.then_inc(a2_out, 1)

        def attention2_step_act(act, s):
            u = s - 1
            if 0 <= u < NQ:
                act.wait_ge(a2_max, u + 1)
                if u >= 2:
                    act.wait_ge(a2_turned, u - 1)
                act.activation(probs2[:, u % 2, :], pst[:, u % 2, :], ACT.Exp, scale=SCALE_B,
                               bias=row2[:, 0, u:u + 1], accum_out=row2[:, 1, u:u + 1]).then_inc(a2_probs, 1)
            u = s - 2
            if 0 <= u < NQ:
                act.wait_ge(a2_turned, u + 1)
                if u >= 2:
                    act.wait_ge(a2_out, u - 1)
                act.activation(probs2_t[:, u % 2, :], pst[:, 2, :], ACT.Copy).then_inc(a2_copied, 1)

        def attention2_step_dve(dve, s):
            u = s - 4
            if 0 <= u < NQ:
                head, h = u // 2, u % 2
                dve.wait_ge(a2_out, u + 1)
                steps.did(dve.reciprocal(row2[:, 2, u:u + 1], row2[:, 1, u:u + 1]))
                steps.settle()
                dve.tensor_scalar(ob[:, h, head * HD_B:(head + 1) * HD_B], pst[:, 3, 0:HD_B],
                                  row2[:, 2, u:u + 1], None, M_).then_inc(a2_fetched, 1)
            if s < NQ:
                dve.wait_ge(a2_scores, s + 1)
                steps.did(dve.tensor_reduce(row2[:, 2, s:s + 1], pst[:, s % 2, :], X_AXIS, ALU.max))
                steps.settle()
                dve.tensor_scalar(row2[:, 0, s:s + 1], row2[:, 2, s:s + 1], -SCALE_B, None, M_).then_inc(a2_max, 1)

        def sg_fetch(act, sg):
            def fetch(m, blk, p):
                act.activation(sg[:, :, bass.ds(blk * BLK, BLK)], acc[:, m, :, :], ACT.Sigmoid).then_inc(fetched[m], 1)
            return fetch

        def ba_fetch(dve):
            def fetch(m, blk, p):
                o = sg_a[:, :, bass.ds(blk * BLK, BLK)]
                dve.tensor_tensor(o, o, acc[:, m, :, :], M_).then_inc(fetched[m], 1)
            return fetch

        bb_prod = sem("bb_prod")

        def bb_fetch(dve):
            def fetch(m, blk, p):
                o, g = (x[:, :, bass.ds(blk * BLK, BLK)] for x in (sg_a, sg_b))
                dve.tensor_tensor(g, g, acc[:, m, :, :], M_).then_inc(bb_prod, 1)
                dve.wait_ge(bb_prod, blk + 1)
                dve.tensor_tensor(o, o, g, A_).then_inc(fetched[m], 1)
            return fetch

        GR_STEPS = 5

        def gate_row_step_dve(dve, s):
            if s == 0:
                dve.wait_ge(nt_turned, turns["ob"][0] + 16)
                dve.memset(ones_full[:], 1.0)
            else:
                dve.wait_ge(gr_row, s)
                dve.tensor_copy(gate_row[:, (s - 1) * BLK:s * BLK], pst[:, (s - 1) % 2, :]).then_inc(gr_done, 1)
            if s < 4:
                for t in range(4):
                    ins = dve.tensor_scalar(diag_g[:, t, :], ident[:], mod_col[:, 2 * KT + 4 * s + t, 0:1], None, M_)
                ins.then_inc(gr_diag, 1)

        def gate_row_step_pe(pe, s):
            if s < 4:
                pe.wait_ge(gr_diag, s + 1)
                if s >= 2:
                    pe.wait_ge(gr_done, s - 1)
                for t in range(4):
                    mm = pe.matmul(pst[:, s % 2, t * P:(t + 1) * P], ones_full[:], diag_g[:, t, :], start=True, stop=True)
                mm.then_inc(gr_row, 1)

        wo_prod = sem("wo_prod")

        def wo_fetch(dve):
            def fetch(m, blk, p):
                t = sg_b[:, :, bass.ds(blk * BLK, BLK)]
                o = resid[:, :, bass.ds(blk * BLK, BLK)]
                g = gate_row[:, bass.ds(blk * BLK, BLK)].unsqueeze(1).broadcast_to([P, 2, BLK])
                dve.tensor_tensor(t, acc[:, m, :, :], g, M_).then_inc(wo_prod, 1)
                dve.wait_ge(wo_prod, blk + 1)
                dve.scalar_tensor_tensor(out=o, in0=o, scalar=ALPHA, in1=t, op0=M_, op1=A_).then_inc(fetched[m], 1)
            return fetch

        def end_act(act):
            for m in range(2):
                act.wait_ge(fetched[m], AT["end"][1] + 1)
            row_sums_act(act, resid, junk_full)
            act.wait_ge(cen_sum, 6)
            for h in range(2):
                act.wait_ge(cen_done, 5 + h)
                ins = act.activation(junk_full[:, h, :], resid[:, h, :], ACT.Square, accum_out=stat[:, 52 + h:53 + h])
            ins.then_inc(end_sq, 1)
            act.wait_ge(end_ms, 1)
            act.activation(stat[:, 56:58], stat[:, 54:56], ACT.Sqrt).then_inc(end_root, 1)

        def end_dve(dve):
            for m in range(2):
                dve.wait_ge(fetched[m], AT["end"][1] + 1)
            centre_dve(dve, 2, resid, resid)
            dve.wait_ge(end_sq, 1)
            dve.tensor_scalar(stat[:, 54:56], stat[:, 52:54], 1.0 / D, EPS, M_, A_).then_inc(end_ms, 1)
            dve.wait_ge(end_root, 1)
            steps.did(dve.reciprocal(stat[:, 58:60], stat[:, 56:58]))
            steps.settle()
            dve.wait_ge(ln_loaded, 32)
            for h in range(2):
                steps.did(dve.scalar_tensor_tensor(out=resid[:, h, :], in0=resid[:, h, :], scalar=stat[:, 58 + h:59 + h],
                                                   in1=ln_w_row[:], op0=M_, op1=M_))
                steps.settle()
                dve.tensor_tensor(resid[:, h, :], resid[:, h, :], ln_b_row[:], A_).then_inc(end_done, 1)

        B2_LOADS = ((gate_w[:], "gate_w"), (b_mod_col[:], "b_mod_col"), (conv_w[:], "conv_w"),
                    (conv_b[:], "conv_b"), (mh_col[:], "mh_col"), (rope[:], "rope"))
        B2_ROWS = ((b_if_row[:], "b_if_2"), (q_gain[:], "q_norm_w_2"), (k_gain[:], "k_norm_w_2"))
        N_B2 = len(B2_LOADS) + len(B2_ROWS)

        block = ctx.enter_context(nc.Block())

        @block.sync
        def _(sp):
            sp.dma_start(resid[:], A["x"].rearrange("(h p) d -> p h d", p=P)).then_inc(x_ready, 16)
            sp.dma_start(ident[:], A["ident"]).then_inc(consts_ready, 16)
            sp.dma_start(gains[:].rearrange("p a k -> p (a k)"), A["gains"]).then_inc(consts_ready, 16)
            ffn_sp(sp, "ffn1", A["ffn1_w_gate"], A["ffn1_w_up"], A["ffn1_w_down"])
            stream_sp(sp, "w_u", A["w_in"], 3 * HALF)
            stream_sp(sp, "w_qkv", A["w_in"], 0)
            stream_sp(sp, "glu", A["ssm_w_glu"], 0)
            stream_sp(sp, "mod", A["w_mod_2"], 0)
            stream_sp(sp, "w_out", A["w_out"], 0)
            ffn_sp(sp, "ffn2", A["ffn2_w_gate"], A["ffn2_w_up"], A["ffn2_w_down"])
            win2 = A["w_in_2"]
            stream_sp(sp, "mod_gate", A["w_mod_2"], 2 * D)
            for name, col in (("ctx_k", DK_A * NH_A), ("ctx_v", 2 * DK_A * NH_A), ("ctx_kv", KB0), ("x_qk", 0),
                              ("x_v", 2 * DK_A * NH_A), ("x_kv", KB0)) + tuple(
                    (n, KB0 + BLK * b) for n, b in (("x_o", 2), ("x_q", 10), ("x_z", 6), ("x_ga", 18), ("x_zb", 14), ("x_gb", 22))):
                stream_sp(sp, name, win2, col)
            stream_sp(sp, "ba", A["w_branch_a_2"], 0)
            stream_sp(sp, "bb", A["w_branch_b_2"], 0)
            stream_sp(sp, "wo", A["w_out_2"], 0)
            for h in range(2):
                sp.wait_ge(end_done, h + 1)
                sp.dma_start(out.rearrange("(h p) d -> p h d", p=P)[:, h, :], resid[:, h, :]).then_inc(out_done, 16)
            sp.wait_ge(out_done, 32)

        @block.scalar
        def _(act):
            for j in range(LEAD):
                round_chunk(act, j)
            ssm_params_act(act, 0)
            act.wait_ge(x_ready, 16)
            act.wait_ge(consts_ready, 32)
            norm_act(act, "ffn1", resid, junk_full)
            turn_act(act, "ffn1", gains[:, 0, :])
            ssm_params_act(act, 1)
            ffn_act(act, "ffn1", 0)
            act.wait_ge(fetched[1], AT["w_u"][1] + 1)
            norm_act(act, "mix", resid, junk_full)
            turn_act(act, "mix", gains[:, 1, :])
            stream_split(act, "w_u", fetch_prj(act, 6))
            turn_qku_fetch(act, 0, 0, 4, lambda o, i: act.activation(o, i, ACT.Copy))
            stream_split(act, "w_qkv", fetch_prj(act, 0), unrolled=True)
            mod_act(act, 0)
            turn_qku_fetch(act, 0, 4, 12, lambda o, i: act.activation(o, i, ACT.Copy))
            ssm_act(act)
            turn_act(act, "y")
            stream_split(act, "glu")
            glu_act(act)
            act.wait_ge(glu_out, 2)
            act.wait_ge(w_used, AT["mod"][0])
            norm_act(act, "ssm", ssm_y, junk_lo_half)
            stream_split(act, "mod", mod_fetch(act, 0), between=spread(attention1_step_act, act, ATT1_STEPS, "mod"))
            turn_act(act, "ssm", gains[:, 2, 0:8])
            act.wait_ge(at_fetched, N_HEADS1)
            norm_act(act, "att", att, junk_lo_half)
            turn_act(act, "att", gains[:, 2, 8:16], dst=8)
            stream_split(act, "w_out")
            act.wait_ge(fetched[1], AT["ffn2"][1] + 1)
            norm_act(act, "ffn2", resid, junk_full)
            turn_act(act, "ffn2", gains[:, 3, :])
            ffn_act(act, "ffn2", 1)
            mod_act(act, 1)
            act.activation(gate_w_hi, gate_w[:], ACT.Copy).then_inc(gw_hi, 1)
            stream_split(act, "mod_gate", mod_fetch(act, 1), spread(mg_step_act, act, MG_STEPS, "mod_gate"))
            act.wait_ge(w_used, AT["ctx_k"][0])
            turn_act(act, "u_ctx", mod_col[:, KT:2 * KT, 1], bias=mod_col[:, 0:KT, 1])

            def store(place):
                def fetch(m, blk, p):
                    act.activation(place(blk), acc[:, m, :, :], ACT.Copy).then_inc(fetched[m], 1)
                return fetch

            def store_values(dst):
                def fetch(m, blk, p):
                    act.activation(dst[:, :, bass.ds(blk * 2, 2), 0:DV_A],
                                   acc[:, m, :, :].rearrange("p h (n v) -> p h n v", v=DV_A), ACT.Copy).then_inc(fetched[m], 1)
                return fetch
            stream_split(act, "ctx_k", store(lambda blk: ck_nat[:, :, blk * BLK:(blk + 1) * BLK]),
                         spread(ck_step_act, act, CK_STEPS, "ctx_k"))
            stream_split(act, "ctx_v", store_values(va), spread(cv_step_act, act, XV_STEPS, "ctx_v"))
            stream_split(act, "ctx_kv", store(lambda blk: vals[:, 0:2, :] if blk else ckb_nat[:]))
            turn_act(act, "u_x", mod_col[:, KT:2 * KT, 0], bias=mod_col[:, 0:KT, 0])
            stream_split(act, "x_qk", store(lambda blk: qk_nat[:, :, blk * BLK:(blk + 1) * BLK]),
                         spread(ctx_step_act, act, CTX_STEPS, "x_qk", skip=8))
            act.wait_ge(ks_prod, NH_A)
            stream_split(act, "x_v", store_values(va), spread(xv_step_act, act, XV_STEPS, "x_v"))
            between = spread(mlstm_step_act, act, MLSTM_STEPS, "x_kv", "x_o")
            stream_split(act, "x_kv", store(lambda blk: vals[:, 2:4, :] if blk else kb_nat[:]), between)
            stream_split(act, "x_o", gated_act(act, ACT.Sigmoid, 0), between)
            head_norm_act(act)
            stream_split(act, "x_q", store(lambda blk: qb_nat[:, :, bass.ds(blk * BLK, BLK)]))
            stream_split(act, "x_z", gated_act(act, ACT.Silu, 4), spread(xz_step_act, act, XZ_STEPS, "x_z"))
            stream_split(act, "x_ga", sg_fetch(act, sg_a), spread(attention2_step_act, act, ATT2_STEPS, "x_ga"))
            stream_split(act, "x_zb", gated_act(act, ACT.Silu, 8))
            stream_split(act, "x_gb", sg_fetch(act, sg_b))
            turn_act(act, "ha", mh_col)
            stream_split(act, "ba")
            turn_act(act, "ob")
            stream_split(act, "bb")
            turn_act(act, "merge")
            stream_split(act, "wo")
            end_act(act)

        @block.vector
        def _(dve):
            nonlocal steps
            steps = Steps(dve, dve_steps)
            dve.sem_inc(fetched[0], 1)
            dve.sem_inc(fetched[1], 1)
            dve.sem_inc(g_lo_done, 1)
            for j in range(LEAD):
                rest_chunk(dve, j)
            dve.wait_ge(consts_ready, 32)
            norm_dve(dve, "ffn1")
            turn_dve(dve, "ffn1", gains[:, 0, :])
            dve.wait_ge(sp_ready, 2)
            dve.reciprocal(pr(T1), pr(DEN)).then_inc(sp_recip, 1)
            ffn_dve(dve, "ffn1", 0)
            norm_dve(dve, "mix")
            turn_dve(dve, "mix", gains[:, 1, :])
            stream_split(dve, "w_u")
            turn_qku_fetch(dve, 1, 0, 4, dve.tensor_copy)
            dve.wait_ge(tq_turned, 4)
            dve.wait_ge(row_ready, 16)
            for h in range(2):
                steps.did(dve.tensor_tensor(u_nat[:, h, :], u_nat[:, h, :], row_d[:], ALU.mult))
            dve.wait_ge(tables_ready, 1)
            steps.settle()
            stream_split(dve, "w_qkv", between=spread(ssm_step_dve, dve, SSM_STEPS, "w_qkv"))
            mod_dve(dve, 0)
            turn_qku_fetch(dve, 1, 4, 12, dve.tensor_copy)
            turn_dve(dve, "y")
            stream_split(dve, "glu", glu_fetch_dve(dve))
            glu_dve(dve)
            norm_dve(dve, "ssm", HALF)
            dve.wait_ge(att_consts, 16)
            stream_split(dve, "mod", between=spread(attention1_step_dve, dve, ATT1_STEPS, "mod"))
            turn_dve(dve, "ssm", gains[:, 2, 0:8])
            norm_dve(dve, "att", HALF)
            turn_dve(dve, "att", gains[:, 2, 8:16], dst=8)
            stream_split(dve, "w_out", fetch_residual(dve), spread(wo1_step_dve, dve, 2, "w_out", skip=8))
            norm_dve(dve, "ffn2")
            turn_dve(dve, "ffn2", gains[:, 3, :])
            ffn_dve(dve, "ffn2", 1)
            mod_dve(dve, 1)
            dve.wait_ge(gw_hi, 1)
            dve.tensor_tensor(gate_w_lo, gate_w[:], gate_w_hi.bitcast(F32), ALU.subtract).then_inc(gw_lo, 1)
            stream_split(dve, "mod_gate", between=spread(mg_step_dve, dve, MG_STEPS, "mod_gate"))
            turn_dve(dve, "u_ctx", mod_col[:, KT:2 * KT, 1], bias=mod_col[:, 0:KT, 1], tmp=turn_tmp2)
            stream_split(dve, "ctx_k", between=spread(ck_step_dve, dve, CK_STEPS, "ctx_k"))
            dve.memset(va[:, :, :, DV_A:VA], 1.0)
            dve.memset(ones_row[:], 1.0).then_inc(ones_set, 1)
            dve.wait_ge(ones_set, 1)
            stream_split(dve, "ctx_v", between=spread(cv_step_dve, dve, XV_STEPS, "ctx_v"))
            stream_split(dve, "ctx_kv")
            turn_dve(dve, "u_x", mod_col[:, KT:2 * KT, 0], bias=mod_col[:, 0:KT, 0], tmp=turn_tmp2)
            stream_split(dve, "x_qk", between=spread(ctx_step_dve, dve, CTX_STEPS, "x_qk", skip=8))
            stream_split(dve, "x_v", between=spread(xv_step_dve, dve, XV_STEPS, "x_v"))
            between = spread(mlstm_step_dve, dve, MLSTM_STEPS, "x_kv", "x_o")
            stream_split(dve, "x_kv", between=between)
            stream_split(dve, "x_o", gated_dve(dve, ha, 0, "o"), between)
            head_norm_dve(dve)
            stream_split(dve, "x_q")
            stream_split(dve, "x_z", gated_dve(dve, ha, 4, "z"), spread(xz_step_dve, dve, XZ_STEPS, "x_z"))
            stream_split(dve, "x_ga", between=spread(attention2_step_dve, dve, ATT2_STEPS, "x_ga"))
            stream_split(dve, "x_zb", gated_dve(dve, ob, 8))
            stream_split(dve, "x_gb")
            turn_dve(dve, "ha", mh_col)
            stream_split(dve, "ba", ba_fetch(dve))
            turn_dve(dve, "ob")
            stream_split(dve, "bb", bb_fetch(dve), spread(gate_row_step_dve, dve, GR_STEPS, "bb", skip=8))
            turn_dve(dve, "merge")
            stream_split(dve, "wo", wo_fetch(dve))
            end_dve(dve)

        @block.tensor
        def _(pe):
            pe.wait_ge(x_ready, 16)
            ffn_pe(pe, "ffn1", 0, TurnedFirst(pe, ("ffn1", resid)))
            stream_pe(pe, "w_u", turning=TurnedFirst(pe, ("mix", resid)))
            turn_qku_pe(pe, 0, 4, "w_qkv")
            for par in range(2):
                pe.wait_ge(tq_fetched[par], 2)
            pe.wait_ge(b_ready, 32)
            ssm_input_pe(pe, 0)
            stream_pe(pe, "w_qkv", between=spread(ssm_step_pe, pe, SSM_STEPS, "w_qkv"))
            pe.wait_ge(ssm_y_read, 2)
            turn_qku_pe(pe, 4, 12, "glu")
            for par in range(2):
                pe.wait_ge(tq_fetched[par], 6)
            pe.wait_ge(ssm_gelu, 2)
            stream_pe(pe, "glu", turning=TurnedFirst(pe, ("y", ssm_y)))
            mod_pe(pe, "mod", 0, spread(attention1_step_pe, pe, ATT1_STEPS, "mod"))
            stream_pe(pe, "w_out", spread(wo1_step_pe, pe, 2, "w_out", skip=8), TurnedFirst(pe, ("ssm", ssm_y), ("att", att)))
            pe.wait_ge(mod_done, 1)
            ffn_pe(pe, "ffn2", 1, TurnedFirst(pe, ("ffn2", resid)))
            mod_pe(pe, "mod_gate", 1)
            stream_pe(pe, "ctx_k", spread(ck_step_pe, pe, CK_STEPS, "ctx_k"), TurnedFirst(pe, ("u_ctx", cen)))
            pe.wait_ge(mod_done, 2)
            gates_pe_product(pe, 0)
            stream_pe(pe, "ctx_v", spread(cv_step_pe, pe, XV_STEPS, "ctx_v"))
            stream_pe(pe, "ctx_kv")
            pe.wait_ge(gt_done, 1)
            stream_pe(pe, "x_qk", spread(ctx_step_pe, pe, CTX_STEPS, "x_qk", skip=8), TurnedFirst(pe, ("u_x", cen)))
            pe.wait_ge(gt_pre, 2)
            for m in range(2):
                pe.wait_ge(fetched[m], AT["x_v"][1] + 1)
            stream_pe(pe, "x_v", between=spread(xv_step_pe, pe, XV_STEPS, "x_v"))
            between = spread(mlstm_step_pe, pe, MLSTM_STEPS, "x_kv", "x_o")
            stream_pe(pe, "x_kv", between=between)
            stream_pe(pe, "x_o", between=between)
            stream_pe(pe, "x_q")
            stream_pe(pe, "x_z", between=spread(xz_step_pe, pe, XZ_STEPS, "x_z"))
            stream_pe(pe, "x_ga", between=spread(attention2_step_pe, pe, ATT2_STEPS, "x_ga"))
            stream_pe(pe, "x_zb")
            stream_pe(pe, "x_gb")
            stream_pe(pe, "ba", turning=TurnedFirst(pe, ("ha", ha)))
            stream_pe(pe, "bb", spread(gate_row_step_pe, pe, GR_STEPS, "bb", skip=8), TurnedFirst(pe, ("ob", ob)))
            for m in range(2):
                pe.wait_ge(fetched[m], AT["wo"][1] + 1)
            pe.wait_ge(gr_done, 4)
            stream_pe(pe, "wo", turning=TurnedFirst(pe, ("merge", sg_a)))

        @block.gpsimd
        def _(pool):
            steps = Steps(pool, pool_steps)
            for dst, name in ((pr(LDT), "ssm_log_dt"), (pr(LR), "ssm_a_re"), (pr(LI), "ssm_a_im"),
                              (cf_re[:], "ssm_c_re"), (cf_im[:], "ssm_c_im")):
                pool.dma_start(dst, A[name]).then_inc(ssm_consts, 16)
            pool.dma_start(c_col[:], A["c_col"]).then_inc(c_loaded, 16)
            ssm_params_pool(pool, steps)
            pool.wait_ge(w_used, AT["w_u"][0])
            for dst, name in ((b_re[:], "ssm_b_re"), (b_im[:], "ssm_b_im")):
                pool.dma_start(dst, A[name]).then_inc(b_ready, 16)
            pool.dma_start(row_d[:], A["ssm_d"].partition_broadcast(P)).then_inc(row_ready, 16)
            ssm_tables_pool(pool, steps)
            ssm_steps_pool(pool, steps)
            pool.wait_ge(ssm_y_done, ST)
            pool.dma_start(log_mask[:], A["log_mask"]).then_inc(att_consts, 16)
            pool.dma_start(row_bglu[:], A["ssm_b_glu"].partition_broadcast(P)).then_inc(row_ready, 16)
            for dst, name in B2_LOADS:
                pool.dma_start(dst, A[name]).then_inc(b2_consts, 16)
            for dst, name in B2_ROWS:
                pool.dma_start(dst, A[name].partition_broadcast(P)).then_inc(b2_consts, 16)
            pool.wait_ge(w_used, AT["mod_gate"][0])
            pool.dma_start(fin_row[:], A["final_norm"].partition_broadcast(P)).then_inc(fin_loaded, 16)
            pool.dma_start(cen[:], A["ctx_2"].rearrange("(h p) d -> p h d", p=P)).then_inc(ctx_loaded, 16)
            pool.wait_ge(gt_prod, 2)
            pool.dma_start(neg_mask[:], A["neg_mask"]).then_inc(mask_loaded, 16)
            for h in range(2):
                q_gain_pool(pool, h)
            pool.wait_ge(nt_turned, turns["ha"][0] + 16)
            pool.dma_start(ln_w_row[:], A["ln_w_2"].partition_broadcast(P)).then_inc(ln_loaded, 16)
            pool.dma_start(ln_b_row[:], A["ln_b_2"].partition_broadcast(P)).then_inc(ln_loaded, 16)


def lay_out(inputs):
    def a(name):
        return np.ascontiguousarray(inputs[name])

    def by_feature(v):
        return np.ascontiguousarray(v.reshape(-1, P).T)

    o = {"x": a("x")[0]}
    for n in ("ffn1_w_gate", "ffn1_w_up", "ffn1_w_down"):
        o[n] = a(n)[0]
    o["gains"] = np.concatenate([by_feature(a("ffn1_norm")), by_feature(a("mix_norm")),
                                 np.concatenate([by_feature(a("ssm_out_norm")), by_feature(a("attn_out_norm"))], 1),
                                 by_feature(a("ffn2_norm"))], axis=1)
    for n in ("w_in", "ssm_w_glu", "w_out", "ffn2_w_gate", "ffn2_w_up", "ffn2_w_down"):
        o[n] = a(n)[0]
    for n in ("ssm_a_re", "ssm_a_im"):
        o[n] = np.ascontiguousarray(a(n)[0].reshape(ST, P).T)
    o["ssm_log_dt"] = np.ascontiguousarray(np.repeat(a("ssm_log_dt")[0], STATE).reshape(ST, P).T)
    for n in ("ssm_c_re", "ssm_c_im"):
        c = a(n)[0].reshape(ST, 2, GROUP, STATE)
        o[n] = np.zeros((P, ST, 2 * GROUP), np.float32)
        for g in range(2):
            o[n][STATE * g:STATE * (g + 1), :, GROUP * g:GROUP * (g + 1)] = c[:, g].transpose(2, 0, 1)
    for n in ("ssm_b_re", "ssm_b_im"):
        b = a(n)[0].reshape(8, 4, 2, STATE, GROUP)
        o[n] = np.zeros((P, 8, P), np.float32)
        for j in range(4):
            for g in range(2):
                q = 32 * j + GROUP * g
                o[n][q:q + GROUP, :, STATE * g:STATE * (g + 1)] = b[:, j, g].transpose(2, 0, 1)
    o["ssm_d"] = a("ssm_d").reshape(-1)
    o["ssm_b_glu"] = a("ssm_b_glu").reshape(-1)
    for n in ("w_mod_2", "w_in_2", "w_branch_a_2", "w_branch_b_2", "w_out_2"):
        o[n] = a(n)[0]
    o["ctx_2"] = a("ctx_2")[0]
    for n in ("final_norm", "b_if_2", "q_norm_w_2", "k_norm_w_2", "ln_w_2", "ln_b_2"):
        o[n] = a(n).reshape(-1)
    o["c_col"] = np.stack([by_feature(a("c_2").reshape(-1)), by_feature(a("c_ctx_2").reshape(-1))], axis=1)
    o["b_mod_col"] = by_feature(a("b_mod_2").reshape(-1))
    o["conv_w"] = np.ascontiguousarray(a("conv_w_2")[0].reshape(3, KT, P).transpose(2, 1, 0))
    o["conv_b"] = by_feature(a("conv_b_2").reshape(-1))
    o["mh_col"] = by_feature(a("mh_norm_w_2").reshape(-1))
    o["gate_w"] = np.ascontiguousarray(a("w_in_2")[0][:, GATE0:KB0].reshape(KT, P, KB0 - GATE0).transpose(1, 0, 2))
    half = HD_B // 4
    inv = 10000.0 ** (-np.arange(0, 2 * half, 2) / (2 * half))
    tok = np.arange(SEQ)
    angle = np.stack([(tok // GRID_W)[:, None] * inv, (tok % GRID_W)[:, None] * inv], axis=1)
    o["rope"] = np.ascontiguousarray(np.stack([np.cos(angle), np.sin(angle)]).reshape(2, 2, P, 2, half)
                                     .transpose(2, 0, 1, 3, 4).astype(np.float32))
    key, query = np.arange(SEQ)[:, None], np.arange(SEQ)[None, :]
    seen = np.stack([key <= query, key >= query])
    o["neg_mask"] = np.ascontiguousarray(np.where(seen, 0.0, BIG_NEG).astype(np.float32)
                                         .reshape(2, 2, P, SEQ).transpose(2, 0, 1, 3))
    t, s = np.arange(SEQ)[:, None], np.arange(SEQ)[None, :]
    n_branches = sum((t >= s) & (t - s <= w) & ((t - s) % d == 0) for w, d in ((128, 1), (512, 4), (2048, 16)))
    log_n = np.where(n_branches > 0, np.log(np.maximum(n_branches, 1)), BIG_NEG).astype(np.float32)
    o["log_mask"] = np.concatenate([log_n[:P, :P], log_n[P:, :]], axis=1)
    o["ident"] = np.eye(P, dtype=np.float32)
    return o


def kernel(**inputs):
    from concourse import bacc
    from concourse.bass_utils import run_bass_kernel_spmd

    nc = bacc.Bacc("TRN2", target_bir_lowering=False, num_devices=1)
    arrays, A = {}, {}
    for name, a in lay_out({k: np.asarray(v) for k, v in inputs.items()}).items():
        arrays[f"in_{name}"] = a
        A[name] = nc.dram_tensor(f"in_{name}", a.shape, mybir.dt.from_np(a.dtype), kind="ExternalInput").ap()
    out = nc.dram_tensor("out_x", (SEQ, D), F32, kind="ExternalOutput").ap()
    build(nc, A, out)
    r = run_bass_kernel_spmd(nc, [arrays], core_ids=[0])
    return r.results[0]["out_x"].reshape(1, SEQ, D)
```
